# Optimizing a Trainium2 kernel written in Bass

```python
import jax, jax.numpy as jnp
from jax import lax
import numpy as np
import math

D_MODEL = 1024
BATCH = 1
SEQ = 256
DEPTH = 2

HEAD_DIM = 64
H_GDN = (3 * D_MODEL) // (8 * HEAD_DIM)
H_MOBA = D_MODEL // (4 * HEAD_DIM)
H_MLSTM = D_MODEL // HEAD_DIM - H_GDN - H_MOBA
W_GDN = H_GDN * HEAD_DIM
W_MOBA = H_MOBA * HEAD_DIM
W_MLSTM = H_MLSTM * HEAD_DIM
MIX_WIDTH = W_GDN + W_MOBA + W_MLSTM
CONV_WIDTH = 4
GDN_CHUNK = 64
MLSTM_CHUNK = 64
MOBA_BLOCK = 256
MOBA_TOPK = 3
MOBA_Q_BLOCK = 128
D_FF = 2816
N_SUB = 3
ALPHA = (2 * DEPTH) ** 0.25
BETA_INIT = (8 * DEPTH) ** -0.25
ADA_INIT = 0.1
LN_EPS = 1e-5
NORM_EPS = 1e-6

IN_SIZES = [3 * W_GDN, H_GDN, H_GDN, W_GDN,
            3 * W_MOBA,
            2 * W_MLSTM, W_MLSTM, H_MLSTM, H_MLSTM, W_MLSTM]
IN_SPLITS = [int(s) for s in np.cumsum(IN_SIZES)[:-1]]
D_IN = int(sum(IN_SIZES))


def layer_norm(x, g, b):
    xf = x.astype(jnp.float32)
    mu = jnp.mean(xf, -1, keepdims=True)
    var = jnp.mean(jnp.square(xf - mu), -1, keepdims=True)
    return ((xf - mu) * lax.rsqrt(var + LN_EPS) * g + b).astype(x.dtype)

def modulate(x, shift, scale):
    return x * (1 + scale[:, None, :]) + shift[:, None, :]

def swiglu(h, w13, w2):
    a, b = jnp.split(h @ w13, 2, axis=-1)
    return (jax.nn.silu(a) * b) @ w2

def causal_conv_silu(x, w):
    y = lax.conv_general_dilated(x, w[:, None, :], window_strides=(1,), padding=[(CONV_WIDTH - 1, 0)],
                                 dimension_numbers=('NWC', 'WIO', 'NWC'), feature_group_count=x.shape[-1])
    return jax.nn.silu(y)

def split_heads(t):
    b_, t_, w = t.shape
    return t.reshape(b_, t_, w // HEAD_DIM, HEAD_DIM).transpose(0, 2, 1, 3)

def l2norm(x):
    return x * lax.rsqrt(jnp.sum(x * x, -1, keepdims=True) + NORM_EPS)

def to_chunks(a, size):
    b_, h_, t_ = a.shape[:3]
    return jnp.moveaxis(a.reshape(b_, h_, t_ // size, size, *a.shape[3:]), 2, 0)

def from_chunks(a):
    n, b_, h_, l, d = a.shape
    return jnp.moveaxis(a, 0, 2).reshape(b_, h_, n * l, d)

def gated_delta_rule(q, k, v, g, beta):
    b_, h_, t_, dk = q.shape
    dv = v.shape[-1]
    L = GDN_CHUNK
    q = to_chunks(q * dk ** -0.5, L); k = to_chunks(k, L); v = to_chunks(v, L)
    g = to_chunks(g, L); beta = to_chunks(beta, L)
    G = jnp.cumsum(g, axis=-1)
    incl = jnp.tril(jnp.ones((L, L), dtype=bool))
    strict = jnp.tril(jnp.ones((L, L), dtype=bool), -1)
    decay = jnp.exp(jnp.where(incl, G[..., :, None] - G[..., None, :], -jnp.inf))
    kb = k * beta[..., None]
    A = jnp.where(strict, jnp.einsum('nbhid,nbhjd->nbhij', kb, k) * decay, 0.0)
    M = A + jnp.eye(L, dtype=A.dtype)
    u = lax.linalg.triangular_solve(M, v * beta[..., None], left_side=True, lower=True, unit_diagonal=True)
    w = lax.linalg.triangular_solve(M, kb * jnp.exp(G)[..., None], left_side=True, lower=True, unit_diagonal=True)
    attn = jnp.einsum('nbhid,nbhjd->nbhij', q, k) * decay
    q_dec = q * jnp.exp(G)[..., None]
    k_dec = k * jnp.exp(G[..., -1:] - G)[..., None]
    g_last = jnp.exp(G[..., -1])

    def step(S, inp):
        q_i, w_i, u_i, k_i, a_i, gl_i = inp
        v_new = u_i - jnp.einsum('bhld,bhde->bhle', w_i, S)
        o = jnp.einsum('bhld,bhde->bhle', q_i, S) + jnp.einsum('bhls,bhse->bhle', a_i, v_new)
        S = S * gl_i[..., None, None] + jnp.einsum('bhld,bhle->bhde', k_i, v_new)
        return S, o

    S0 = jnp.zeros((b_, h_, dk, dv), q.dtype)
    _, o = lax.scan(step, S0, (q_dec, w, u, k_dec, attn, g_last))
    return from_chunks(o)

def moba_attention(q, k, v):
    b_, h_, t_, d = q.shape
    n_blk = -(-t_ // MOBA_BLOCK)
    top_k = min(MOBA_TOPK, n_blk)
    pad = n_blk * MOBA_BLOCK - t_
    kp = jnp.pad(k, ((0, 0), (0, 0), (0, pad), (0, 0)))
    vp = jnp.pad(v, ((0, 0), (0, 0), (0, pad), (0, 0)))
    k_blk = kp.reshape(b_, h_, n_blk, MOBA_BLOCK, d)
    v_blk = vp.reshape(b_, h_, n_blk, MOBA_BLOCK, d)
    k_mean = jnp.mean(k_blk, axis=3)
    scale = d ** -0.5
    bi = jnp.arange(b_)[:, None, None, None]
    hi = jnp.arange(h_)[None, :, None, None]
    blk_ids = jnp.arange(n_blk)
    n_sel = top_k * MOBA_BLOCK

    def one_block(qb):
        q0 = qb * MOBA_Q_BLOCK
        own = q0 // MOBA_BLOCK
        qc = lax.dynamic_slice_in_dim(q, q0, MOBA_Q_BLOCK, axis=2)
        gate = jnp.einsum('bhqd,bhnd->bhqn', qc, k_mean)
        gate = jnp.where(blk_ids < own, gate, -jnp.inf)
        _, sel = lax.top_k(gate, top_k)
        sel_ok = jnp.repeat(jnp.arange(top_k) < own, MOBA_BLOCK)
        k_sel = k_blk[bi, hi, sel].reshape(b_, h_, MOBA_Q_BLOCK, n_sel, d)
        v_sel = v_blk[bi, hi, sel].reshape(b_, h_, MOBA_Q_BLOCK, n_sel, d)
        s_sel = jnp.where(sel_ok, jnp.einsum('bhqd,bhqkd->bhqk', qc, k_sel) * scale, -jnp.inf)
        k_own = lax.dynamic_slice_in_dim(kp, own * MOBA_BLOCK, MOBA_BLOCK, axis=2)
        v_own = lax.dynamic_slice_in_dim(vp, own * MOBA_BLOCK, MOBA_BLOCK, axis=2)
        q_pos = q0 + jnp.arange(MOBA_Q_BLOCK)
        k_pos = own * MOBA_BLOCK + jnp.arange(MOBA_BLOCK)
        s_own = jnp.where(k_pos[None, :] <= q_pos[:, None],
                          jnp.einsum('bhqd,bhkd->bhqk', qc, k_own) * scale, -jnp.inf)
        p = jax.nn.softmax(jnp.concatenate([s_sel, s_own], -1).astype(jnp.float32), axis=-1).astype(q.dtype)
        return (jnp.einsum('bhqk,bhqkd->bhqd', p[..., :n_sel], v_sel)
                + jnp.einsum('bhqk,bhkd->bhqd', p[..., n_sel:], v_own))

    out = lax.map(one_block, jnp.arange(t_ // MOBA_Q_BLOCK))
    return from_chunks(out)

def mlstm_chunkwise(q, k, v, i_pre, logf):
    b_, h_, t_, d = q.shape
    L = MLSTM_CHUNK
    q = to_chunks(q, L); k = to_chunks(k * d ** -0.5, L); v = to_chunks(v, L)
    i_pre = to_chunks(i_pre, L); logf = to_chunks(logf, L)
    bcum = jnp.cumsum(logf, axis=-1)
    incl = jnp.tril(jnp.ones((L, L), dtype=bool))
    D = jnp.where(incl, bcum[..., :, None] - bcum[..., None, :] + i_pre[..., None, :], -jnp.inf)
    D_max = jnp.max(D, axis=-1)
    w_end = bcum[..., -1:] - bcum + i_pre
    qk = jnp.einsum('nbhtd,nbhsd->nbhts', q, k)

    def step(carry, inp):
        C, n, m = carry
        q_i, k_i, v_i, b_i, D_i, Dm_i, qk_i, we_i = inp
        inter = b_i + m[..., None]
        m_t = jnp.maximum(inter, Dm_i)
        a_inter = jnp.exp(inter - m_t)
        P = qk_i * jnp.exp(D_i - m_t[..., None])
        num = a_inter[..., None] * jnp.einsum('bhld,bhde->bhle', q_i, C) + jnp.einsum('bhls,bhse->bhle', P, v_i)
        den = a_inter * jnp.einsum('bhld,bhd->bhl', q_i, n) + jnp.sum(P, -1)
        h = num / jnp.maximum(jnp.abs(den), jnp.exp(-m_t))[..., None]
        inter_end = b_i[..., -1] + m
        m_new = jnp.maximum(inter_end, jnp.max(we_i, -1))
        s = jnp.exp(we_i - m_new[..., None])
        decay = jnp.exp(inter_end - m_new)
        C = decay[..., None, None] * C + jnp.einsum('bhl,bhld,bhle->bhde', s, k_i, v_i)
        n = decay[..., None] * n + jnp.einsum('bhl,bhld->bhd', s, k_i)
        return (C, n, m_new), h

    init = (jnp.zeros((b_, h_, d, d), q.dtype), jnp.zeros((b_, h_, d), q.dtype), jnp.zeros((b_, h_), q.dtype))
    _, h = lax.scan(step, init, (q, k, v, bcum, D, D_max, qk, w_end))
    return from_chunks(h)

def token_mixer(h, w_in, w_out, gdn_conv, gdn_a_log, gdn_dt_bias, gdn_norm,
                mlstm_conv, mlstm_i_bias, mlstm_f_bias, mlstm_norm):
    b_, t_, _ = h.shape
    dt = h.dtype
    f32 = jnp.float32
    qkv_a, a_a, b_a, z_a, qkv_b, qk_c, v_c, i_c, f_c, o_c = jnp.split(h @ w_in, IN_SPLITS, axis=-1)
    qa, ka, va = jnp.split(causal_conv_silu(qkv_a, gdn_conv), 3, axis=-1)
    qa = l2norm(split_heads(qa).astype(f32))
    ka = l2norm(split_heads(ka).astype(f32))
    va = split_heads(va).astype(f32)
    g = -jnp.exp(gdn_a_log.astype(f32)) * jax.nn.softplus((a_a + gdn_dt_bias).astype(f32))
    beta = jax.nn.sigmoid(b_a.astype(f32))
    oa = gated_delta_rule(qa, ka, va, g.transpose(0, 2, 1), beta.transpose(0, 2, 1)).transpose(0, 2, 1, 3)
    oa = oa * lax.rsqrt(jnp.mean(oa * oa, -1, keepdims=True) + NORM_EPS) * gdn_norm
    oa = (oa.reshape(b_, t_, W_GDN) * jax.nn.silu(z_a.astype(f32))).astype(dt)
    qb, kb, vb = jnp.split(qkv_b, 3, axis=-1)
    ob = moba_attention(split_heads(qb), split_heads(kb), split_heads(vb))
    ob = ob.transpose(0, 2, 1, 3).reshape(b_, t_, W_MOBA).astype(dt)
    qc, kc = jnp.split(causal_conv_silu(qk_c, mlstm_conv), 2, axis=-1)
    i_pre = (i_c + mlstm_i_bias).astype(f32).transpose(0, 2, 1)
    logf = jax.nn.log_sigmoid((f_c + mlstm_f_bias).astype(f32)).transpose(0, 2, 1)
    hc = mlstm_chunkwise(split_heads(qc).astype(f32), split_heads(kc).astype(f32),
                         split_heads(v_c).astype(f32), i_pre, logf).transpose(0, 2, 1, 3)
    hc = hc * jax.nn.sigmoid(o_c.astype(f32)).reshape(b_, t_, H_MLSTM, HEAD_DIM)
    mu = jnp.mean(hc, -1, keepdims=True)
    var = jnp.mean(jnp.square(hc - mu), -1, keepdims=True)
    hc = (hc - mu) * lax.rsqrt(var + NORM_EPS) * mlstm_norm.reshape(H_MLSTM, HEAD_DIM)
    hc = hc.reshape(b_, t_, W_MLSTM).astype(dt)
    return jnp.concatenate([oa, ob, hc], axis=-1) @ w_out

def first_inputs(seed: int = 0) -> dict:
    key = jax.random.key(seed)
    ks = jax.random.split(key, 18)
    nrm = lambda k, shape, s: jax.random.normal(k, shape, jnp.float32) * s
    dt_init = jnp.exp(jax.random.uniform(ks[10], (DEPTH, H_GDN), jnp.float32,
                                         float(np.log(1e-3)), float(np.log(1e-1))))
    return {
        "x": nrm(ks[0], (BATCH, SEQ, D_MODEL), 1.0),
        "c": nrm(ks[1], (BATCH, D_MODEL), 1.0),
        "ada_w": nrm(ks[2], (DEPTH, D_MODEL, N_SUB * 3 * D_MODEL), ADA_INIT * D_MODEL ** -0.5),
        "ada_b": nrm(ks[3], (DEPTH, N_SUB * 3 * D_MODEL), 0.01),
        "ffn_w13": nrm(ks[4], (DEPTH, 2, D_MODEL, 2 * D_FF), D_MODEL ** -0.5),
        "ffn_w2": nrm(ks[5], (DEPTH, 2, D_FF, D_MODEL), BETA_INIT * D_FF ** -0.5),
        "w_in": nrm(ks[6], (DEPTH, D_MODEL, D_IN), D_MODEL ** -0.5),
        "w_out": nrm(ks[7], (DEPTH, MIX_WIDTH, D_MODEL), BETA_INIT * MIX_WIDTH ** -0.5),
        "gdn_conv": nrm(ks[8], (DEPTH, CONV_WIDTH, 3 * W_GDN), CONV_WIDTH ** -0.5),
        "gdn_a_log": jnp.log(jax.random.uniform(ks[9], (DEPTH, H_GDN), jnp.float32, 1.0, 16.0)),
        "gdn_dt_bias": dt_init + jnp.log(-jnp.expm1(-dt_init)),
        "gdn_norm": 1.0 + nrm(ks[11], (DEPTH, HEAD_DIM), 0.02),
        "mlstm_conv": nrm(ks[12], (DEPTH, CONV_WIDTH, 2 * W_MLSTM), CONV_WIDTH ** -0.5),
        "mlstm_i_bias": nrm(ks[13], (DEPTH, H_MLSTM), 0.1),
        "mlstm_f_bias": jnp.linspace(3.0, 6.0, H_MLSTM, dtype=jnp.float32)[None, :] + nrm(ks[14], (DEPTH, H_MLSTM), 0.1),
        "mlstm_norm": 1.0 + nrm(ks[15], (DEPTH, W_MLSTM), 0.02),
        "ln_g": 1.0 + nrm(ks[16], (DEPTH, N_SUB, D_MODEL), 0.02),
        "ln_b": nrm(ks[17], (DEPTH, N_SUB, D_MODEL), 0.02),
    }

def first_block(x, c, ada_w, ada_b, ffn_w13, ffn_w2, w_in, w_out, gdn_conv, gdn_a_log, gdn_dt_bias,
              gdn_norm, mlstm_conv, mlstm_i_bias, mlstm_f_bias, mlstm_norm, ln_g, ln_b):
    b_ = x.shape[0]
    for l in range(DEPTH):
        mod = (jax.nn.silu(c) @ ada_w[l] + ada_b[l]).reshape(b_, N_SUB, 3, D_MODEL)
        y = swiglu(modulate(x, mod[:, 0, 0], mod[:, 0, 1]), ffn_w13[l, 0], ffn_w2[l, 0])
        x = layer_norm(ALPHA * x + 0.5 * (1 + mod[:, 0, 2])[:, None, :] * y, ln_g[l, 0], ln_b[l, 0])
        y = token_mixer(modulate(x, mod[:, 1, 0], mod[:, 1, 1]), w_in[l], w_out[l], gdn_conv[l], gdn_a_log[l],
                        gdn_dt_bias[l], gdn_norm[l], mlstm_conv[l], mlstm_i_bias[l], mlstm_f_bias[l], mlstm_norm[l])
        x = layer_norm(ALPHA * x + (1 + mod[:, 1, 2])[:, None, :] * y, ln_g[l, 1], ln_b[l, 1])
        y = swiglu(modulate(x, mod[:, 2, 0], mod[:, 2, 1]), ffn_w13[l, 1], ffn_w2[l, 1])
        x = layer_norm(ALPHA * x + 0.5 * (1 + mod[:, 2, 2])[:, None, :] * y, ln_g[l, 2], ln_b[l, 2])
    return x


GRID_W = 64
CTX_LEN = 256
N_MIXERS = 4
Q_BLOCK = 128
ROPE_BASE = 10000.0
EPS = 1e-6
F32 = jnp.float32

MLA_HEADS = 16
MLA_Q_RANK = 384
MLA_KV_RANK = 256
MLA_NOPE = 64
MLA_ROPE = 32
MLA_V = 64
MLA_WIDTH = MLA_HEADS * MLA_V

GLA_HEADS = 4
GLA_DK = D_MODEL // 2
GLA_DV = D_MODEL
GLA_GATE_RANK = 16
GLA_GATE_NORM = 16.0
GLA_CHUNK = 64

GQA_HEADS = 16
GQA_KV_HEADS = 4
GQA_HEAD_DIM = 64
GQA_WIDTH = GQA_HEADS * GQA_HEAD_DIM

SSD_INNER = 2 * D_MODEL
SSD_HEAD_DIM = 64
SSD_HEADS = SSD_INNER // SSD_HEAD_DIM
SSD_GROUPS = 4
SSD_STATE = 128
SSD_CONV = 5
SSD_CHUNK = 64
SSD_XBC = SSD_INNER + 2 * SSD_GROUPS * SSD_STATE


def _n_layers_of(kind):
    return len(range(kind, DEPTH, N_MIXERS))

def split_last(t, sizes):
    idx = [int(v) for v in np.cumsum(sizes)[:-1]]
    return jnp.split(t, idx, axis=-1)

def rms_norm(x, g, eps=EPS):
    xf = x.astype(F32)
    y = xf * lax.rsqrt(jnp.mean(xf * xf, axis=-1, keepdims=True) + eps)
    return (y * g.astype(F32)).astype(x.dtype)

def grid_positions(n):
    rows = n // GRID_W
    row = jnp.repeat(jnp.arange(rows, dtype=jnp.int32), GRID_W)
    col = jnp.tile(jnp.arange(GRID_W, dtype=jnp.int32), rows)
    return row, col

def _rope_1d(x, pos):
    half = x.shape[-1] // 2
    inv = ROPE_BASE ** (-jnp.arange(half, dtype=F32) / half)
    ang = pos.astype(F32)[:, None] * inv[None, :]
    cos = jnp.cos(ang)[:, None, :]
    sin = jnp.sin(ang)[:, None, :]
    xf = x.astype(F32)
    x1, x2 = xf[..., :half], xf[..., half:]
    return jnp.concatenate([x1 * cos - x2 * sin, x2 * cos + x1 * sin], axis=-1).astype(x.dtype)

def axial_rope(x, row, col):
    d = x.shape[-1] // 2
    return jnp.concatenate([_rope_1d(x[..., :d], row), _rope_1d(x[..., d:], col)], axis=-1)

def attention_blocks(q, k, v):
    b, lq, h, dk = q.shape
    hkv = k.shape[2]
    rep = h // hkv
    dv = v.shape[-1]
    scale = dk ** -0.5
    blk = min(Q_BLOCK, lq)
    nb = lq // blk
    qb = jnp.moveaxis(q.reshape(b, nb, blk, hkv, rep, dk), 1, 0)

    def one_block(qi):
        s = jnp.einsum('bqhrd,bkhd->bhrqk', qi, k, preferred_element_type=F32) * scale
        p = jax.nn.softmax(s, axis=-1).astype(v.dtype)
        return jnp.einsum('bhrqk,bkhe->bqhre', p, v)

    o = lax.map(one_block, qb)
    return jnp.moveaxis(o, 0, 1).reshape(b, lq, h, dv)

def modulation(cond, w, bias):
    m = jax.nn.silu(cond) @ w + bias
    return jnp.split(m, 3, axis=-1)

def mla_mixer(hc, hx, row, col, w_in, q_norm_g, w_uq, kv_norm_g, w_ukv, w_out):
    def project(h, rotate):
        b, n, _ = h.shape
        cq, ckv, kr, gate = split_last(h @ w_in, (MLA_Q_RANK, MLA_KV_RANK, MLA_ROPE, MLA_WIDTH))
        q = (rms_norm(cq, q_norm_g) @ w_uq).reshape(b, n, MLA_HEADS, MLA_NOPE + MLA_ROPE)
        kv = (rms_norm(ckv, kv_norm_g) @ w_ukv).reshape(b, n, MLA_HEADS, MLA_NOPE + MLA_V)
        q_nope, q_rope = q[..., :MLA_NOPE], q[..., MLA_NOPE:]
        k_nope, v = kv[..., :MLA_NOPE], kv[..., MLA_NOPE:]
        kr = kr[:, :, None, :]
        if rotate:
            q_rope = axial_rope(q_rope, row, col)
            kr = axial_rope(kr, row, col)
        k = jnp.concatenate([k_nope, jnp.broadcast_to(kr, (b, n, MLA_HEADS, MLA_ROPE))], axis=-1)
        q = jnp.concatenate([q_nope, q_rope], axis=-1)
        return q, k, v, gate

    qc, kc, vc, gc = project(hc, False)
    qx, kx, vx, gx = project(hx, True)
    oc = attention_blocks(qc, kc, vc)
    ox = attention_blocks(qx, jnp.concatenate([kc, kx], axis=1), jnp.concatenate([vc, vx], axis=1))

    def out(o, gate):
        b, n = gate.shape[:2]
        return (o.reshape(b, n, MLA_WIDTH) * jax.nn.silu(gate)) @ w_out

    return out(oc, gc), out(ox, gx)

def gla_chunk_scan(q, k, v, g, s0):
    b, l, h, dk = q.shape
    dv = v.shape[-1]
    c = GLA_CHUNK
    nc = l // c
    causal = jnp.tril(jnp.ones((c, c), dtype=bool))

    def to_chunks(t):
        return t.astype(F32).reshape(b, nc, c, h, t.shape[-1]).transpose(1, 0, 3, 2, 4)

    def step(s, inp):
        qc, kc, vc, gc = inp
        bc = jnp.cumsum(gc, axis=2)
        o_inter = jnp.einsum('bhcd,bhde->bhce', qc * jnp.exp(bc), s)
        diff = bc[:, :, :, None, :] - bc[:, :, None, :, :]
        decay = jnp.exp(jnp.where(causal[:, :, None], diff, -jnp.inf))
        a = jnp.einsum('bhid,bhijd->bhij', qc, kc[:, :, None, :, :] * decay)
        o = o_inter + jnp.einsum('bhij,bhje->bhie', a, vc)
        blast = bc[:, :, -1:, :]
        s_new = jnp.exp(blast[:, :, 0, :])[..., None] * s + jnp.einsum('bhcd,bhce->bhde', kc * jnp.exp(blast - bc), vc)
        return s_new, o

    s, o = lax.scan(step, s0, (to_chunks(q), to_chunks(k), to_chunks(v), to_chunks(g)))
    o = o.transpose(1, 0, 3, 2, 4).reshape(b, l, h, dv)
    return o, s

def gla_bidirectional(q, k, v, gf, gb, s0f, s0b):
    flip = lambda t: t[:, ::-1]
    of, sf = gla_chunk_scan(q, k, v, gf, s0f)
    ob, sb = gla_chunk_scan(flip(q), flip(k), flip(v), flip(gb), s0b)
    return of + flip(ob), sf, sb

def gla_mixer(hc, hx, w_in, w_gf, b_gf, w_gb, b_gb, o_norm_g, w_out):
    dk = GLA_DK // GLA_HEADS
    dv = GLA_DV // GLA_HEADS
    sizes = (GLA_DK, GLA_DK, GLA_DV, GLA_DV, GLA_GATE_RANK, GLA_GATE_RANK)

    def project(h):
        b, n, _ = h.shape
        q, k, v, gate, rf, rb = split_last(h @ w_in, sizes)
        heads = lambda t, d: t.reshape(b, n, GLA_HEADS, d)
        gf = jax.nn.log_sigmoid((rf @ w_gf + b_gf).astype(F32)) / GLA_GATE_NORM
        gb = jax.nn.log_sigmoid((rb @ w_gb + b_gb).astype(F32)) / GLA_GATE_NORM
        return heads(q, dk) * (dk ** -0.5), heads(k, dk), heads(v, dv), heads(gf, dk), heads(gb, dk), gate

    qc, kc, vc, gfc, gbc, gatec = project(hc)
    qx, kx, vx, gfx, gbx, gatex = project(hx)
    s0 = jnp.zeros((hc.shape[0], GLA_HEADS, dk, dv), F32)
    oc, sf, sb = gla_bidirectional(qc, kc, vc, gfc, gbc, s0, s0)
    ox, _, _ = gla_bidirectional(qx, kx, vx, gfx, gbx, sf, sb)

    def out(o, gate):
        b, n = gate.shape[:2]
        o = rms_norm(o.astype(gate.dtype), o_norm_g).reshape(b, n, GLA_DV)
        return (o * jax.nn.silu(gate)) @ w_out

    return out(oc, gatec), out(ox, gatex)

def gqa_mixer(hc, hx, row, col, w_in, q_norm_g, k_norm_g, w_out):
    kvw = GQA_KV_HEADS * GQA_HEAD_DIM

    def project(h, rotate):
        b, n, _ = h.shape
        q, k, v, gate = split_last(h @ w_in, (GQA_WIDTH, kvw, kvw, GQA_WIDTH))
        q = rms_norm(q.reshape(b, n, GQA_HEADS, GQA_HEAD_DIM), q_norm_g)
        k = rms_norm(k.reshape(b, n, GQA_KV_HEADS, GQA_HEAD_DIM), k_norm_g)
        v = v.reshape(b, n, GQA_KV_HEADS, GQA_HEAD_DIM)
        if rotate:
            q = axial_rope(q, row, col)
            k = axial_rope(k, row, col)
        return q, k, v, gate

    qc, kc, vc, gc = project(hc, False)
    qx, kx, vx, gx = project(hx, True)
    oc = attention_blocks(qc, kc, vc)
    ox = attention_blocks(qx, jnp.concatenate([kc, kx], axis=1), jnp.concatenate([vc, vx], axis=1))

    def out(o, gate):
        b, n = gate.shape[:2]
        return (o.reshape(b, n, GQA_WIDTH) * jax.nn.silu(gate)) @ w_out

    return out(oc, gc), out(ox, gx)

def dwconv_centred(u, w, bias):
    kw = w.shape[0]
    pad = kw // 2
    out = lax.conv_general_dilated(u, w[:, None, :], window_strides=(1,), padding=[(pad, kw - 1 - pad)],
                                   dimension_numbers=('NWC', 'WIO', 'NWC'), feature_group_count=u.shape[-1])
    return out + bias

def ssd_chunk_scan(x, dt, a, bm, cm, h0):
    b, l, h, p = x.shape
    g, n = bm.shape[2], bm.shape[3]
    rep = h // g
    c = SSD_CHUNK
    nc = l // c
    causal = jnp.tril(jnp.ones((c, c), dtype=bool))

    def to_chunks(t):
        return jnp.swapaxes(t.astype(F32).reshape(b, nc, c, *t.shape[2:]), 0, 1)

    def step(hs, inp):
        xc, dtc, bc, cc = inp
        la = jnp.cumsum(dtc * a, axis=1)
        xg = (xc * dtc[..., None]).reshape(b, c, g, rep, p)
        hg = hs.reshape(b, g, rep, p, n)
        y_inter = jnp.einsum('bcgn,bgrpn->bcgrp', cc, hg) * jnp.exp(la).reshape(b, c, g, rep)[..., None]
        diff = la[:, :, None, :] - la[:, None, :, :]
        lmat = jnp.exp(jnp.where(causal[None, :, :, None], diff, -jnp.inf)).reshape(b, c, c, g, rep)
        cb = jnp.einsum('bign,bjgn->bijg', cc, bc)
        y_intra = jnp.einsum('bijgr,bjgrp->bigrp', cb[..., None] * lmat, xg)
        dlast = jnp.exp(la[:, -1:, :] - la).reshape(b, c, g, rep)
        h_new = jnp.exp(la[:, -1, :]).reshape(b, g, rep)[..., None, None] * hg + \
            jnp.einsum('bcgrp,bcgn->bgrpn', dlast[..., None] * xg, bc)
        return h_new.reshape(b, h, p, n), (y_inter + y_intra).reshape(b, c, h, p)

    hs, y = lax.scan(step, h0, (to_chunks(x), to_chunks(dt), to_chunks(bm), to_chunks(cm)))
    return jnp.swapaxes(y, 0, 1).reshape(b, l, h, p), hs

def ssd_bidirectional(x, dtf, dtb, af, ab, bm, cm, h0f, h0b):
    flip = lambda t: t[:, ::-1]
    yf, hf = ssd_chunk_scan(x, dtf, af, bm, cm, h0f)
    yb, hb = ssd_chunk_scan(flip(x), flip(dtb), ab, flip(bm), flip(cm), h0b)
    return yf + flip(yb), hf, hb

def ssd_mixer(hc, hx, w_in, conv_w, conv_b, dt_bias_f, dt_bias_b, a_log_f, a_log_b, d_skip, gnorm_g, w_out):
    af = -jnp.exp(a_log_f.astype(F32))
    ab = -jnp.exp(a_log_b.astype(F32))
    gw = SSD_GROUPS * SSD_STATE

    def project(h):
        b, n, _ = h.shape
        z, xbc, dtf, dtb = split_last(h @ w_in, (SSD_INNER, SSD_XBC, SSD_HEADS, SSD_HEADS))
        xbc = jax.nn.silu(dwconv_centred(xbc, conv_w, conv_b))
        xs, bm, cm = split_last(xbc, (SSD_INNER, gw, gw))
        xs = xs.reshape(b, n, SSD_HEADS, SSD_HEAD_DIM)
        bm = bm.reshape(b, n, SSD_GROUPS, SSD_STATE)
        cm = cm.reshape(b, n, SSD_GROUPS, SSD_STATE)
        dtf = jax.nn.softplus(dtf.astype(F32) + dt_bias_f.astype(F32))
        dtb = jax.nn.softplus(dtb.astype(F32) + dt_bias_b.astype(F32))
        return z, xs, bm, cm, dtf, dtb

    zc, xsc, bmc, cmc, dtfc, dtbc = project(hc)
    zx, xsx, bmx, cmx, dtfx, dtbx = project(hx)
    h0 = jnp.zeros((hc.shape[0], SSD_HEADS, SSD_HEAD_DIM, SSD_STATE), F32)
    yc, hf, hb = ssd_bidirectional(xsc, dtfc, dtbc, af, ab, bmc, cmc, h0, h0)
    yx, _, _ = ssd_bidirectional(xsx, dtfx, dtbx, af, ab, bmx, cmx, hf, hb)

    def out(y, xs, z):
        b, n = z.shape[:2]
        y = y.astype(z.dtype) + xs * d_skip[:, None]
        y = y.reshape(b, n, SSD_INNER) * jax.nn.silu(z)
        y = rms_norm(y.reshape(b, n, SSD_GROUPS, SSD_INNER // SSD_GROUPS),
                     gnorm_g.reshape(SSD_GROUPS, SSD_INNER // SSD_GROUPS)).reshape(b, n, SSD_INNER)
        return y @ w_out

    return out(yc, xsc, zc), out(yx, xsx, zx)

def second_inputs(seed: int = 0) -> dict:
    key = jax.random.key(seed)
    ks = iter(jax.random.split(key, 64))
    nA, nB, nC, nD = (_n_layers_of(t) for t in range(N_MIXERS))

    def nrm(shape, fan_in, scale=1.0):
        return jax.random.normal(next(ks), shape, F32) * (scale * fan_in ** -0.5)

    def gain(shape):
        return 1.0 + 0.05 * jax.random.normal(next(ks), shape, F32)

    def small(shape, s=0.02):
        return s * jax.random.normal(next(ks), shape, F32)

    def dt_bias(shape):
        u = jax.random.uniform(next(ks), shape, F32)
        dt = jnp.exp(u * (math.log(0.1) - math.log(0.001)) + math.log(0.001))
        dt = jnp.maximum(dt, 1e-4)
        return dt + jnp.log(-jnp.expm1(-dt))

    def a_log(shape):
        return jnp.log(jax.random.uniform(next(ks), shape, F32, 1.0, 16.0))

    D = D_MODEL
    mla_in = MLA_Q_RANK + MLA_KV_RANK + MLA_ROPE + MLA_WIDTH
    gla_in = 2 * GLA_DK + 2 * GLA_DV + 2 * GLA_GATE_RANK
    gqa_in = 2 * GQA_WIDTH + 2 * GQA_KV_HEADS * GQA_HEAD_DIM
    ssd_in = SSD_INNER + SSD_XBC + 2 * SSD_HEADS
    return {
        "x": jax.random.normal(next(ks), (BATCH, SEQ, D), F32),
        "c": jax.random.normal(next(ks), (BATCH, D), F32),
        "ctx": jax.random.normal(next(ks), (BATCH, CTX_LEN, D), F32),
        "c_ctx": jax.random.normal(next(ks), (D,), F32),
        "ada_w": nrm((DEPTH, D, 3 * D), D, 0.5),
        "ada_b": small((DEPTH, 3 * D)),
        "norm_g": gain((DEPTH, D)),
        "final_g": gain((D,)),
        "mla_w_in": nrm((nA, D, mla_in), D),
        "mla_q_norm": gain((nA, MLA_Q_RANK)),
        "mla_w_uq": nrm((nA, MLA_Q_RANK, MLA_HEADS * (MLA_NOPE + MLA_ROPE)), MLA_Q_RANK),
        "mla_kv_norm": gain((nA, MLA_KV_RANK)),
        "mla_w_ukv": nrm((nA, MLA_KV_RANK, MLA_HEADS * (MLA_NOPE + MLA_V)), MLA_KV_RANK),
        "mla_w_out": nrm((nA, MLA_WIDTH, D), MLA_WIDTH),
        "gla_w_in": nrm((nB, D, gla_in), D),
        "gla_w_gf": nrm((nB, GLA_GATE_RANK, GLA_DK), GLA_GATE_RANK),
        "gla_b_gf": small((nB, GLA_DK), 0.1),
        "gla_w_gb": nrm((nB, GLA_GATE_RANK, GLA_DK), GLA_GATE_RANK),
        "gla_b_gb": small((nB, GLA_DK), 0.1),
        "gla_o_norm": gain((nB, GLA_DV // GLA_HEADS)),
        "gla_w_out": nrm((nB, GLA_DV, D), GLA_DV),
        "gqa_w_in": nrm((nC, D, gqa_in), D),
        "gqa_q_norm": gain((nC, GQA_HEAD_DIM)),
        "gqa_k_norm": gain((nC, GQA_HEAD_DIM)),
        "gqa_w_out": nrm((nC, GQA_WIDTH, D), GQA_WIDTH),
        "ssd_w_in": nrm((nD, D, ssd_in), D),
        "ssd_conv_w": nrm((nD, SSD_CONV, SSD_XBC), SSD_CONV),
        "ssd_conv_b": small((nD, SSD_XBC)),
        "ssd_dt_bias_f": dt_bias((nD, SSD_HEADS)),
        "ssd_dt_bias_b": dt_bias((nD, SSD_HEADS)),
        "ssd_a_log_f": a_log((nD, SSD_HEADS)),
        "ssd_a_log_b": a_log((nD, SSD_HEADS)),
        "ssd_d": gain((nD, SSD_HEADS)),
        "ssd_norm": gain((nD, SSD_INNER)),
        "ssd_w_out": nrm((nD, SSD_INNER, D), SSD_INNER),
    }

def second_block(x, c, ctx, c_ctx, ada_w, ada_b, norm_g, final_g,
              mla_w_in, mla_q_norm, mla_w_uq, mla_kv_norm, mla_w_ukv, mla_w_out,
              gla_w_in, gla_w_gf, gla_b_gf, gla_w_gb, gla_b_gb, gla_o_norm, gla_w_out,
              gqa_w_in, gqa_q_norm, gqa_k_norm, gqa_w_out,
              ssd_w_in, ssd_conv_w, ssd_conv_b, ssd_dt_bias_f, ssd_dt_bias_b,
              ssd_a_log_f, ssd_a_log_b, ssd_d, ssd_norm, ssd_w_out):
    row, col = grid_positions(x.shape[1])
    for i in range(DEPTH):
        kind, j = i % N_MIXERS, i // N_MIXERS
        sx, scx, gx = (m[:, None, :] for m in modulation(c, ada_w[i], ada_b[i]))
        sc, scc, gc = modulation(c_ctx, ada_w[i], ada_b[i])
        hx = rms_norm(x, norm_g[i]) * (1 + scx) + sx
        hc = rms_norm(ctx, norm_g[i]) * (1 + scc) + sc
        if kind == 0:
            yc, yx = mla_mixer(hc, hx, row, col, mla_w_in[j], mla_q_norm[j], mla_w_uq[j],
                               mla_kv_norm[j], mla_w_ukv[j], mla_w_out[j])
        elif kind == 1:
            yc, yx = gla_mixer(hc, hx, gla_w_in[j], gla_w_gf[j], gla_b_gf[j], gla_w_gb[j], gla_b_gb[j],
                               gla_o_norm[j], gla_w_out[j])
        elif kind == 2:
            yc, yx = gqa_mixer(hc, hx, row, col, gqa_w_in[j], gqa_q_norm[j], gqa_k_norm[j], gqa_w_out[j])
        else:
            yc, yx = ssd_mixer(hc, hx, ssd_w_in[j], ssd_conv_w[j], ssd_conv_b[j], ssd_dt_bias_f[j],
                               ssd_dt_bias_b[j], ssd_a_log_f[j], ssd_a_log_b[j], ssd_d[j], ssd_norm[j],
                               ssd_w_out[j])
        x = x + gx * yx
        if i < DEPTH - 1:
            ctx = ctx + gc * yc
    return rms_norm(x, final_g)


def setup_inputs(seed=0):
    out = dict(first_inputs(seed))
    for name, value in second_inputs(seed + 1).items():
        if name != "x":
            out[name + "_2"] = value
    return out


def reference(
    x, c, ada_w, ada_b, ffn_w13, ffn_w2, w_in, w_out, gdn_conv, gdn_a_log, gdn_dt_bias,
    gdn_norm, mlstm_conv, mlstm_i_bias, mlstm_f_bias, mlstm_norm, ln_g, ln_b, c_2, ctx_2,
    c_ctx_2, ada_w_2, ada_b_2, norm_g_2, final_g_2, mla_w_in_2, mla_q_norm_2, mla_w_uq_2,
    mla_kv_norm_2, mla_w_ukv_2, mla_w_out_2, gla_w_in_2, gla_w_gf_2, gla_b_gf_2, gla_w_gb_2,
    gla_b_gb_2, gla_o_norm_2, gla_w_out_2, gqa_w_in_2, gqa_q_norm_2, gqa_k_norm_2, gqa_w_out_2,
    ssd_w_in_2, ssd_conv_w_2, ssd_conv_b_2, ssd_dt_bias_f_2, ssd_dt_bias_b_2, ssd_a_log_f_2,
    ssd_a_log_b_2, ssd_d_2, ssd_norm_2, ssd_w_out_2,
):
    x = first_block(
        x, c, ada_w, ada_b, ffn_w13, ffn_w2, w_in, w_out, gdn_conv, gdn_a_log, gdn_dt_bias,
        gdn_norm, mlstm_conv, mlstm_i_bias, mlstm_f_bias, mlstm_norm, ln_g, ln_b,
    )
    return second_block(
        x, c_2, ctx_2, c_ctx_2, ada_w_2, ada_b_2, norm_g_2, final_g_2, mla_w_in_2, mla_q_norm_2,
        mla_w_uq_2, mla_kv_norm_2, mla_w_ukv_2, mla_w_out_2, gla_w_in_2, gla_w_gf_2, gla_b_gf_2,
        gla_w_gb_2, gla_b_gb_2, gla_o_norm_2, gla_w_out_2, gqa_w_in_2, gqa_q_norm_2,
        gqa_k_norm_2, gqa_w_out_2, ssd_w_in_2, ssd_conv_w_2, ssd_conv_b_2, ssd_dt_bias_f_2,
        ssd_dt_bias_b_2, ssd_a_log_f_2, ssd_a_log_b_2, ssd_d_2, ssd_norm_2, ssd_w_out_2,
    )


_drawn_inputs = setup_inputs


def setup_inputs(seed=0):
    import zlib

    import numpy as np

    out = dict(_drawn_inputs(seed))
    spreads = {}
    factors = {'ada_b': 3.015,
     'gdn_norm': 8.0,
     'mlstm_i_bias': 8.0,
     'mlstm_norm': 7.971,
     'ada_b_2': 2.808,
     'norm_g_2': 2.798,
     'mla_q_norm_2': 8.0,
     'mla_w_uq_2': 3.043,
     'mla_kv_norm_2': 8.0,
     'gla_b_gf_2': 7.374,
     'gla_b_gb_2': 8.0,
     'gla_o_norm_2': 5.885}
    for name, (base, spread) in spreads.items():
        noise = np.random.default_rng([zlib.crc32(name.encode()), seed]).standard_normal(out[name].shape)
        drawn = base * np.exp(spread * noise) if base else spread * noise
        out[name] = __import__('jax').numpy.asarray(drawn.astype(out[name].dtype))
    for name, factor in factors.items():
        out[name] = (out[name] * factor).astype(out[name].dtype)
    return out
```

```python
from contextlib import ExitStack

import numpy as np

import concourse.bass as bass
from concourse import mybir

ALU = mybir.AluOpType
ACT = mybir.ActivationFunctionType
AX = mybir.AxisListType
F32 = mybir.dt.float32

P = 128
T = 256
D = 1024
KT = D // P
DEPTH = 2
FF = 2816
FT = FF // P
ALPHA = (2 * DEPTH) ** 0.25
LN_EPS, EPS = 1e-5, 1e-6
NEG = -1e30
CHUNK = 2048
RING = 6
LEVELS = [1, 2, 4, 8, 16, 32, 64]
HD = 64
QS = HD ** -0.5
MLA_H, MLA_DK = 16, 96
MLA_SCALE = MLA_DK ** -0.5
GLA_H, GLA_SCALE = 4, P ** -0.5

GDN0, GA0, GB0, GZ0 = 0, 1152, 1158, 1164
MOBA0, MLQK0, MLV0, MLI0, MLF0, MLO0 = 1548, 2316, 3084, 3468, 3474, 3480
WIN_TILES = ([GDN0 + P * i for i in range(9)] + [GZ0 + P * i for i in range(3)] + [MOBA0 + P * i for i in range(4)]
             + [MLQK0 + P * i for i in range(6)] + [MLO0 + P * i for i in range(3)])
WIN_ORDER = [12] + list(range(12)) + [13, 14, 15]
ROW_A, ROW_B, ROW_I, ROW_F = 0, 32, 64, 96

COLS = {}
_at = 0
for _name, _n in [("c", 8), ("c2", 16), ("ada_b", 144), ("ada_b2", 48), ("ln_g", 48), ("ln_b", 48),
                  ("gconv", 72), ("mconv", 48), ("row_bias", 2), ("row_sign", 1), ("row_keep", 1), ("row_log", 2),
                  ("gdn_norm", 2), ("ml_norm", 6), ("norm_g", 16), ("final_g", 8), ("q_norm", 3), ("kv_norm", 2),
                  ("b_g", 8), ("o_norm", 2)]:
    COLS[_name] = (_at, _n)
    _at += _n
NCOLS = _at

TAB = {}
_at = 0
for _name, _n in [("ident", 128), ("ones", 256), ("blk", 128), ("first", 7 * 128), ("second", 7 * 128), ("strict", 128),
                  ("neg_t", 512), ("neg_q", 512), ("rope", 512), ("pair", 384)]:
    TAB[_name] = (_at, _n)
    _at += _n
NTAB = _at

WK = 26112
QKV, ZG, MQK, OG, VT, ROWS, COLT, MIX, SCR = 0, 3840, 4608, 5632, 6400, 7680, 9728, 9984, 12032


class Steps:

    def __init__(self, semaphore, found):
        self.semaphore, self.found, self.count = semaphore, found, 0

    def named(self, *key):
        self.count += 1
        if key:
            assert key not in self.found, key
            self.found[key] = (self.semaphore.name, self.count)


def build(nc, stream, cols_in, tab_in, wg_in, xt_in, ct_in, out, marks):
    found, order = {}, []
    with ExitStack() as ctx:
        def sb(name, shape):
            return ctx.enter_context(nc.sbuf_tensor(name, shape, F32))

        def sem(name):
            return ctx.enter_context(nc.semaphore(name))

        ring = sb("ring", [P, RING, CHUNK])
        res = sb("res", [P, KT, 2 * T])
        xm = sb("xm", [P, KT, 2 * T])
        tab = sb("tab", [P, NTAB])
        cols = sb("cols", [P, NCOLS])
        wk = sb("wk", [P, WK])
        wg = sb("wg", [48, 512])
        sc = sb("sc", [P, 24])
        mod = sb("mod", [P, 2, 48])
        aux = sb("aux", [P, 2, 32])
        small = sb("small", [P, 64])
        PS = ctx.enter_context(nc.psum_tensor("ps", [P, 8, 512], F32))

        tensor_done, scalar_done = sem("tensor_done"), sem("scalar_done")
        vector_done, gpsimd_done = sem("vector_done"), sem("gpsimd_done")
        signals = {"tensor_done": tensor_done, "scalar_done": scalar_done, "vector_done": vector_done, "gpsimd_done": gpsimd_done}
        params_in = sem("params_in")
        tokens_in = sem("tokens_in")
        out_stored = sem("out_stored")
        landed = [sem(f"chunk_landed_{i}") for i in range(RING)]

        def step(*key):
            return marks[key][1] if marks else 1

        def step_of(*key):
            return (signals[marks[key][0]], marks[key][1]) if marks else (vector_done, 1)

        def bank(b, lo=0, hi=512):
            return PS[:, b, lo:hi]

        def banks(b, n):
            return PS[:, :, :].rearrange("p b n -> p (b n)")[:, b * 512:b * 512 + n]

        def W(at, n):
            return wk[:, at:at + n]

        def table(name, lo=0, n=None):
            a, m = TAB[name]
            return tab[:, a + lo:a + lo + (m - lo if n is None else n)]

        def col(name, i=0, n=1):
            a, _ = COLS[name]
            return cols[:, a + i:a + i + n]

        def tiles(ap, n):
            return ap.rearrange("p (t n) -> p t n", n=n)

        def over(ap, k):
            return ap.unsqueeze(1).to_broadcast([ap.shape[0], k, ap.shape[1]])

        def each(ap, n):
            return ap.unsqueeze(2).to_broadcast([ap.shape[0], ap.shape[1], n])

        ident = table("ident")
        ones = table("ones", 0, 128)
        blk = table("blk")
        XS = slice(T, 2 * T)
        CS = slice(0, T)

        ff_ax, ff_res, ff_cen, ff_sq = W(SCR, 2048), W(SCR + 2048, 2048), W(SCR + 4096, 2048), W(SCR + 6144, 2048)
        ff_rstd = W(SCR + 8192, 256)
        ff_h = [W(SCR + 8704 + 256 * i, 256) for i in range(4)]
        ff_sil = [W(SCR + 9728 + 256 * i, 256) for i in range(2)]
        conv_tmp = [W(SCR + 256 * i, 256) for i in range(2)]
        qkv = tiles(W(QKV, 3840), 256)
        zg, mqk, og = tiles(W(ZG, 768), 256), tiles(W(MQK, 1024), 256), tiles(W(OG, 768), 256)
        vt = tiles(W(VT, 1280), 640)
        r_u, r_ab, r_ln, r_cs, r_rw, r_max, r_nm, r_beta = [W(ROWS + 256 * i, 256) for i in range(8)]
        colt = tiles(W(COLT, 256), 128)
        mix = tiles(W(MIX, 2048), 256)
        g_t, g_tt, g_dt, g_at, g_att = [W(SCR + 1536 * i, 1536) for i in range(5)]
        g_x = g_dt
        g0 = SCR + 7680
        g_eg, g_kb, g_vb, g_kg, g_qd = [tiles(W(g0 + 768 * i, 768), 256) for i in range(5)]
        g_kd, g_ekd = tiles(W(g0 + 3840, 384), 128), tiles(W(g0 + 4224, 384), 128)
        g_vbt = tiles(W(g0 + 4608, 768), 384)
        g_kdt = W(g0 + 5376, 384)
        g_vn = tiles(W(g0 + 1536, 768), 384)
        g_r1, g_s = W(g0 + 768, 384), W(g0 + 768 + 384, 192)
        o_sq, o_rstd, o_tmp = W(SCR, 768), W(SCR + 1536, 768), W(SCR + 3072, 768)
        m_s, m_pt = W(SCR, 2048), W(SCR + 2048, 2048)
        l_w = W(SCR, 3072)
        l_em, l_h, l_sq, l_rstd = [W(SCR + 4608 + 768 * i, 768) for i in range(4)]
        nm8, sm8 = small[:, 0:8], small[:, 8:16]
        glast = small[:, 16:19]
        rkeep = small[:, 20:21]
        rcoef = small[:, 22:24]

        k_h = tiles(W(0, 8192), 512)
        v_h = tiles(W(8192, 4096), 1024)
        gate2 = tiles(W(12288, 4096), 512)
        cq = tiles(W(16384, 2560), 512)
        q_h = [W(18944 + 512 * i, 512) for i in range(2)]
        p_h = [W(19968 + 1536 * i, 1536) for i in range(2)]
        pt_h = [W(23040 + 1536 * i, 1536) for i in range(2)]
        sq2 = W(0, 4096)
        rs2 = W(23040, 1024)
        rope_t = [W(24576, 512), W(25088, 512)]
        nmx = small[:, 24:32]
        rsm = small[:, 32:40]
        a_k = [tiles(W(0, 1024), 256), tiles(W(1024, 1024), 256)]
        a_q = tiles(W(2048, 1024), 256)
        a_gate = tiles(W(3072, 2048), 256)
        a_v = tiles(W(5120, 4096), 1024)
        a_b = [[tiles(W(9216 + 1024 * (2 * d + s), 1024), 256) for s in range(2)] for d in range(2)]
        a_u, a_ab = W(13312, 2048), W(15360, 2048)
        a_r = W(17408, 512)
        a_atd = W(17920, 1024)
        a_ato = [W(18944 + 512 * d, 512) for d in range(2)]
        a_st = tiles(W(19968, 2048), 256)
        a_qd = [tiles(W(22016 + 1024 * d, 1024), 256) for d in range(2)]
        a_e = [W(13312 + 1024 * i, 1024) for i in range(2)]
        a_m = [W(15360 + 1024 * i, 1024) for i in range(2)]
        a_kd, a_kdt = a_e, a_m
        a_o = W(13312, 2048)
        a_rs = W(24064, 1024)
        a_sq = W(15360, 2048)

        def mod_acc(m, ch):
            at = (19968 if m == 7 else SCR + 10240) + 1024 * (ch % 2)
            return tiles(W(at, 1024), 256)

        block = ctx.enter_context(nc.Block())

        @block.tensor
        def _(eng):
            done = Steps(tensor_done, found)
            last = [None]

            def mm(o, l, r, start, stop, free=False):
                last[0] = nc.tensor.matmul(o, l, r, start=start, stop=stop, skip_group_check=free)

            def turn(o, i, k=128):
                last[0] = nc.tensor.transpose(o, i, ident[0:k, 0:k])

            def row_tile(parity):
                if parity:
                    last[0].then_inc(tensor_done, 1)
                    done.named()
                    eng.wait_ge(tensor_done, done.count)

            def take(*tag):
                n = len(order)
                order.append(tag)
                eng.wait_ge(landed[n % RING], 16 * (n // RING + 1))
                return ring[:, n % RING, :]

            def release():
                last[0].then_inc(tensor_done, 1)
                done.named("chunk", len(order) - 1)

            def leave(*tag):
                found[("chunk_no",) + tag] = ("", len(order))
                order.append(tag)

            def mod_cols(m, ch):
                eng.wait_ge(gpsimd_done, step("modsum", m, ch))
                n = 1 if m < 6 else 2
                if ch == 0 and m:
                    eng.wait_ge(vector_done, step("mod", m - 1))
                for t in range(2):
                    for i in range(n):
                        c = (2 * ch + t) * n + i
                        mm(bank(7, c, c + 1), mod_acc(m, ch)[:, 2 * i, P * t:P * t + P], ones[:, 0:1], True, True)
                last[0].then_inc(tensor_done, 1)
                done.named("modcol", m, ch)
                if ch == 11:
                    found["modps", m] = found["modcol", m, ch]

            def ffn(l, f):
                m = 3 * l + 2 * f
                eng.wait_ge(scalar_done, step("xm_a", m))
                eng.wait_ge(vector_done, step("xm_d", m))
                for p in range(12):
                    if p < FT // 2:
                        for j in (2 * p, 2 * p + 1):
                            w = tiles(take("w13", l, f, j), 256)
                            b = 4 + j % 3
                            if j >= 3:
                                eng.wait_ge(vector_done, step("h", m, j - 3))
                            for half in range(2):
                                for k in range(KT):
                                    mm(bank(b, 256 * half, 256 * half + 256), w[:, k, P * half:P * half + P],
                                       xm[:, k, XS], k == 0, k == KT - 1)
                            release()
                            found["ab", m, j] = found["chunk", len(order) - 1]
                    if p >= 1:
                        w = tiles(take("w2", l, f, p - 1), D)
                        for i in range(2):
                            j = 2 * p - 2 + i
                            eng.wait_ge(vector_done, step("h", m, j))
                            for t in range(KT):
                                mm(bank(t // 2, 256 * (t % 2), 256 * (t % 2) + 256), w[:, i, P * t:P * t + P],
                                   ff_h[j % 4], j == 0 and t % 2 == 0, j == FT - 1, free=True)
                            if i:
                                release()
                                found["down", m, j] = found["down", m, j - 1] = found["chunk", len(order) - 1]
                    leave("ada", m + 1, p)
                    if p >= 1:
                        mod_cols(m + 1, p - 1)
                found["acc", m] = found["down", m, FT - 1]

            def norm_sums(m):
                for t in range(KT):
                    eng.wait_ge(vector_done, step("res", m, t))
                    mm(bank(4, 0, 256), ones, tiles(ff_res, 256)[:, t], t == 0, t == KT - 1)
                last[0].then_inc(tensor_done, 1)
                done.named("mu", m)
                if m % 3 != 1:
                    mod_cols(m + 1, 11)
                for t in range(KT):
                    eng.wait_ge(scalar_done, step("sq", m, t // 4))
                    mm(bank(5, 0, 256), ones, tiles(ff_sq, 256)[:, t], t == 0, t == KT - 1)
                last[0].then_inc(tensor_done, 1)
                done.named("var", m)

            def mixer(l):
                m = 3 * l + 1
                eng.wait_ge(scalar_done, step("xm_a", m))
                eng.wait_ge(vector_done, step("xm_d", m))
                for i, ch in enumerate(WIN_ORDER):
                    w = tiles(take("win", l, ch), 256)
                    b = i % 7
                    if i >= 7:
                        eng.wait_ge(*step_of("proj_read", m, i - 7))
                    if ch < 13:
                        for t in range(2):
                            for k in range(KT):
                                mm(bank(b, 256 * t, 256 * t + 256), w[:, k, P * t:P * t + P], xm[:, k, XS],
                                   k == 0, k == KT - 1)
                    else:
                        n = 256 if ch < 15 else 128
                        for t in range(2):
                            for k in range(KT):
                                mm(bank(b, n * t, n * t + n), xm[:, k, T + P * t:T + P * t + P], w[:, k, 0:n],
                                   k == 0, k == KT - 1)
                    release()
                    found["proj", m, i] = found["chunk", len(order) - 1]
                    if i < 12:
                        leave("ada", m + 1, i)
                    if 1 <= i < 13:
                        mod_cols(m + 1, i - 1)
                eng.wait_ge(*step_of("proj_read", m, 15))
                eng.wait_ge(*step_of("proj_read", m, 14))
                eng.wait_ge(*step_of("proj_read", m, 13))
                eng.wait_ge(vector_done, step("mod", m + 1))
                eng.wait_ge(*step_of("proj_read", m, 12))
                eng.wait_ge(*step_of("proj_read", m, 10))
                eng.wait_ge(*step_of("proj_read", m, 11))
                eng.wait_ge(*step_of("proj_read", m, 9))
                eng.wait_ge(scalar_done, step("l2sq", m))
                for t in range(6):
                    mm(banks(1, 1536)[:, 256 * t:256 * t + 256], blk, tiles(g_t, 256)[:, t], True, True)
                last[0].then_inc(tensor_done, 1)
                done.named("l2", m)
                eng.wait_ge(vector_done, step("rows", m))
                for t in range(2):
                    turn(bank(0, P * t, P * t + P), r_rw[:, P * t:P * t + P])
                for t in range(3):
                    mm(banks(4, 768)[:, 256 * t:256 * t + 256],
                       table("pair", P * t, P)[ROW_B:ROW_B + 32, :], r_beta[ROW_B:ROW_B + 32, :], True, True)
                for t in range(3):
                    mm(banks(6, 768)[:, 256 * t:256 * t + 256],
                       table("pair", P * t, P)[0:32, :], r_cs[0:32, :], True, True)
                last[0].then_inc(tensor_done, 1)
                done.named("pairs", m)
                eng.wait_ge(vector_done, step("l2_read", m))
                for h in range(6):
                    mm(banks(1, 1536)[:, 256 * h:256 * h + 256], each(ident[0:32, h:h + 1], 128)[:, 0, :], r_cs[0:32, :], True, True)
                last[0].then_inc(tensor_done, 1)
                done.named("gb", m)
                eng.wait_ge(vector_done, step("kb", m))
                eng.wait_ge(vector_done, step("gb_read", m))

                def head(ap, h, c=None):
                    a = ap[64 * (h % 2):64 * (h % 2) + 64, h // 2, :]
                    return a if c is None else a[:, P * c:P * c + P]
                K, Q = qkv[:, 3:6], qkv[:, 0:3]
                for h in [0, 2, 4, 1, 3, 5]:
                    if h == 1:
                        row_tile(1)
                    for c in range(2):
                        u = 2 * h + c
                        mm(banks(1, 1536)[:, P * u:P * u + P], head(K, h, c), head(g_kb, h, c), True, True)
                last[0].then_inc(tensor_done, 1)
                done.named("kk", m)
                eng.wait_ge(vector_done, step("pairs_read", m))
                eng.wait_ge(vector_done, step("gdn_in", m))
                for h in [0, 2, 4, 1, 3, 5]:
                    if h == 1:
                        row_tile(1)
                    for c in range(2):
                        u = 2 * h + c
                        mm(banks(4, 1536)[:, P * u:P * u + P], head(K, h, c), head(Q, h, c), True, True)
                last[0].then_inc(tensor_done, 1)
                done.named("qk", m)
                for c in range(2):
                    for t in range(3):
                        turn(bank(7 * c, P * t, P * t + P), g_vb[:, t, P * c:P * c + P])
                last[0].then_inc(tensor_done, 1)
                done.named("vbt", m)
                eng.wait_ge(scalar_done, step("vbt_read", m))
                for t in range(3):
                    turn(bank(0, P * t, P * t + P), g_kd[:, t, :])
                last[0].then_inc(tensor_done, 1)
                done.named("kdt", m)
                for li, s in enumerate(LEVELS):
                    for g in range(3):
                        eng.wait_ge(vector_done, step("t", m, li, g))
                        for u in range(4 * g, 4 * g + 4):
                            o = bank(1 + g, P * (u % 4), P * (u % 4) + P)
                            mm(o, g_at[:, P * u:P * u + P], g_t[:, P * u:P * u + P], True, True)
                        last[0].then_inc(tensor_done, 1)
                        done.named("x", m, li, g)
                    for g in range(3):
                        eng.wait_ge(vector_done, step("xs", m, li, g))
                        for u in range(4 * g, 4 * g + 4):
                            us = slice(P * u, P * u + P)
                            if li < 6:
                                mm(bank(1 + g, P * (u % 4), P * (u % 4) + P), g_tt[:, us], g_x[:, us], True, True)
                            mm(bank(4 + g, P * (u % 4), P * (u % 4) + P), g_x[:, us], g_tt[:, us], True, True)
                        last[0].then_inc(tensor_done, 1)
                        done.named("y", m, li, g)
                eng.wait_ge(vector_done, step("t", m, 7, 2))
                eng.wait_ge(vector_done, step("t", m, 7, 1))
                eng.wait_ge(vector_done, step("t", m, 7, 0))
                eng.wait_ge(scalar_done, step("kdt_read", m))

                def tt(h, c):
                    return g_tt[:, P * (2 * h + c):P * (2 * h + c) + P]
                for h in range(6):
                    mm(bank(0, 64 * h, 64 * h + 64), tt(h, 0), g_vbt[:, 0, 64 * h:64 * h + 64], True, True)
                last[0].then_inc(tensor_done, 1)
                done.named("vn0", m)
                eng.wait_ge(vector_done, step("vn0s", m))
                for h in range(6):
                    mm(PS[64 * (h % 2):64 * (h % 2) + 64, 7, 64 * (h // 2):64 * (h // 2) + 64],
                       g_kdt[:, 64 * h:64 * h + 64], g_vn[:, 0, 64 * h:64 * h + 64], True, True)
                last[0].then_inc(tensor_done, 1)
                done.named("s", m)
                eng.wait_ge(vector_done, step("ss", m))
                S = tiles(g_s, 64)
                for h in [0, 2, 4, 1, 3, 5]:
                    if h == 1:
                        row_tile(1)
                    mm(bank(0, 64 * h, 64 * h + 64), head(g_kg, h, 1), head(S, h), True, True)
                last[0].then_inc(tensor_done, 1)
                done.named("ks", m)
                eng.wait_ge(vector_done, step("r1", m))
                for h in range(6):
                    mm(bank(7, 64 * h, 64 * h + 64), tt(h, 1), g_r1[:, 64 * h:64 * h + 64], True, True)
                last[0].then_inc(tensor_done, 1)
                done.named("vn1", m)
                eng.wait_ge(vector_done, step("vn1s", m))
                for h in range(6):
                    for c in range(2):
                        o = banks(0, 1024)[64 * (h % 2):64 * (h % 2) + 64, 256 * (h // 2) + P * c:256 * (h // 2) + P * c + P]
                        u = 2 * h + c
                        mm(o, g_vn[:, c, 64 * h:64 * h + 64], g_att[:, P * u:P * u + P], True, c == 0)
                        if c:
                            mm(o, head(S, h), head(g_qd, h, 1), False, True)
                last[0].then_inc(tensor_done, 1)
                done.named("oa", m)
                eng.wait_ge(scalar_done, step("oa_sq", m))
                for t in range(3):
                    mm(banks(2, 1024)[:, 256 * t:256 * t + 256], blk, tiles(o_sq, 256)[:, t], True, True)
                last[0].then_inc(tensor_done, 1)
                done.named("oa_sum", m)
                for h in [0, 2, 1, 3]:
                    if h == 1:
                        row_tile(1)
                    for t in range(2):
                        u = 2 * h + t
                        mm(banks(4, 2048)[:, 256 * u:256 * u + 256], head(mqk[:, 0:2], h, t), head(mqk[:, 2:4], h), True, True)
                last[0].then_inc(tensor_done, 1)
                done.named("ms", m)
                eng.wait_ge(vector_done, step("mp", m))
                eng.wait_ge(vector_done, step("oa_done", m))
                for h in range(4):
                    for q in range(2):
                        for k in range(2):
                            at = 512 * h + 256 * k + P * q
                            turn(banks(0, 2048)[:, at:at + P], m_s[:, 512 * h + 256 * q + P * k:512 * h + 256 * q + P * k + P])
                last[0].then_inc(tensor_done, 1)
                done.named("mpt", m)
                eng.wait_ge(scalar_done, step("mpts", m))
                for h in range(4):
                    o = PS[64 * (h % 2):64 * (h % 2) + 64, 4, 256 * (h // 2):256 * (h // 2) + 256]
                    for k in range(2):
                        mm(o, vt[:, k, 64 * h:64 * h + 64], m_pt[:, 512 * h + 256 * k:512 * h + 256 * k + 256], k == 0, k == 1)
                last[0].then_inc(tensor_done, 1)
                done.named("mo", m)
                for h in range(6):
                    mm(banks(0, 1536)[:, 256 * h:256 * h + 256],
                       each(ident[ROW_I:ROW_I + 32, ROW_I + h:ROW_I + h + 1], 128)[:, 0, :], r_max[ROW_I:ROW_I + 32, :], True, True)
                eng.wait_ge(scalar_done, step("mo_read", m))
                for t in range(3):
                    mm(banks(3, 1024)[:, 256 * t:256 * t + 256],
                       table("pair", P * t, P)[ROW_I:ROW_I + 32, :], r_nm[ROW_I:ROW_I + 32, :], True, True)
                last[0].then_inc(tensor_done, 1)
                done.named("mb", m)
                eng.wait_ge(vector_done, step("mb_read", m))
                eng.wait_ge(scalar_done, step("em", m))
                for h in [0, 2, 4, 1, 3, 5]:
                    if h == 1:
                        row_tile(1)
                    for st in range(2):
                        u = 2 * h + st
                        mm(banks(0, 3072)[:, 256 * u:256 * u + 256], head(qkv[:, 12:15], h, st), head(qkv[:, 9:12], h), True, True)
                last[0].then_inc(tensor_done, 1)
                done.named("ls", m)
                eng.wait_ge(vector_done, step("lp", m))
                for what in range(2):
                    for h in range(6):
                        o = banks(6 if what == 0 else 0, 1024)[64 * (h % 2):64 * (h % 2) + 64, 256 * (h // 2):256 * (h // 2) + 256]
                        for st in range(2):
                            lhs = vt[:, st, 256 + 64 * h:256 + 64 * h + 64] if what == 0 else ones[:, 0:64]
                            mm(o, lhs, l_w[:, 512 * h + 256 * st:512 * h + 256 * st + 256], st == 0, st == 1)
                last[0].then_inc(tensor_done, 1)
                done.named("lo", m)
                eng.wait_ge(vector_done, step("lh", m))
                for t in range(3):
                    mm(banks(2, 1024)[:, 256 * t:256 * t + 256], blk, tiles(l_h, 256)[:, t], True, True)
                last[0].then_inc(tensor_done, 1)
                done.named("lmu", m)
                eng.wait_ge(scalar_done, step("lsq", m))
                for t in range(3):
                    mm(banks(4, 1024)[:, 256 * t:256 * t + 256], blk, tiles(l_sq, 256)[:, t], True, True)
                last[0].then_inc(tensor_done, 1)
                done.named("lvar", m)
                eng.wait_ge(vector_done, step("mixed", m))
                eng.wait_ge(scalar_done, step("mixed_a", m))
                for ch in range(4):
                    w = tiles(take("wout", l, ch), 256)
                    for t in range(2):
                        for k in range(KT):
                            mm(bank(ch, 256 * t, 256 * t + 256), w[:, k, P * t:P * t + P], mix[:, k], k == 0, k == KT - 1)
                    release()
                found["acc", m] = found["chunk", len(order) - 1]

            def rms(m):
                for t in range(KT):
                    eng.wait_ge(scalar_done, step("sq2", m, t // 4))
                    mm(bank(6), ones, tiles(sq2, 512)[:, t], t == 0, t == KT - 1)
                last[0].then_inc(tensor_done, 1)
                done.named("ms2", m)

            def mla():
                m = 6
                rms(m)
                eng.wait_ge(scalar_done, step("xm_a", m))
                eng.wait_ge(vector_done, step("xm_d", m))
                for i in range(7):
                    w = tiles(take("mla_in", i), 256)
                    for t in range(2):
                        n = 2 * i + t
                        if n >= 6:
                            eng.wait_ge(*step_of("in2_read", m, n - 6))
                        for k in range(KT):
                            mm(bank(n % 6), w[:, k, P * t:P * t + P], xm[:, k, :], k == 0, k == KT - 1)
                        if t == 0:
                            last[0].then_inc(tensor_done, 1)
                            done.named("in2", m, n)
                    release()
                    found["in2", m, 2 * i + 1] = found["chunk", len(order) - 1]
                    for c in ((2 * i, 2 * i + 1) if i < 6 else ()):
                        leave("ada", 7, c)
                    for c in ((2 * i - 2, 2 * i - 1) if i else ()):
                        mod_cols(7, c)
                for n in range(8, 14):
                    eng.wait_ge(*step_of("in2_read", m, n))
                eng.wait_ge(scalar_done, step("cqsq", m))
                for t in range(3):
                    mm(bank(0), ones, tiles(W(0, 2560), 512)[:, t], t == 0, t == 2)
                for t in range(3, 5):
                    mm(bank(1), ones, tiles(W(0, 2560), 512)[:, t], t == 3, t == 4)
                last[0].then_inc(tensor_done, 1)
                done.named("cqsum", m)
                eng.wait_ge(vector_done, step("cqn", m))
                w = tiles(take("ukn"), D)
                for t in range(8):
                    b = 2 + t % 4
                    if t >= 4:
                        eng.wait_ge(*step_of("kn_read", t - 4, 0))
                        eng.wait_ge(*step_of("kn_read", t - 4, 1))
                    for k in range(2):
                        mm(bank(b), w[:, k, P * t:P * t + P], cq[:, 3 + k, :], k == 0, k == 1)
                    if t < 7:
                        last[0].then_inc(tensor_done, 1)
                        done.named("kn", t)
                release()
                found["kn", 7] = found["chunk", len(order) - 1]
                w = tiles(take("ukv"), D)
                for t in range(4):
                    for half in range(2):
                        n = 2 * t + half
                        b = 2 + n % 4
                        if n < 4:
                            eng.wait_ge(*step_of("kn_read", 4 + n, 0))
                            eng.wait_ge(*step_of("kn_read", 4 + n, 1))
                        else:
                            eng.wait_ge(*step_of("v2_read", n - 4))
                        for k in range(2):
                            mm(bank(b), cq[:, 3 + k, P * t:P * t + P], w[:, k, 512 * half:512 * half + 512], k == 0, k == 1)
                        if n < 7:
                            last[0].then_inc(tensor_done, 1)
                            done.named("v2", n)
                release()
                found["v2", 7] = found["chunk", len(order) - 1]
                for n in range(8):
                    eng.wait_ge(*step_of("v2_read", n))
                eng.wait_ge(scalar_done, step("k_rope"))
                eng.wait_ge(vector_done, step("mod", 7))

                wq = [None]

                def scores(h):
                    if h % 4 == 0:
                        wq[0] = take("uq", h // 4)[:, 0:1536].rearrange("p (k n) -> p k n", k=3)
                    hh = h % 4
                    if h:
                        eng.wait_ge(vector_done, step("q_read", h - 1))
                    for k in range(3):
                        mm(bank(0), wq[0][:, k, P * hh:P * hh + P], cq[:, k, :], k == 0, k == 2)
                    if hh == 3:
                        release()
                        found["q2", h] = found["chunk", len(order) - 1]
                    else:
                        last[0].then_inc(tensor_done, 1)
                        done.named("q2", h)
                    eng.wait_ge(vector_done, step("q_read", h))
                    if h:
                        eng.wait_ge(scalar_done, step("exp2", h - 1))
                    for t in range(2):
                        mm(bank(2, 256 * t, 256 * t + 256), q_h[h % 2][0:96, P * t:P * t + P], k_h[0:96, h, CS], True, True)
                    for t in range(2):
                        mm(bank(3 + t), q_h[h % 2][0:96, T + P * t:T + P * t + P], k_h[0:96, h, :], True, True)
                    last[0].then_inc(tensor_done, 1)
                    done.named("s2", h)

                scores(0)
                for h in range(MLA_H):
                    if h + 1 < MLA_H:
                        scores(h + 1)
                    eng.wait_ge(gpsimd_done, step("pn", h))
                    if h:
                        eng.wait_ge(scalar_done, step("pt_a", h - 1))
                        eng.wait_ge(vector_done, step("pt_d", h - 1))
                    for q in range(2):
                        for k in range(2):
                            turn(bank(5, 256 * k + P * q, 256 * k + P * q + P), p_h[h % 2][:, 256 * q + P * k:256 * q + P * k + P])
                    for q in range(2):
                        for k in range(4):
                            at = 256 * k + P * q
                            turn(banks(6, 1024)[:, at:at + P], p_h[h % 2][:, 512 + 512 * q + P * k:512 + 512 * q + P * k + P])
                    last[0].then_inc(tensor_done, 1)
                    done.named("pt", h)
                    eng.wait_ge(scalar_done, step("pt_a", h))
                    eng.wait_ge(vector_done, step("pt_d", h))
                    if h % 2 == 0 and h:
                        eng.wait_ge(vector_done, step("o_read", h // 2 - 1))
                    pt = pt_h[h % 2]
                    hp = slice(64 * (h % 2), 64 * (h % 2) + 64)
                    for k in range(2):
                        mm(PS[hp, 1, 0:256], v_h[:, k, 64 * h:64 * h + 64], pt[:, 256 * k:256 * k + 256], k == 0, k == 1)
                    for k in range(4):
                        mm(PS[hp, 1, 256:512], v_h[:, k, 64 * h:64 * h + 64], pt[:, 512 + 256 * k:768 + 256 * k], k == 0, k == 3)
                    last[0].then_inc(tensor_done, 1)
                    done.named("o2", h)
                eng.wait_ge(vector_done, step("o_read", 7))
                for ch in range(4):
                    w = tiles(take("wout2", 0, ch), 256)
                    for t in range(2):
                        n = 2 * ch + t
                        b = 2 + n % 4
                        if n >= 4:
                            eng.wait_ge(vector_done, step("res2", m, n - 4))
                        for k in range(KT):
                            mm(bank(b), w[:, k, P * t:P * t + P], xm[:, k, :], k == 0, k == KT - 1)
                        if t == 0:
                            last[0].then_inc(tensor_done, 1)
                            done.named("y2", m, n)
                    release()
                    found["y2", m, 2 * ch + 1] = found["chunk", len(order) - 1]

            def gla():
                m = 7
                rms(m)
                eng.wait_ge(scalar_done, step("xm_a", m))
                eng.wait_ge(vector_done, step("xm_d", m))
                for i in range(9):
                    w = tiles(take("gla_in", i), 256)
                    for t in range(2):
                        n = 2 * i + t
                        if n == 17:
                            break
                        if n >= 6:
                            eng.wait_ge(*step_of("in2_read", m, n - 6))
                        cs = slice(0, 512) if n < 5 else XS
                        for k in range(KT):
                            mm(bank(n % 6, 0, 512 if n < 5 else 256), w[:, k, P * t:P * t + P], xm[:, k, cs], k == 0, k == KT - 1)
                        if t == 0 and n < 16:
                            last[0].then_inc(tensor_done, 1)
                            done.named("in2", m, n)
                    release()
                    found["in2", m, min(2 * i + 1, 16)] = found["chunk", len(order) - 1]
                for ch in range(4):
                    w = tiles(take("gla_v", ch), 256)
                    for t in range(4):
                        n = 17 + 2 * ch + t // 2
                        if t % 2 == 0:
                            eng.wait_ge(*step_of("in2_read", m, n - 6))
                        at = 256 * (t % 2)
                        for k in range(KT):
                            mm(bank(n % 6, at, at + 256), xm[:, k, P * t:P * t + P], w[:, k, :], k == 0, k == KT - 1)
                        if t == 1:
                            last[0].then_inc(tensor_done, 1)
                            done.named("in2", m, n)
                    release()
                    found["in2", m, 18 + 2 * ch] = found["chunk", len(order) - 1]
                for n in range(19, 25):
                    eng.wait_ge(*step_of("in2_read", m, n))
                for d in range(2):
                    for t in range(4):
                        mm(bank(4 * d + t), wg[32 * d:32 * d + 16, P * t:P * t + P], a_r[32 * d:32 * d + 16, :], True, True)
                    last[0].then_inc(tensor_done, 1)
                    done.named("ga", d)
                for d in range(2):
                    eng.wait_ge(vector_done, step("kd", d))
                    eng.wait_ge(vector_done, step("ga_read", d))
                    for t in range(2):
                        for h in range(4):
                            turn(bank(t, P * h, P * h + P) if d == 0 else bank(4 + t, P * h, P * h + P),
                                 tiles(a_kd[d], 256)[:, h, P * t:P * t + P])
                    last[0].then_inc(tensor_done, 1)
                    done.named("akdt", d)
                    eng.wait_ge(scalar_done, step("akdts", d))
                    for h in range(4):
                        o = banks(2 + 4 * d, 1024)[:, 256 * h:256 * h + 256]
                        for t in range(2):
                            mm(o, a_kdt[d][:, 512 * t + P * h:512 * t + P * h + P], a_v[:, t, 256 * h:256 * h + 256], t == 0, t == 1)
                    last[0].then_inc(tensor_done, 1)
                    done.named("ast", d)
                for h in range(4):
                    for t in range(2):
                        u = 2 * h + t
                        mm(banks(0, 1024)[:, P * u:P * u + P], a_k[1][:, h, P * t:P * t + P], a_q[:, h, P * t:P * t + P], True, True)
                last[0].then_inc(tensor_done, 1)
                done.named("diag")
                n = 0
                for li in range(8):
                    for d in range(2):
                        eng.wait_ge(vector_done, step("z", n))
                        eng.wait_ge(vector_done, step("lev_read", n - 1))
                        eng.wait_ge(scalar_done, step("ast_read", 1))
                        z = tiles(a_e[n % 2], 256)
                        b = 0 if n % 2 else 2
                        for h in range(4):
                            if li < 7:
                                for t in range(2):
                                    u = 2 * h + t
                                    zz = z[:, h, P * t:P * t + P]
                                    mm(banks(b, 1024)[:, P * u:P * u + P], zz, zz, True, True)
                            else:
                                k_, q_ = (z[:, h, 0:P], z[:, h, P:T]) if d == 0 else (z[:, h, P:T], z[:, h, 0:P])
                                mm(bank(b, P * h, P * h + P), k_, q_, True, True)
                        last[0].then_inc(tensor_done, 1)
                        done.named("lev", n)
                        n += 1
                eng.wait_ge(gpsimd_done, step("at_done"))
                eng.wait_ge(vector_done, step("lev_read", 14))
                eng.wait_ge(vector_done, step("lev_read", 15))
                eng.wait_ge(vector_done, step("aqd", 0))
                eng.wait_ge(vector_done, step("aqd", 1))
                for h in range(4):
                    for dvh in range(2):
                        lo = 256 * h + P * dvh
                        for t in range(2):
                            o = banks(4, 2048)[:, 2 * lo + P * t:2 * lo + P * t + P]
                            u = 2 * h + t
                            mm(o, a_v[:, 2 + t, lo:lo + P], a_atd[:, P * u:P * u + P], True, False)
                            mm(o, a_v[:, 3 - t, lo:lo + P], a_ato[1 - t][:, P * h:P * h + P], False, False)
                            for d in range(2):
                                mm(o, a_st[:, 4 * d + h, P * dvh:P * dvh + P], a_qd[d][:, h, P * t:P * t + P], False, d == 1)
                last[0].then_inc(tensor_done, 1)
                done.named("ao")
                eng.wait_ge(scalar_done, step("aosq"))
                for h in range(4):
                    for dvh in range(2):
                        mm(banks(0, 1024)[:, 256 * h:256 * h + 256], ones, tiles(a_sq, 256)[:, 2 * h + dvh], dvh == 0, dvh == 1)
                last[0].then_inc(tensor_done, 1)
                done.named("aosum")
                eng.wait_ge(vector_done, step("aod"))
                for ch in range(4):
                    w = tiles(take("wout2", 1, ch), 256)
                    for t in range(2):
                        n = 2 * ch + t
                        for k in range(KT):
                            mm(bank(4 + ch, 256 * t, 256 * t + 256), w[:, k, P * t:P * t + P], xm[:, k, XS], k == 0, k == KT - 1)
                    release()
                    found["y2", m, ch] = found["chunk", len(order) - 1]
                for t in range(KT):
                    eng.wait_ge(scalar_done, step("fsq"))
                    mm(bank(0, 0, 256), ones, tiles(ff_sq, 256)[:, t], t == 0, t == KT - 1)
                last[0].then_inc(tensor_done, 1)
                done.named("fsum")

            eng.wait_ge(params_in, 48)
            for ch in range(12):
                leave("ada", 0, ch)
                mod_cols(0, ch)
            for l in range(DEPTH):
                ffn(l, 0)
                norm_sums(3 * l)
                mixer(l)
                norm_sums(3 * l + 1)
                ffn(l, 1)
                norm_sums(3 * l + 2)
            mla()
            gla()

        @block.sync
        def _(eng):
            eng.dma_start(cols[:, :], cols_in).then_inc(params_in, 16)
            eng.dma_start(tab[:, :], tab_in).then_inc(params_in, 16)
            eng.dma_start(wg[:, :], wg_in).then_inc(params_in, 16)
            eng.dma_start(res[:, :, XS], xt_in.rearrange("(k p) t -> p k t", p=P)).then_inc(tokens_in, 16)
            eng.dma_start(res[:, :, CS], ct_in.rearrange("(k p) t -> p k t", p=P)).then_inc(tokens_in, 16)
            for n in range(stream.shape[0]):
                if n >= RING:
                    eng.wait_ge(*step_of("chunk", n - RING))
                eng.dma_start(ring[:, n % RING, :], stream[n]).then_inc(landed[n % RING], 16)
            eng.wait_ge(vector_done, step("final"))
            eng.dma_start(out.rearrange("(k p) t -> p k t", p=P), tiles(ff_cen, 256)).then_inc(out_stored, 16)
            eng.wait_ge(out_stored, 16)

        @block.scalar
        def _(eng):
            done = Steps(scalar_done, found)

            def act(o, i, f, *key, **kw):
                done.named(*key)
                return nc.scalar.activation(o, i, f, **kw)

            def rsqrt(ap, *key):
                eng.wait_ge(scalar_done, done.count)
                act(ap, ap, ACT.Ln).then_inc(scalar_done, 1)
                eng.wait_ge(scalar_done, done.count)
                act(ap, ap, ACT.Exp, *key, scale=-0.5).then_inc(scalar_done, 1)

            def affine(m, o, i, scale, bias, kts, *key):
                for t in kts:
                    act(o[:, t], i[:, t], ACT.Identity, *(key if t == kts[-1] else ()),
                        scale=scale[:, t:t + 1], bias=bias[:, t:t + 1]).then_inc(scalar_done, 1)

            def modulate(m):
                eng.wait_ge(scalar_done, done.count)
                x = aux[:, m % 2, :]
                eng.wait_ge(vector_done, step("aux", m))
                eng.wait_ge(vector_done, step("x_d", m))
                if m > 0:
                    eng.wait_ge(tensor_done, step("acc", m - 1))
                affine(m, xm[:, :, XS], res[:, :, XS], x[:, 0:8], mod[:, m % 2, 0:8], range(0, 4), "xm_a", m)

            def norm(m):
                l, s = m // 3, m % 3
                for half in range(2):
                    eng.wait_ge(vector_done, step("cen", m))
                    act(ff_sq[:, 1024 * half:1024 * half + 1024], ff_cen[:, 1024 * half:1024 * half + 1024], ACT.Square, "sq", m, half).then_inc(scalar_done, 1)
                eng.wait_ge(vector_done, step("ve", m))
                rsqrt(ff_rstd, "rstd", m)
                eng.wait_ge(vector_done, step("xn", m))
                g0_, b0_ = COLS["ln_g"][0] + 8 * m, COLS["ln_b"][0] + 8 * m
                affine(m, res[:, :, XS], tiles(ff_cen, 256), cols[:, g0_:g0_ + 8], cols[:, b0_:b0_ + 8], range(0, 4), "x_a", m)

            def ffn(l, f):
                m = 3 * l + 2 * f
                modulate(m)
                eng.wait_ge(scalar_done, done.count)
                act(tiles(ff_ax, 256), res[:, :, XS], ACT.Copy, "ax", m, scale=ALPHA).then_inc(scalar_done, 1)
                for j in range(FT):
                    eng.wait_ge(tensor_done, step("ab", m, j))
                    if j >= 2:
                        eng.wait_ge(vector_done, step("h", m, j - 2))
                    act(ff_sil[j % 2], bank(4 + j % 3, 0, 256), ACT.Silu, "sil", m, j).then_inc(scalar_done, 1)
                norm(m)

            def mixer(l):
                m = 3 * l + 1
                modulate(m)
                for i, ch in enumerate(WIN_ORDER):
                    b = i % 7
                    eng.wait_ge(tensor_done, step("proj", m, i))
                    key = ("proj_read", m, i)
                    if ch in (12, 4):
                        key = ("proj_read_a", m, i)
                    if ch < 13:
                        todo = [t for t in (2 * ch, 2 * ch + 1) if 9 <= t < 16 or 22 <= t < 25]
                        for t in todo:
                            src = bank(b, 256 * (t % 2), 256 * (t % 2) + 256)
                            k = key if t == todo[-1] else ()
                            if t < 12:
                                act(zg[:, t - 9], src, ACT.Silu, *k).then_inc(scalar_done, 1)
                            elif t < 16:
                                act(mqk[:, t - 12], src, ACT.Copy, *k).then_inc(scalar_done, 1)
                            else:
                                act(og[:, t - 22], src, ACT.Sigmoid, *k).then_inc(scalar_done, 1)
                    else:
                        n = 256 if ch < 15 else 128
                        act(vt[:, :, 256 * (ch - 13):256 * (ch - 13) + n], tiles(bank(b, 0, 2 * n), n), ACT.Copy, *key).then_inc(scalar_done, 1)
                    if ch < 5:
                        for t in (2 * ch, 2 * ch + 1):
                            if t < 9:
                                eng.wait_ge(vector_done, step("conv", m, t))
                                act(qkv[:, t], qkv[:, t], ACT.Silu, *(("silu", m, t))).then_inc(scalar_done, 1)
                    if 8 <= ch < 11:
                        for t in (2 * ch, 2 * ch + 1):
                            eng.wait_ge(vector_done, step("conv", m, t))
                            act(qkv[:, t - 7], qkv[:, t - 7], ACT.Silu, "silu", m, t).then_inc(scalar_done, 1)
                eng.wait_ge(vector_done, step("rab", m))
                eng.wait_ge(scalar_done, done.count)
                act(r_ln, r_ab, ACT.Exp, scale=-1.0).then_inc(scalar_done, 1)
                eng.wait_ge(scalar_done, done.count)
                act(r_ln, r_ln, ACT.Ln, "rln", m, bias=1.0).then_inc(scalar_done, 1)
                eng.wait_ge(scalar_done, done.count)
                act(r_beta[32:64, :], r_u[32:64, :], ACT.Exp, "rbe", m).then_inc(scalar_done, 1)
                eng.wait_ge(scalar_done, done.count)
                act(rcoef[:, 0:1], col("row_log", l), ACT.Exp, "rco", m).then_inc(scalar_done, 1)
                eng.wait_ge(scalar_done, done.count)
                act(g_t, W(QKV, 1536), ACT.Square, "l2sq", m).then_inc(scalar_done, 1)
                eng.wait_ge(vector_done, step("l2e", m))
                rsqrt(g_tt, "ri", m)
                eng.wait_ge(tensor_done, step("pairs", m))
                eng.wait_ge(vector_done, step("glast", m))
                eng.wait_ge(scalar_done, done.count)
                act(W(g0, 768), banks(6, 768), ACT.Exp, "eg", m).then_inc(scalar_done, 1)
                for t in range(3):
                    act(g_ekd[:, t, :], banks(6, 768)[:, 256 * t:256 * t + P], ACT.Exp, *(("ekd", m) if t == 2 else ()),
                        scale=-1.0, bias=glast[:, t:t + 1]).then_inc(scalar_done, 1)
                eng.wait_ge(vector_done, step("gb_read", m))
                eng.wait_ge(vector_done, step("colt", m))
                for h in range(6):
                    for c in range(2):
                        u = slice(P * (2 * h + c), P * (2 * h + c) + P)
                        act(g_dt[:, u], g_dt[:, u], ACT.Exp, *(("dt", m) if h + c == 6 else ()), bias=colt[:, c, h:h + 1]).then_inc(scalar_done, 1)
                eng.wait_ge(tensor_done, step("vbt", m))
                act(g_vbt[:, 0, :], bank(0, 0, 384), ACT.Copy).then_inc(scalar_done, 1)
                act(g_vbt[:, 1, :], bank(7, 0, 384), ACT.Copy, "vbt_read", m).then_inc(scalar_done, 1)
                eng.wait_ge(tensor_done, step("kdt", m))
                act(g_kdt, bank(0, 0, 384), ACT.Copy, "kdt_read", m).then_inc(scalar_done, 1)
                eng.wait_ge(tensor_done, step("oa", m))
                act(o_sq, banks(0, 768), ACT.Square, "oa_sq", m).then_inc(scalar_done, 1)
                eng.wait_ge(vector_done, step("oa_e", m))
                rsqrt(o_rstd, "oa_r", m)
                eng.wait_ge(vector_done, step("msub", m))
                eng.wait_ge(scalar_done, done.count)
                act(m_s, m_s, ACT.Exp, "mexp", m).then_inc(scalar_done, 1)
                eng.wait_ge(tensor_done, step("mpt", m))
                eng.wait_ge(scalar_done, done.count)
                act(m_pt, banks(0, 2048), ACT.Copy, "mpts", m).then_inc(scalar_done, 1)
                eng.wait_ge(tensor_done, step("mo", m))
                eng.wait_ge(scalar_done, done.count)
                act(mix[:, 3:5, :], tiles(bank(4), 256), ACT.Copy, "mo_read", m).then_inc(scalar_done, 1)
                eng.wait_ge(tensor_done, step("mb", m))
                eng.wait_ge(scalar_done, done.count)
                act(l_em, banks(3, 768), ACT.Exp, "em", m).then_inc(scalar_done, 1)
                eng.wait_ge(vector_done, step("mb_read", m))
                for h in range(6):
                    for st in range(2):
                        u = slice(256 * (2 * h + st), 256 * (2 * h + st) + 256)
                        act(l_w[:, u], l_w[:, u], ACT.Exp, *(("lw", m) if h + st == 6 else ()),
                            bias=colt[:, st, ROW_I + h:ROW_I + h + 1]).then_inc(scalar_done, 1)
                eng.wait_ge(vector_done, step("lcen", m))
                eng.wait_ge(scalar_done, done.count)
                act(l_sq, l_h, ACT.Square, "lsq", m).then_inc(scalar_done, 1)
                eng.wait_ge(vector_done, step("lve", m))
                rsqrt(l_rstd, "mixed_a", m)
                eng.wait_ge(vector_done, step("mixed", m))
                eng.wait_ge(tensor_done, step("acc", m))
                eng.wait_ge(scalar_done, done.count)
                act(tiles(ff_ax, 256), res[:, :, XS], ACT.Copy, "ax", m, scale=ALPHA).then_inc(scalar_done, 1)
                norm(m)

            def rms(m):
                if m == 6:
                    eng.wait_ge(tensor_done, step("acc", 5))
                else:
                    eng.wait_ge(vector_done, step("o_read", 7))
                for half in range(2):
                    eng.wait_ge(scalar_done, done.count)
                    if m == 7:
                        eng.wait_ge(vector_done, step("res2", 6, 7))
                    else:
                        eng.wait_ge(vector_done, step("x_d", 5 + 1))
                    act(tiles(sq2, 512)[:, 4 * half:4 * half + 4], res[:, 4 * half:4 * half + 4, :], ACT.Square, "sq2", m, half).then_inc(scalar_done, 1)
                eng.wait_ge(vector_done, step("ms2e", m))
                rsqrt(rs2[:, 0:512], "rs2", m)
                eng.wait_ge(vector_done, step("xn2", m))
                eng.wait_ge(vector_done, step("aux", m))
                x = tiles(aux[:, m % 2, 0:32], 2)
                md = tiles(mod[:, m % 2, :], 2)
                for t in range(KT):
                    act(xm[:, t, CS], xm[:, t, CS], ACT.Identity, *(("xm_a", m) if t == 7 else ()),
                        scale=x[:, t, 1:2], bias=md[:, t, 1:2]).then_inc(scalar_done, 1)

            def mla():
                m = 6
                rms(m)
                for n in range(14):
                    eng.wait_ge(tensor_done, step("in2", m, n))
                    if n < 5:
                        act(cq[:, n], bank(n % 6), ACT.Copy, "in2_read", m, n).then_inc(scalar_done, 1)
                    elif n > 5:
                        act(gate2[:, n - 6], bank(n % 6), ACT.Silu, "in2_read", m, n).then_inc(scalar_done, 1)
                eng.wait_ge(scalar_done, done.count)
                act(W(0, 2560), W(16384, 2560), ACT.Square, "cqsq", m).then_inc(scalar_done, 1)
                eng.wait_ge(vector_done, step("cqe", m))
                rsqrt(rs2, "cqr", m)
                eng.wait_ge(tensor_done, step("cqsum", m))
                eng.wait_ge(vector_done, step("kr"))
                for t in range(8):
                    eng.wait_ge(tensor_done, step("kn", t))
                    act(k_h[0:64, 2 * t], bank(2 + t % 4)[0:64], ACT.Copy, "kn_read", t, 0).then_inc(scalar_done, 1)
                act(k_h[64:96, :, :], over(rope_t[0][64:96, :], 16), ACT.Copy, "k_rope").then_inc(scalar_done, 1)
                for n in range(0, 8, 2):
                    eng.wait_ge(tensor_done, step("v2", n))
                    act(v_h[:, n // 2, 0:512], bank(2 + n % 4), ACT.Copy, "v2_read", n).then_inc(scalar_done, 1)
                for h in range(MLA_H):
                    eng.wait_ge(vector_done, step("nmx", h))
                    if h > 1:
                        eng.wait_ge(tensor_done, step("pt", h - 2))
                    p = p_h[h % 2]
                    eng.wait_ge(scalar_done, done.count)
                    for t in range(2):
                        act(p[:, 256 * t:256 * t + 256], bank(2, 256 * t, 256 * t + 256), ACT.Exp, scale=MLA_SCALE,
                            bias=nmx[:, 4 * (h % 2) + t:4 * (h % 2) + t + 1], accum_out=rsm[:, 4 * (h % 2) + t:4 * (h % 2) + t + 1]).then_inc(scalar_done, 1)
                    for t in range(2):
                        act(p[:, 512 + 512 * t:1024 + 512 * t], bank(3 + t), ACT.Exp, *(("exp2", h) if t else ()), scale=MLA_SCALE,
                            bias=nmx[:, 4 * (h % 2) + 2 + t:4 * (h % 2) + 3 + t], accum_out=rsm[:, 4 * (h % 2) + 2 + t:4 * (h % 2) + 3 + t]).then_inc(scalar_done, 1)
                    if h:
                        pt_copy(h - 1)
                pt_copy(MLA_H - 1)

            def pt_copy(h):
                eng.wait_ge(tensor_done, step("pt", h))
                if h > 1:
                    eng.wait_ge(tensor_done, step("o2", h - 2))
                act(pt_h[h % 2][:, 0:1024], banks(5, 1024), ACT.Copy, "pt_a", h).then_inc(scalar_done, 1)

            def gla():
                m = 7
                rms(m)
                eng.wait_ge(tensor_done, step("y2", 6, 7))
                for n in range(1, 17):
                    eng.wait_ge(tensor_done, step("in2", m, n))
                    if n < 5:
                        act(a_k[0][:, n - 1], bank(n % 6, 0, 256), ACT.Copy).then_inc(scalar_done, 1)
                        act(a_k[1][:, n - 1], bank(n % 6, 256, 512), ACT.Copy, "in2_read", m, n).then_inc(scalar_done, 1)
                    elif n < 9:
                        act(a_q[:, n - 5], bank(n % 6, 0, 256), ACT.Copy, "in2_read", m, n, scale=GLA_SCALE).then_inc(scalar_done, 1)
                    else:
                        act(a_gate[:, n - 9], bank(n % 6, 0, 256), ACT.Silu, "in2_read", m, n).then_inc(scalar_done, 1)
                for d in range(2):
                    eng.wait_ge(vector_done, step("gab", d))
                    eng.wait_ge(scalar_done, done.count)
                    act(a_ab, a_ab, ACT.Exp, scale=-1.0).then_inc(scalar_done, 1)
                    eng.wait_ge(scalar_done, done.count)
                    act(a_ab, a_ab, ACT.Ln, "gln", d, bias=1.0).then_inc(scalar_done, 1)
                for d in range(2):
                    eng.wait_ge(vector_done, step("cum", d))
                    eng.wait_ge(vector_done, step("cum", 1))
                    e = 255 if d == 0 else 0
                    for h in range(4):
                        act(tiles(a_kd[d], 256)[:, h], a_b[d][0][:, h], ACT.Exp, *(("ekc", d) if h == 3 else ()),
                            scale=-1.0, bias=a_b[d][0][:, h, e:e + 1]).then_inc(scalar_done, 1)
                    act(a_qd[d], a_b[d][1], ACT.Exp, "eqd", d).then_inc(scalar_done, 1)
                for d in range(2):
                    eng.wait_ge(tensor_done, step("akdt", d))
                    act(a_kdt[d], banks(4 * d, 1024), ACT.Copy, "akdts", d).then_inc(scalar_done, 1)
                for d in range(2):
                    eng.wait_ge(tensor_done, step("ast", d))
                    act(a_st[:, 4 * d:4 * d + 4, :], tiles(banks(2 + 4 * d, 1024), 256), ACT.Copy, "ast_read", d).then_inc(scalar_done, 1)
                n = 0
                for li in range(8):
                    for d in range(2):
                        eng.wait_ge(vector_done, step("dif", n))
                        act(a_e[n % 2], a_e[n % 2], ACT.Exp, "ez", n).then_inc(scalar_done, 1)
                        n += 1
                eng.wait_ge(tensor_done, step("ao"))
                eng.wait_ge(scalar_done, done.count)
                act(a_sq, banks(4, 2048), ACT.Square, "aosq").then_inc(scalar_done, 1)
                eng.wait_ge(vector_done, step("aoe"))
                rsqrt(a_rs, "aor")
                eng.wait_ge(vector_done, step("fres"))
                eng.wait_ge(scalar_done, done.count)
                act(ff_sq, tiles(ff_res, 256), ACT.Square, "fsq").then_inc(scalar_done, 1)
                eng.wait_ge(vector_done, step("fe"))
                rsqrt(ff_rstd, "frs")

            eng.wait_ge(params_in, 48)
            eng.wait_ge(scalar_done, done.count)
            act(sc[:, 0:8], col("c", 0, 8), ACT.Silu).then_inc(scalar_done, 1)
            eng.wait_ge(scalar_done, done.count)
            act(sc[:, 8:24], col("c2", 0, 16), ACT.Silu, "sc").then_inc(scalar_done, 1)
            eng.wait_ge(tokens_in, 32)
            for l in range(DEPTH):
                ffn(l, 0)
                mixer(l)
                ffn(l, 1)
            mla()
            gla()

        @block.vector
        def _(eng):
            done = Steps(vector_done, found)
            v = nc.vector

            def do(ins, *key):
                done.named(*key)
                return ins

            def tt(o, a, b, op, *key):
                return do(v.tensor_tensor(o, a, b, op), *key)

            def ts(o, a, s1, op0, s2=None, op1=None, *key):
                return do(v.tensor_scalar(o, a, s1, None, op0) if op1 is None else v.tensor_scalar(o, a, s1, s2, op0, op1), *key)

            def stt(o, a, s, b, op0, op1, *key):
                return do(v.scalar_tensor_tensor(out=o, in0=a, scalar=s, in1=b, op0=op0, op1=op1), *key)

            def copy(o, a, *key):
                return do(v.tensor_copy(o, a), *key)

            MUL, ADD, SUB = ALU.mult, ALU.add, ALU.subtract

            def mod_part(m, ch):
                n = found["chunk_no", "ada", m, ch][1]
                w = tiles(ring[:, n % RING, :], 256)
                acc = mod_acc(m, ch)
                if m == 0 and ch == 0:
                    eng.wait_ge(scalar_done, step("sc"))
                if ch >= 2:
                    eng.wait_ge(tensor_done, step("modcol", m, ch - 2))
                elif m == 7 or m == 0:
                    pass
                else:
                    eng.wait_ge(vector_done, done.count)
                    if m % 3 == 2:
                        eng.wait_ge(tensor_done, step("modps", m - 1))
                eng.wait_ge(landed[n % RING], 16 * (n // RING + 1))
                vecs = 1 if m < 6 else 2
                for k in range(KT):
                    for i in range(vecs):
                        c = sc[:, k:k + 1] if m < 6 else sc[:, 8 + 2 * k + i:9 + 2 * k + i]
                        a = acc[:, 2 * i + k % 2, :]
                        if k < 2:
                            ts(a, w[:, k, :], c, MUL).then_inc(vector_done, 1)
                        else:
                            eng.wait_ge(vector_done, done.count + 1 - 2 * vecs)
                            stt(a, w[:, k, :], c, a, MUL, ADD, *(("chunk", n) if k == KT - 1 and i == vecs - 1 else ())).then_inc(vector_done, 1)
                found["modacc", m, ch] = found["chunk", n]

            def modulation(m):
                eng.wait_ge(tensor_done, step("modps", m))
                if m >= 2:
                    eng.wait_ge(scalar_done, step("xm_a", m - 2))
                o = mod[:, m % 2, :]
                x = aux[:, m % 2, :]
                if m < 6:
                    eng.wait_ge(vector_done, done.count)
                    tt(o[:, 0:24], bank(7, 0, 24), col("ada_b", 24 * m, 24), ADD, "mod", m).then_inc(vector_done, 1)
                    eng.wait_ge(vector_done, done.count)
                    ts(x[:, 0:8], o[:, 8:16], 1.0, ADD).then_inc(vector_done, 1)
                    if m % 3 == 1:
                        eng.wait_ge(vector_done, done.count)
                        ts(x[:, 8:16], o[:, 16:24], 1.0, ADD, None, None, "aux", m).then_inc(vector_done, 1)
                    else:
                        eng.wait_ge(vector_done, done.count)
                        ts(x[:, 8:16], o[:, 16:24], 1.0, ADD, 0.5, MUL, "aux", m).then_inc(vector_done, 1)
                else:
                    eng.wait_ge(vector_done, done.count)
                    tt(tiles(o, 2), tiles(bank(7, 0, 48), 2), each(col("ada_b2", 24 * (m - 6), 24), 2), ADD, "mod", m).then_inc(vector_done, 1)
                    eng.wait_ge(vector_done, done.count)
                    ts(x[:, 0:16], o[:, 16:32], 1.0, ADD).then_inc(vector_done, 1)
                    eng.wait_ge(vector_done, done.count)
                    tt(tiles(x[:, 0:16], 2), tiles(x[:, 0:16], 2), each(col("norm_g", 8 * (m - 6), 8), 2), MUL, "aux", m).then_inc(vector_done, 1)

            def affine(o, i, scale, bias, kts, *key):
                eng.wait_ge(vector_done, done.count)
                for t in kts:
                    ts(o[:, t], i[:, t], scale[:, t:t + 1], MUL, bias[:, t:t + 1], ADD, *(key if t == kts[-1] else ())).then_inc(vector_done, 1)

            def modulate(m):
                x = aux[:, m % 2, :]
                if m > 0:
                    eng.wait_ge(tensor_done, step("acc", m - 1))
                if m == 0:
                    eng.wait_ge(vector_done, done.count)
                    do(v.tensor_copy(small[:, 60:61], ident[:, 0:1]), "x_d", 0).then_inc(vector_done, 1)
                affine(xm[:, :, XS], res[:, :, XS], x[:, 0:8], mod[:, m % 2, 0:8], range(4, 8), "xm_d", m)

            def norm(m):
                g = aux[:, m % 2, 8:16]
                eng.wait_ge(tensor_done, step("acc", m))
                eng.wait_ge(scalar_done, step("ax", m))
                eng.wait_ge(vector_done, done.count)
                for t in range(KT):
                    stt(tiles(ff_res, 256)[:, t], bank(t // 2, 256 * (t % 2), 256 * (t % 2) + 256), g[:, t:t + 1],
                        tiles(ff_ax, 256)[:, t], MUL, ADD, "res", m, t).then_inc(vector_done, 1)
                eng.wait_ge(tensor_done, step("mu", m))
                eng.wait_ge(vector_done, done.count)
                stt(tiles(ff_cen, 256), over(bank(4, 0, 256), KT), -1.0 / D, tiles(ff_res, 256), MUL, ADD, "cen", m).then_inc(vector_done, 1)
                eng.wait_ge(tensor_done, step("var", m))
                eng.wait_ge(vector_done, done.count)
                ts(ff_rstd, bank(5, 0, 256), 1.0 / D, MUL, LN_EPS, ADD, "ve", m).then_inc(vector_done, 1)
                if m % 3 != 1:
                    modulation(m + 1)
                eng.wait_ge(scalar_done, step("rstd", m))
                eng.wait_ge(vector_done, done.count)
                tt(tiles(ff_cen, 256), tiles(ff_cen, 256), over(ff_rstd, KT), MUL, "xn", m).then_inc(vector_done, 1)
                affine(res[:, :, XS], tiles(ff_cen, 256), col("ln_g", 8 * m, 8), col("ln_b", 8 * m, 8), range(4, 8), "x_d", m + 1)
                eng.wait_ge(scalar_done, step("x_a", m))

            def ffn(l, f):
                m = 3 * l + 2 * f
                modulate(m)
                for j in range(FT):
                    eng.wait_ge(tensor_done, step("ab", m, j))
                    eng.wait_ge(scalar_done, step("sil", m, j))
                    if j >= 4:
                        eng.wait_ge(tensor_done, step("down", m, j - 4))
                    tt(ff_h[j % 4], ff_sil[j % 2], bank(4 + j % 3, 256, 512), MUL, "h", m, j).then_inc(vector_done, 1)
                    if j % 2:
                        mod_part(m + 1, j // 2)
                mod_part(m + 1, 11)
                norm(m)

            def mixer(l):
                m = 3 * l + 1
                modulate(m)
                for i, ch in enumerate(WIN_ORDER):
                    b = i % 7
                    mine = [t for t in (2 * ch, 2 * ch + 1) if t < 9 or 16 <= t < 22 or t == 25] if ch < 13 else []
                    if mine:
                        eng.wait_ge(tensor_done, step("proj", m, i))
                    if ch in (12, 4):
                        eng.wait_ge(scalar_done, step("proj_read_a", m, i))
                    for t in mine:
                        src = bank(b, 256 * (t % 2), 256 * (t % 2) + 256)
                        key = ("proj_read", m, i) if t == mine[-1] else ()
                        if t == 25:
                            eng.wait_ge(vector_done, done.count)
                            ts(r_u, src, col("row_bias", l), ADD, col("row_sign"), MUL, *key).then_inc(vector_done, 1)
                            eng.wait_ge(vector_done, done.count)
                            stt(r_ab, r_u, -1.0, r_u, MUL, ALU.max, "rab", m).then_inc(vector_done, 1)
                            continue
                        y = qkv[:, t if t < 9 else t - 7]

                        def cw(tap):
                            return col("gconv", 36 * l + 9 * tap + t) if t < 9 else col("mconv", 24 * l + 6 * tap + t - 16)
                        eng.wait_ge(vector_done, done.count)
                        ts(y, src, cw(3), MUL).then_inc(vector_done, 1)
                        for back in (1, 2, 3):
                            if back == 3:
                                eng.wait_ge(vector_done, done.count)
                                v.scalar_tensor_tensor(out=y[:, back:], in0=src[:, :T - back], scalar=cw(3 - back),
                                                                in1=y[:, back:], op0=MUL, op1=ADD).then_inc(vector_done, 1)
                                done.named("conv", m, t)
                            else:
                                eng.wait_ge(vector_done, done.count)
                                stt(y[:, back:], src[:, :T - back], cw(3 - back), y[:, back:], MUL, ADD).then_inc(vector_done, 1)
                    if mine and 25 not in mine:
                        found["proj_read", m, i] = found["conv", m, mine[-1]]
                    if i < 12:
                        mod_part(m + 1, i)
                modulation(m + 1)
                eng.wait_ge(scalar_done, step("rln", m))
                eng.wait_ge(scalar_done, step("rco", m))
                eng.wait_ge(scalar_done, step("rbe", m))
                eng.wait_ge(vector_done, done.count)
                stt(r_ln, r_u, 0.0, r_ln, ALU.max, ADD).then_inc(vector_done, 1)
                eng.wait_ge(vector_done, done.count)
                ts(rcoef[:, 1:2], rcoef[:, 0:1], -1.0, MUL).then_inc(vector_done, 1)
                eng.wait_ge(vector_done, done.count)
                ts(r_ln, r_ln, rcoef[:, 1:2], MUL).then_inc(vector_done, 1)
                onesrow = table("ones")
                eng.wait_ge(vector_done, done.count)
                do(v.tensor_tensor_scan(r_cs[:, 0:P], onesrow[:, 0:P], r_ln[:, 0:P], 0.0, MUL, ADD)).then_inc(vector_done, 1)
                eng.wait_ge(vector_done, done.count)
                ts(rkeep, r_cs[:, P - 1:P], col("row_keep"), MUL).then_inc(vector_done, 1)
                eng.wait_ge(vector_done, done.count)
                do(v.tensor_tensor_scan(r_cs[:, P:T], onesrow[:, 0:P], r_ln[:, P:T], rkeep, MUL, ADD)).then_inc(vector_done, 1)
                eng.wait_ge(vector_done, done.count)
                ts(r_rw, r_cs, -1.0, MUL).then_inc(vector_done, 1)
                I = slice(ROW_I, ROW_I + 32)
                eng.wait_ge(vector_done, done.count)
                copy(r_nm[I, :], r_cs[ROW_F:ROW_F + 32, :]).then_inc(vector_done, 1)
                eng.wait_ge(vector_done, done.count)
                tt(r_rw[I, :], r_u[I, :], r_nm[I, :], SUB).then_inc(vector_done, 1)
                eng.wait_ge(vector_done, done.count)
                do(v.tensor_tensor_scan(r_max[I, :], r_rw[I, :], r_rw[I, :], 0.0, ALU.max, ALU.max)).then_inc(vector_done, 1)
                eng.wait_ge(vector_done, done.count)
                stt(r_nm[I, :], r_max[I, :], -1.0, r_nm[I, :], MUL, SUB).then_inc(vector_done, 1)
                B = slice(ROW_B, ROW_B + 32)
                eng.wait_ge(vector_done, done.count)
                ts(r_beta[B, :], r_beta[B, :], 1.0, ADD).then_inc(vector_done, 1)
                eng.wait_ge(vector_done, done.count)
                do(v.reciprocal(r_beta[B, :], r_beta[B, :]), "rows", m).then_inc(vector_done, 1)
                eng.wait_ge(tensor_done, step("l2", m))
                eng.wait_ge(vector_done, done.count)
                ts(g_tt, banks(1, 1536), EPS, ADD, None, None, "l2e", m).then_inc(vector_done, 1)
                found["l2_read", m] = found["l2e", m]
                eng.wait_ge(scalar_done, step("ri", m))
                eng.wait_ge(vector_done, done.count)
                tt(W(QKV, 1536), W(QKV, 1536), g_tt, MUL).then_inc(vector_done, 1)
                eng.wait_ge(tensor_done, step("pairs", m))
                eng.wait_ge(vector_done, done.count)
                copy(glast, tiles(banks(6, 768), 256)[:, :, P - 1], "glast", m).then_inc(vector_done, 1)
                eng.wait_ge(vector_done, done.count)
                copy(W(COLT, 256), bank(0, 0, 256), "colt", m).then_inc(vector_done, 1)
                eng.wait_ge(vector_done, done.count)
                tt(g_kb, qkv[:, 3:6], tiles(banks(4, 768), 256), MUL, "kb0", m).then_inc(vector_done, 1)
                eng.wait_ge(scalar_done, step("silu", m, 8))
                eng.wait_ge(vector_done, done.count)
                tt(g_vb, qkv[:, 6:9], tiles(banks(4, 768), 256), MUL, "kb", m).then_inc(vector_done, 1)
                eng.wait_ge(tensor_done, step("gb", m))
                eng.wait_ge(vector_done, done.count)
                tt(tiles(g_dt, 128), tiles(banks(1, 1536), 128), over(table("neg_t", 0, 128), 12), ADD, "gb_read", m).then_inc(vector_done, 1)
                eng.wait_ge(scalar_done, step("eg", m))
                eng.wait_ge(scalar_done, step("ekd", m))
                eng.wait_ge(vector_done, done.count)
                tt(g_kg, g_kb, g_eg, MUL).then_inc(vector_done, 1)
                eng.wait_ge(vector_done, done.count)
                stt(W(g0 + 3072, 768), W(QKV, 768), QS, W(g0, 768), MUL, MUL, "pairs_read", m).then_inc(vector_done, 1)
                eng.wait_ge(vector_done, done.count)
                tt(g_kd, qkv[:, 3:6, 0:P], g_ekd, MUL, "gdn_in", m).then_inc(vector_done, 1)
                eng.wait_ge(tensor_done, step("kk", m))
                eng.wait_ge(scalar_done, step("dt", m))
                eng.wait_ge(vector_done, done.count)
                tt(g_at, banks(1, 1536), g_dt, MUL).then_inc(vector_done, 1)
                eng.wait_ge(vector_done, done.count)
                tt(tiles(g_at, 128), tiles(g_at, 128), over(table("strict"), 12), MUL).then_inc(vector_done, 1)
                eng.wait_ge(vector_done, done.count)
                copy(tiles(g_t, 128), over(ident, 12)).then_inc(vector_done, 1)
                eng.wait_ge(vector_done, done.count)
                copy(tiles(g_tt, 128), over(ident, 12)).then_inc(vector_done, 1)
                eng.wait_ge(tensor_done, step("qk", m))
                eng.wait_ge(vector_done, done.count)
                stt(g_att, banks(4, 1536), QS, g_dt, MUL, MUL, "t", m, 0, 0).then_inc(vector_done, 1)
                found["t", m, 0, 1] = found["t", m, 0, 2] = found["t", m, 0, 0]
                for li in range(7):
                    mask = table("second", P * li, P)
                    for g in range(3):
                        sl = slice(512 * g, 512 * g + 512)
                        eng.wait_ge(tensor_done, step("x", m, li, g))
                        eng.wait_ge(vector_done, done.count)
                        tt(tiles(g_x[:, sl], 128), tiles(bank(1 + g), 128), over(mask, 4), MUL, "xs", m, li, g).then_inc(vector_done, 1)
                    for g in range(3):
                        sl = slice(512 * g, 512 * g + 512)
                        eng.wait_ge(tensor_done, step("y", m, li, g))
                        if li < 6:
                            tt(g_t[:, sl], g_t[:, sl], bank(1 + g), SUB).then_inc(vector_done, 1)
                        tt(g_tt[:, sl], g_tt[:, sl], bank(4 + g), SUB, "t", m, li + 1, g).then_inc(vector_done, 1)
                eng.wait_ge(tensor_done, step("vn0", m))
                eng.wait_ge(vector_done, done.count)
                copy(g_vn[:, 0, :], bank(0, 0, 384), "vn0s", m).then_inc(vector_done, 1)
                eng.wait_ge(tensor_done, step("s", m))
                eng.wait_ge(vector_done, done.count)
                copy(g_s, bank(7, 0, 192), "ss", m).then_inc(vector_done, 1)
                eng.wait_ge(tensor_done, step("ks", m))
                eng.wait_ge(scalar_done, step("vbt_read", m))
                eng.wait_ge(vector_done, done.count)
                tt(g_r1, g_vbt[:, 1, :], bank(0, 0, 384), SUB, "r1", m).then_inc(vector_done, 1)
                eng.wait_ge(tensor_done, step("vn1", m))
                eng.wait_ge(vector_done, done.count)
                copy(g_vn[:, 1, :], bank(7, 0, 384), "vn1s", m).then_inc(vector_done, 1)
                eng.wait_ge(tensor_done, step("oa_sum", m))
                eng.wait_ge(vector_done, done.count)
                ts(o_rstd, banks(2, 768), 1.0 / HD, MUL, EPS, ADD, "oa_e", m).then_inc(vector_done, 1)
                eng.wait_ge(scalar_done, step("oa_r", m))
                eng.wait_ge(vector_done, done.count)
                tt(o_tmp, banks(0, 768), o_rstd, MUL).then_inc(vector_done, 1)
                eng.wait_ge(vector_done, done.count)
                stt(W(MIX, 768), o_tmp, col("gdn_norm", l), W(ZG, 768), MUL, MUL, "oa_done", m).then_inc(vector_done, 1)
                eng.wait_ge(tensor_done, step("ms", m))
                eng.wait_ge(vector_done, done.count)
                stt(tiles(m_s, 512), tiles(banks(4, 2048), 512), QS, over(table("neg_q"), 4), MUL, ADD).then_inc(vector_done, 1)
                s3 = tiles(m_s, 256)
                eng.wait_ge(vector_done, done.count)
                do(v.tensor_reduce(nm8, s3, AX.X, ALU.max, negate=True)).then_inc(vector_done, 1)
                eng.wait_ge(vector_done, done.count)
                tt(s3, s3, each(nm8, 256), ADD, "msub", m).then_inc(vector_done, 1)
                eng.wait_ge(scalar_done, step("mexp", m))
                eng.wait_ge(vector_done, done.count)
                do(v.tensor_reduce(sm8, s3, AX.X, ADD)).then_inc(vector_done, 1)
                eng.wait_ge(vector_done, done.count)
                do(v.reciprocal(sm8, sm8)).then_inc(vector_done, 1)
                eng.wait_ge(vector_done, done.count)
                tt(s3, s3, each(sm8, 256), MUL, "mp", m).then_inc(vector_done, 1)
                eng.wait_ge(tensor_done, step("mb", m))
                eng.wait_ge(tensor_done, step("mo", m))
                for h in range(6):
                    tt(tiles(l_w[:, 512 * h:512 * h + 512], 256), tiles(table("neg_t"), 256),
                       over(banks(0, 1536)[:, 256 * h:256 * h + 256], 2), SUB, *(("mb_read", m) if h == 5 else ())).then_inc(vector_done, 1)
                eng.wait_ge(tensor_done, step("ls", m))
                eng.wait_ge(scalar_done, step("lw", m))
                eng.wait_ge(vector_done, done.count)
                stt(l_w, banks(0, 3072), QS, l_w, MUL, MUL, "lp", m).then_inc(vector_done, 1)
                eng.wait_ge(tensor_done, step("lo", m))
                eng.wait_ge(scalar_done, step("em", m))
                eng.wait_ge(vector_done, done.count)
                stt(l_em, banks(0, 768), -1.0, l_em, MUL, ALU.max).then_inc(vector_done, 1)
                eng.wait_ge(vector_done, done.count)
                tt(l_em, banks(0, 768), l_em, ALU.max).then_inc(vector_done, 1)
                eng.wait_ge(vector_done, done.count)
                do(v.reciprocal(l_em, l_em)).then_inc(vector_done, 1)
                eng.wait_ge(vector_done, done.count)
                tt(l_h, banks(6, 768), l_em, MUL).then_inc(vector_done, 1)
                eng.wait_ge(vector_done, done.count)
                tt(l_h, l_h, W(OG, 768), MUL, "lh", m).then_inc(vector_done, 1)
                eng.wait_ge(tensor_done, step("lmu", m))
                eng.wait_ge(vector_done, done.count)
                stt(l_h, banks(2, 768), -1.0 / HD, l_h, MUL, ADD, "lcen", m).then_inc(vector_done, 1)
                eng.wait_ge(tensor_done, step("lvar", m))
                eng.wait_ge(vector_done, done.count)
                ts(l_rstd, banks(4, 768), 1.0 / HD, MUL, EPS, ADD, "lve", m).then_inc(vector_done, 1)
                eng.wait_ge(scalar_done, step("mixed_a", m))
                eng.wait_ge(vector_done, done.count)
                for t in range(3):
                    stt(mix[:, 5 + t], tiles(l_h, 256)[:, t], col("ml_norm", 3 * l + t), tiles(l_rstd, 256)[:, t], MUL, MUL,
                        *(("mixed", m) if t == 2 else ())).then_inc(vector_done, 1)
                norm(m)

            def rms(m):
                eng.wait_ge(tensor_done, step("ms2", m))
                eng.wait_ge(vector_done, done.count)
                ts(rs2[:, 0:512], bank(6), 1.0 / D, MUL, EPS, ADD, "ms2e", m).then_inc(vector_done, 1)
                eng.wait_ge(scalar_done, step("rs2", m))
                if m == 6:
                    eng.wait_ge(scalar_done, step("x_a", 5))
                else:
                    eng.wait_ge(tensor_done, step("y2", 6, 7))
                eng.wait_ge(vector_done, done.count)
                tt(xm[:, :, :], res[:, :, :], over(rs2[:, 0:512], KT), MUL, "xn2", m).then_inc(vector_done, 1)
                x = tiles(aux[:, m % 2, 0:32], 2)
                md = tiles(mod[:, m % 2, :], 2)
                eng.wait_ge(vector_done, done.count)
                for t in range(KT):
                    ts(xm[:, t, XS], xm[:, t, XS], x[:, t, 0:1], MUL, md[:, t, 0:1], ADD, *(("xm_d", m) if t == 7 else ())).then_inc(vector_done, 1)

            def mla():
                m = 6
                rms(m)
                rope = table("rope")
                for ch in range(6):
                    mod_part(7, ch)
                eng.wait_ge(tensor_done, step("in2", m, 5))
                eng.wait_ge(vector_done, done.count)
                tt(rope_t[0][64:96, :], PS[64:96, 5, :], rope[64:96, :], MUL).then_inc(vector_done, 1)
                eng.wait_ge(vector_done, done.count)
                tt(rope_t[1][64:96, :], PS[96:128, 5, :], rope[96:128, :], MUL, "in2_read", m, 5).then_inc(vector_done, 1)
                eng.wait_ge(vector_done, done.count)
                tt(rope_t[0][64:96, :], rope_t[0][64:96, :], rope_t[1][64:96, :], ADD, "kr").then_inc(vector_done, 1)
                for ch in range(6, 12):
                    mod_part(7, ch)
                modulation(7)
                eng.wait_ge(tensor_done, step("cqsum", m))
                eng.wait_ge(vector_done, done.count)
                ts(rs2[:, 0:512], bank(0), 1.0 / 384, MUL, EPS, ADD).then_inc(vector_done, 1)
                eng.wait_ge(vector_done, done.count)
                ts(rs2[:, 512:1024], bank(1), 1.0 / 256, MUL, EPS, ADD, "cqe", m).then_inc(vector_done, 1)
                eng.wait_ge(scalar_done, step("cqr", m))
                for t in range(5):
                    g = col("q_norm", t) if t < 3 else col("kv_norm", t - 3)
                    eng.wait_ge(vector_done, done.count)
                    stt(cq[:, t], cq[:, t], g, rs2[:, 0:512] if t < 3 else rs2[:, 512:1024], MUL, MUL, *(("cqn", m) if t == 4 else ())).then_inc(vector_done, 1)
                for t in range(8):
                    eng.wait_ge(tensor_done, step("kn", t))
                    copy(k_h[0:64, 2 * t + 1], PS[64:128, 2 + t % 4, :], "kn_read", t, 1).then_inc(vector_done, 1)
                for n in range(1, 8, 2):
                    eng.wait_ge(tensor_done, step("v2", n))
                    copy(v_h[:, n // 2, 512:1024], bank(2 + n % 4), "v2_read", n).then_inc(vector_done, 1)

                def q_part(h):
                    eng.wait_ge(tensor_done, step("q2", h))
                    eng.wait_ge(scalar_done, step("k_rope"))
                    if h > 1:
                        eng.wait_ge(tensor_done, step("s2", h - 2))
                    q = q_h[h % 2]
                    eng.wait_ge(vector_done, done.count)
                    tt(q[0:96, :], PS[0:96, 0, :], rope[0:96, :], MUL).then_inc(vector_done, 1)
                    eng.wait_ge(vector_done, done.count)
                    tt(mla_tmp[64:96, :], PS[96:128, 0, :], rope[96:128, :], MUL).then_inc(vector_done, 1)
                    eng.wait_ge(vector_done, done.count)
                    tt(q[64:96, :], q[64:96, :], mla_tmp[64:96, :], ADD, "q_read", h).then_inc(vector_done, 1)

                mla_tmp = W(16384 + 1536, 512)
                q_part(0)
                for h in range(MLA_H):
                    eng.wait_ge(tensor_done, step("s2", h))
                    if h > 1:
                        eng.wait_ge(scalar_done, step("exp2", h - 2))
                    nm = nmx[:, 4 * (h % 2):4 * (h % 2) + 4]
                    do(v.tensor_reduce(nm[:, 0:2], tiles(bank(2), 256), AX.X, ALU.max, negate=True)).then_inc(vector_done, 1)
                    do(v.tensor_reduce(nm[:, 2:4], tiles(banks(3, 1024), 512), AX.X, ALU.max, negate=True)).then_inc(vector_done, 1)
                    eng.wait_ge(vector_done, done.count)
                    ts(nm, nm, MLA_SCALE, MUL, None, None, "nmx", h).then_inc(vector_done, 1)
                    if h:
                        pt_copy(h - 1)
                    if h + 1 < MLA_H:
                        q_part(h + 1)
                    eng.wait_ge(scalar_done, step("exp2", h))
                    sm = rsm[:, 4 * (h % 2):4 * (h % 2) + 4]
                    eng.wait_ge(vector_done, done.count)
                    do(v.reciprocal(sm, sm), "rec", h).then_inc(vector_done, 1)
                pt_copy(MLA_H - 1)
                for ch in range(4):
                    for t in (2 * ch, 2 * ch + 1):
                        eng.wait_ge(tensor_done, step("y2", m, t))
                        for s, cs in ((1, CS), (0, XS)):
                            stt(res[:, t, cs], PS[:, 2 + t % 4, cs], mod[:, 0, 32 + 2 * t + s:33 + 2 * t + s], res[:, t, cs], MUL, ADD,
                                *(("res2", m, t) if s == 0 else ())).then_inc(vector_done, 1)

            def pt_copy(h):
                eng.wait_ge(tensor_done, step("pt", h))
                if h > 1:
                    eng.wait_ge(tensor_done, step("o2", h - 2))
                copy(pt_h[h % 2][:, 1024:1536], bank(7), "pt_d", h).then_inc(vector_done, 1)
                if h % 2:
                    eng.wait_ge(tensor_done, step("o2", h))
                    t = h // 2
                    tt(xm[:, t, :], bank(1), gate2[:, t, :], MUL, "o_read", t).then_inc(vector_done, 1)

            def gla():
                m = 7
                rms(m)
                eng.wait_ge(tensor_done, step("in2", m, 0))
                eng.wait_ge(vector_done, done.count)
                copy(a_r, bank(0), "in2_read", m, 0).then_inc(vector_done, 1)
                for ch in range(4):
                    for tp in range(2):
                        n = 17 + 2 * ch + tp
                        eng.wait_ge(tensor_done, step("in2", m, n))
                        copy(a_v[:, 2 * tp:2 * tp + 2, 256 * ch:256 * ch + 256], tiles(bank(n % 6), 256), "in2_read", m, n).then_inc(vector_done, 1)
                ones1 = table("ones")
                for d in range(2):
                    eng.wait_ge(tensor_done, step("ga", d))
                    eng.wait_ge(vector_done, done.count)
                    for t in range(4):
                        ts(a_u[:, 512 * t:512 * t + 512], bank(4 * d + t), col("b_g", 4 * d + t), ADD, None, None).then_inc(vector_done, 1)
                    eng.wait_ge(vector_done, done.count)
                    stt(a_ab, a_u, -1.0, a_u, MUL, ALU.max, "gab", d).then_inc(vector_done, 1)
                    found["ga_read", d] = found["gab", d]
                    eng.wait_ge(scalar_done, step("gln", d))
                    eng.wait_ge(vector_done, done.count)
                    stt(a_u, a_u, 0.0, a_ab, ALU.min, SUB).then_inc(vector_done, 1)
                    eng.wait_ge(vector_done, done.count)
                    ts(a_u, a_u, 1.0 / 16, MUL).then_inc(vector_done, 1)
                    eng.wait_ge(vector_done, done.count)
                    for h in range(4):
                        for s in range(2):
                            src = a_u[:, 512 * h + 256 * s:512 * h + 256 * s + 256]
                            do(v.tensor_tensor_scan(a_b[d][s][:, h], ones1, src, 0.0, MUL, ADD),
                               *(("cum", 0) if h == 3 and s == 1 and d == 0 else ())).then_inc(vector_done, 1)
                    if d == 1:
                        eng.wait_ge(vector_done, done.count)
                        for s in range(2):
                            b = a_b[1][s]
                            copy(small[:, 40 + 4 * s:44 + 4 * s], b[:, :, T - 1]).then_inc(vector_done, 1)
                        for s in range(2):
                            b = a_b[1][s]
                            eng.wait_ge(vector_done, done.count)
                            tt(b, each(small[:, 40 + 4 * s:44 + 4 * s], 256), b, SUB).then_inc(vector_done, 1)
                            eng.wait_ge(vector_done, done.count)
                            tt(b, b, tiles(a_u, 512)[:, :, 256 * s:256 * s + 256], ADD, *(("cum", 1) if s else ())).then_inc(vector_done, 1)
                for d in range(2):
                    eng.wait_ge(scalar_done, step("ekc", d))
                    eng.wait_ge(scalar_done, step("eqd", d))
                    tt(tiles(a_kd[d], 256), tiles(a_kd[d], 256), a_k[0], MUL, "kd", d).then_inc(vector_done, 1)
                    tt(a_qd[d], a_qd[d], a_q, MUL, "aqd", d).then_inc(vector_done, 1)
                eng.wait_ge(tensor_done, step("diag"))
                eng.wait_ge(vector_done, done.count)
                stt(tiles(a_atd, 128), tiles(banks(0, 1024), 128), 2.0, over(ident, 8), MUL, MUL, "at0").then_inc(vector_done, 1)
                found["lev_read", -1] = found["at0",]

                kx, qx = W(1024, 1024), W(2048, 1024)

                def tree(n):
                    li, d = n // 2, n % 2
                    s = 1 << li
                    eng.wait_ge(tensor_done, step("akdt", n % 2))
                    eng.wait_ge(scalar_done, step("akdts", n % 2))
                    if n >= 2:
                        eng.wait_ge(tensor_done, step("lev", n - 2))
                    b = a_b[d][1].rearrange("p h (n b) -> p (h n) b", b=2 * s)
                    e = a_e[n % 2].rearrange("p (n b) -> p n b", b=2 * s)
                    kk = (kx if d == 0 else qx).rearrange("p (n b) -> p n b", b=2 * s)
                    qq = (qx if d == 0 else kx).rearrange("p (n b) -> p n b", b=2 * s)
                    lo, hi = slice(0, s), slice(s, 2 * s)
                    r = s - 1 if d == 0 else s
                    ref = b[:, :, r:r + 1].to_broadcast([P, T * 4 // (2 * s), s])
                    if d == 0:
                        tt(e[:, :, lo], ref, b[:, :, lo], SUB).then_inc(vector_done, 1)
                        tt(e[:, :, hi], b[:, :, hi], ref, SUB, "dif", n).then_inc(vector_done, 1)
                    else:
                        tt(e[:, :, lo], b[:, :, lo], ref, SUB).then_inc(vector_done, 1)
                        tt(e[:, :, hi], ref, b[:, :, hi], SUB, "dif", n).then_inc(vector_done, 1)
                    return e, kk, qq, lo, hi

                def weigh(n, t):
                    e, kk, qq, lo, hi = t
                    eng.wait_ge(scalar_done, step("ez", n))
                    tt(e[:, :, lo], e[:, :, lo], kk[:, :, lo], MUL).then_inc(vector_done, 1)
                    tt(e[:, :, hi], e[:, :, hi], qq[:, :, hi], MUL, "z", n).then_inc(vector_done, 1)

                def gather(n):
                    li, d = n // 2, n % 2
                    eng.wait_ge(tensor_done, step("lev", n))
                    b = 0 if n % 2 else 2
                    if li < 7:
                        if n >= 2:
                            eng.wait_ge(gpsimd_done, step("at", n - 2))
                        eng.wait_ge(tensor_done, step("ast", 0))
                        eng.wait_ge(tensor_done, step("ast", 1))
                        tt(tiles(a_m[n % 2], 128), tiles(banks(b, 1024), 128), over(table("first" if d == 0 else "second", P * li, P), 8), MUL,
                           "lev_read", n).then_inc(vector_done, 1)
                    else:
                        copy(a_ato[d], bank(b), "lev_read", n).then_inc(vector_done, 1)

                t0 = tree(0)
                for n in range(16):
                    weigh(n, t0)
                    if n < 15:
                        t0 = tree(n + 1)
                    gather(n)
                eng.wait_ge(tensor_done, step("aosum"))
                eng.wait_ge(vector_done, done.count)
                ts(a_rs, banks(0, 1024), 1.0 / 256, MUL, EPS, ADD, "aoe").then_inc(vector_done, 1)
                eng.wait_ge(scalar_done, step("aor"))
                ov = banks(4, 2048).rearrange("p (h v t) -> p h v t", h=4, v=2)
                eng.wait_ge(vector_done, done.count)
                tt(a_o.rearrange("p (h v t) -> p h v t", h=4, v=2), ov,
                   tiles(a_rs, 256).unsqueeze(2).to_broadcast([P, 4, 2, 256]), MUL).then_inc(vector_done, 1)
                eng.wait_ge(vector_done, done.count)
                o4 = a_o.rearrange("p (h v t) -> p h v t", h=4, v=2)
                g4 = a_gate.rearrange("p (h v) t -> p h v t", v=2)
                for h in range(4):
                    for dvh in range(2):
                        stt(xm[:, 2 * h + dvh, XS], o4[:, h, dvh], col("o_norm", dvh), g4[:, h, dvh], MUL, MUL,
                            *(("aod",) if h + dvh == 4 else ())).then_inc(vector_done, 1)
                for ch in range(4):
                    eng.wait_ge(tensor_done, step("y2", m, ch))
                    for t in (2 * ch, 2 * ch + 1):
                        eng.wait_ge(vector_done, done.count)
                        stt(tiles(ff_res, 256)[:, t], bank(4 + ch, 256 * (t % 2), 256 * (t % 2) + 256), mod[:, 1, 32 + 2 * t:33 + 2 * t],
                            res[:, t, XS], MUL, ADD, *(("fres",) if t == 7 else ())).then_inc(vector_done, 1)
                eng.wait_ge(tensor_done, step("fsum"))
                eng.wait_ge(vector_done, done.count)
                ts(ff_rstd, bank(0, 0, 256), 1.0 / D, MUL, EPS, ADD, "fe").then_inc(vector_done, 1)
                eng.wait_ge(scalar_done, step("frs"))
                eng.wait_ge(vector_done, done.count)
                for t in range(KT):
                    stt(tiles(ff_cen, 256)[:, t], tiles(ff_res, 256)[:, t], col("final_g", t), ff_rstd, MUL, MUL,
                        *(("final",) if t == 7 else ())).then_inc(vector_done, 1)

            eng.wait_ge(params_in, 48)
            for ch in range(12):
                mod_part(0, ch)
            modulation(0)
            eng.wait_ge(tokens_in, 32)
            for l in range(DEPTH):
                ffn(l, 0)
                mixer(l)
                ffn(l, 1)
            mla()
            gla()

        @block.gpsimd
        def _(eng):
            done = Steps(gpsimd_done, found)

            for m in range(8):
                for ch in range(12):
                    eng.wait_ge(vector_done, step("modacc", m, ch))
                    acc = mod_acc(m, ch).rearrange("p (v e) n -> p v e n", e=2)
                    n = 1 if m < 6 else 2
                    nc.gpsimd.tensor_tensor(acc[:, 0:n, 0, :], acc[:, 0:n, 0, :], acc[:, 0:n, 1, :], ALU.add).then_inc(gpsimd_done, 1)
                    done.named("modsum", m, ch)
            for h in range(MLA_H):
                eng.wait_ge(vector_done, step("rec", h))
                p = p_h[h % 2]
                r = rsm[:, 4 * (h % 2):4 * (h % 2) + 4]
                nc.gpsimd.tensor_tensor(tiles(p[:, 0:512], 256), tiles(p[:, 0:512], 256), each(r[:, 0:2], 256), ALU.mult).then_inc(gpsimd_done, 1)
                done.named()
                nc.gpsimd.tensor_tensor(tiles(p[:, 512:1536], 512), tiles(p[:, 512:1536], 512), each(r[:, 2:4], 512), ALU.mult).then_inc(gpsimd_done, 1)
                done.named("pn", h)
            for n in range(14):
                eng.wait_ge(vector_done, step("lev_read", n))
                eng.wait_ge(vector_done, step("at0"))
                eng.wait_ge(gpsimd_done, done.count)
                nc.gpsimd.tensor_tensor(a_atd, a_atd, a_m[n % 2], ALU.add).then_inc(gpsimd_done, 1)
                done.named("at", n)
            found["at_done",] = found["at", 13]

    return found, order


def constant_tables():
    t = np.zeros((P, NTAB), np.float32)

    def put(name, a):
        at, n = TAB[name]
        t[:, at:at + n] = a.reshape(P, n)
    i = np.arange(P)
    put("ident", np.eye(P))
    put("ones", np.ones((P, 256)))
    put("blk", (i[:, None] // 64 == i[None, :] // 64))
    first = np.stack([(i[:, None] // (2 * s) == i[None, :] // (2 * s)) & (i[:, None] // s % 2 == 0) & (i[None, :] // s % 2 == 1)
                      for s in LEVELS], 1)
    put("first", first)
    put("second", np.transpose(first, (2, 1, 0)))
    put("strict", i[None, :] > i[:, None])
    q = np.arange(T)
    blocks = np.arange(2)[None, :, None] * P + i[:, None, None]
    put("neg_t", np.where(q[None, None, :] >= blocks, 0, NEG))
    put("neg_q", np.where(q[None, None, :] <= blocks, 0, NEG))
    rope = np.zeros((P, 2 * T))
    rope[0:96] = 1.0
    pos = np.stack([np.arange(T) // 64, np.arange(T) % 64]).astype(np.float32)
    inv = np.float32(10000.0) ** (-np.arange(8, dtype=np.float32) / 8)
    for r in range(32):
        ang = pos[r // 16] * inv[r % 8]
        rope[64 + r, T:] = np.cos(ang)
        rope[96 + r, T:] = np.sin(ang) * (-1 if r % 16 < 8 else 1)
    put("rope", rope)
    put("pair", i[:, None, None] % 32 == 2 * np.arange(3)[None, :, None] + i[None, None, :] // 64)
    return t


def parameter_columns(a):
    c = np.zeros((P, NCOLS), np.float32)

    def put(name, x, lo=0):
        at, _ = COLS[name]
        x = np.asarray(x)
        c[:x.shape[0], at + lo:at + lo + x.shape[1]] = x

    def by_tile(v):
        return np.asarray(v).reshape(-1, P).T
    put("c", by_tile(a["c"]))
    put("c2", np.stack([by_tile(a["c_2"]), by_tile(a["c_ctx_2"])], 2).reshape(P, 16))
    put("ada_b", by_tile(a["ada_b"]))
    put("ada_b2", by_tile(a["ada_b_2"]))
    put("ln_g", by_tile(a["ln_g"]))
    put("ln_b", by_tile(a["ln_b"]))
    put("gconv", by_tile(a["gdn_conv"]))
    put("mconv", by_tile(a["mlstm_conv"]))
    at = COLS["row_bias"][0]
    for l in range(DEPTH):
        c[ROW_A:ROW_A + 6, at + l] = a["gdn_dt_bias"][l]
        c[ROW_I:ROW_I + 6, at + l] = a["mlstm_i_bias"][l]
        c[ROW_F:ROW_F + 6, at + l] = a["mlstm_f_bias"][l]
        c[ROW_A:ROW_A + 6, COLS["row_log"][0] + l] = a["gdn_a_log"][l]
        c[:, COLS["gdn_norm"][0] + l] = np.tile(a["gdn_norm"][l], 2)
    c[:, COLS["row_sign"][0]] = np.repeat([1, -1, 1, -1], 32)
    c[:, COLS["row_keep"][0]] = np.repeat([0, 0, 0, 1], 32)
    put("ml_norm", by_tile(a["mlstm_norm"]))
    put("norm_g", by_tile(a["norm_g_2"]))
    put("final_g", by_tile(a["final_g_2"]))
    put("q_norm", by_tile(a["mla_q_norm_2"]))
    put("kv_norm", by_tile(a["mla_kv_norm_2"]))
    put("b_g", np.concatenate([by_tile(a["gla_b_gf_2"]), by_tile(a["gla_b_gb_2"])], 1))
    put("o_norm", by_tile(a["gla_o_norm_2"]))
    return c


def columns(w, starts, kt):
    w = w.reshape(kt, P, -1)
    parts = [np.transpose(w[:, :, s:s + n], (1, 0, 2)) if s >= 0 else np.zeros((P, kt, n), np.float32) for s, n in starts]
    return np.concatenate(parts, 2)


def chunk_of(tag, a):
    kind = tag[0]
    if kind == "ada":
        m, ch = tag[1:]
        w = a["ada_w"][m // 3] if m < 6 else a["ada_w_2"][m - 6]
        return columns(w, [(3072 * (m % 3 if m < 6 else 0) + 256 * ch, 256)], KT)
    if kind == "w13":
        l, f, j = tag[1:]
        return columns(a["ffn_w13"][l, f], [(P * j, P), (FF + P * j, P)], KT)
    if kind == "w2":
        l, f, p = tag[1:]
        return columns(a["ffn_w2"][l, f][256 * p:256 * p + 256], [(0, D)], 2)
    if kind == "win":
        l, ch = tag[1:]
        w = a["w_in"][l]
        if ch < 12:
            return columns(w, [(WIN_TILES[2 * ch], P), (WIN_TILES[2 * ch + 1], P)], KT)
        if ch == 12:
            return columns(w, [(WIN_TILES[24], P), (GA0, 6), (-1, 26), (GB0, 6), (-1, 26), (MLI0, 6), (-1, 26), (MLF0, 6), (-1, 26)], KT)
        if ch == 13:
            return columns(w, [(MOBA0 + 512, 256)], KT)
        return columns(w, [(MLV0, 256)] if ch == 14 else [(MLV0 + 256, 128), (-1, 128)], KT)
    if kind == "wout":
        return columns(a["w_out"][tag[1]], [(256 * tag[2], 256)], KT)
    if kind == "mla_in":
        w, i = a["mla_w_in_2"][0], tag[1]
        perm = [8, 0, 24, 16]
        kr = [(-1, 64), (640, 32)] + [(640 + p, 8) for p in perm]
        if i < 2:
            return columns(w, [(256 * i, 256)], KT)
        if i == 2:
            return columns(w, [(512, 128)] + kr, KT)
        return columns(w, [(672 + 256 * (i - 3), 256)], KT)
    if kind == "ukn":
        return columns(a["mla_w_ukv_2"][0], [(128 * h, 64) for h in range(16)], 2)
    if kind == "ukv":
        return columns(a["mla_w_ukv_2"][0], [(128 * h + 64, 64) for h in range(16)], 2)
    if kind == "uq":
        s = []
        for h in range(4 * tag[1], 4 * tag[1] + 4):
            s += [(96 * h, 96)] + [(96 * h + 64 + p, 8) for p in [8, 0, 24, 16]]
        return columns(a["mla_w_uq_2"][0], s, 3)
    if kind == "wout2":
        w = a["mla_w_out_2"][0] if tag[1] == 0 else a["gla_w_out_2"][0]
        return columns(w, [(256 * tag[2], 256)], KT)
    if kind == "gla_in":
        w, i = a["gla_w_in_2"][0], tag[1]
        t = [[(3072, 16), (-1, 16), (3088, 16), (-1, 80)]] + [[(512 + P * k, P)] for k in range(4)] \
            + [[(P * k, P)] for k in range(4)] + [[(2048 + P * k, P)] for k in range(8)] + [[(-1, P)]]
        return columns(w, t[2 * i] + t[2 * i + 1], KT)
    if kind == "gla_v":
        return columns(a["gla_w_in_2"][0], [(1024 + 256 * tag[1], 256)], KT)
    raise ValueError(tag)


def kernel(**inputs):
    import concourse.bacc as bacc
    from concourse.bass_utils import run_bass_kernel_spmd as run

    a = {k: np.asarray(v) for k, v in inputs.items()}

    def program(n_chunks, marks):
        nc = bacc.Bacc("TRN2", target_bir_lowering=False, num_devices=1)
        shapes = {"stream": (n_chunks, P, CHUNK), "cols": (P, NCOLS), "tab": (P, NTAB), "wg": (48, 512), "xt": (D, T), "ct": (D, T)}
        ins = [nc.dram_tensor(f"in_{k}_dram", s, F32, kind="ExternalInput").ap() for k, s in shapes.items()]
        out = nc.dram_tensor("out_0_dram", (D, T), F32, kind="ExternalOutput").ap()
        return nc, build(nc, *ins, out, marks)

    _, (marks, order) = program(1, None)
    nc, _ = program(len(order), marks)
    stream = np.zeros((len(order), P, CHUNK), np.float32)
    for n, tag in enumerate(order):
        c = chunk_of(tag, a).reshape(P, -1)
        stream[n, :, :c.shape[1]] = c
    wg = np.zeros((48, 512), np.float32)
    wg[0:16] = a["gla_w_gf_2"][0]
    wg[32:48] = a["gla_w_gb_2"][0]
    arrays = {"in_stream_dram": stream, "in_cols_dram": parameter_columns(a), "in_tab_dram": constant_tables(), "in_wg_dram": wg,
              "in_xt_dram": np.ascontiguousarray(a["x"][0].T), "in_ct_dram": np.ascontiguousarray(a["ctx_2"][0].T)}
    r = run(nc, [arrays], core_ids=[0])
    return np.ascontiguousarray(r.results[0]["out_0_dram"].T)[None]
```

```python
from contextlib import ExitStack

import numpy as np

import concourse.bass as bass
from concourse import mybir

ALU = mybir.AluOpType
ACT = mybir.ActivationFunctionType
AX = mybir.AxisListType
F32 = mybir.dt.float32
F32R = mybir.dt.float32r

P = 128
T = 256
D = 1024
KT = D // P
DEPTH = 2
FF = 2816
FT = FF // P
ALPHA = (2 * DEPTH) ** 0.25
LN_EPS, EPS = 1e-5, 1e-6
NEG = -1e30
CHUNK = 2048
RING = 3
SPLIT = 3
LEVELS = [1, 2, 4, 8, 16, 32, 64]
HD = 64
QS = HD ** -0.5
MLA_H, MLA_DK = 16, 96
MLA_SCALE = MLA_DK ** -0.5
GLA_H, GLA_SCALE = 4, P ** -0.5

GDN0, GA0, GB0, GZ0 = 0, 1152, 1158, 1164
MOBA0, MLQK0, MLV0, MLI0, MLF0, MLO0 = 1548, 2316, 3084, 3468, 3474, 3480
WIN_TILES = ([GDN0 + P * i for i in range(9)] + [GZ0 + P * i for i in range(3)] + [MOBA0 + P * i for i in range(4)]
             + [MLQK0 + P * i for i in range(6)] + [MLO0 + P * i for i in range(3)])
WIN_ORDER = [12] + list(range(12)) + [13, 14, 15]
ROW_A, ROW_B, ROW_I, ROW_F = 0, 32, 64, 96

COLS = {}
_at = 0
for _name, _n in [("c", 8), ("c2", 16), ("ada_b", 144), ("ada_b2", 48), ("ln_g", 48), ("ln_b", 48),
                  ("gconv", 72), ("mconv", 48), ("row_bias", 2), ("row_sign", 1), ("row_keep", 1), ("row_log", 2),
                  ("gdn_norm", 2), ("ml_norm", 6), ("norm_g", 16), ("final_g", 8), ("q_norm", 3), ("kv_norm", 2),
                  ("b_g", 8), ("o_norm", 2)]:
    COLS[_name] = (_at, _n)
    _at += _n
NCOLS = _at

TAB = {}
_at = 0
for _name, _n in [("ident", 128), ("ones", 256), ("blk", 128), ("first", 7 * 128), ("second", 7 * 128), ("strict", 128),
                  ("neg_t", 512), ("neg_q", 512), ("rope", 512), ("pair", 384)]:
    TAB[_name] = (_at, _n)
    _at += _n
NTAB = _at

WK = 18944
QKV, MQK, VT, ROWS, COLT, SCR = 0, 3840, 4864, 6144, 7424, 7680


class Steps:

    def __init__(self, semaphore, found):
        self.semaphore, self.found, self.count = semaphore, found, 0

    def named(self, *key):
        self.count += 1
        if key:
            assert key not in self.found, key
            self.found[key] = (self.semaphore.name, self.count)


def build(nc, stream, cols_in, tab_in, wg_in, xt_in, ct_in, out, marks):
    found, order = {}, []
    with ExitStack() as ctx:
        def sb(name, shape, dtype=F32):
            return ctx.enter_context(nc.sbuf_tensor(name, shape, dtype))

        def sem(name):
            return ctx.enter_context(nc.semaphore(name))

        ring = sb("ring", [P, RING, CHUNK])
        res = sb("res", [P, KT, 2 * T])
        xhi = sb("xhi", [P, KT, 2 * T], F32R)
        xlo = sb("xlo", [P, KT, 2 * T], F32R)
        whi = sb("whi", [P, SPLIT, CHUNK], F32R)
        wlo = sb("wlo", [P, SPLIT - 1, CHUNK], F32R)
        tab = sb("tab", [P, NTAB])
        cols = sb("cols", [P, NCOLS])
        wk = sb("wk", [P, WK])
        wg = sb("wg", [48, 512])
        sc = sb("sc", [P, 24])
        mod = sb("mod", [P, 2, 48])
        aux = sb("aux", [P, 2, 32])
        small = sb("small", [P, 48])
        PS = ctx.enter_context(nc.psum_tensor("ps", [P, 8, 512], F32))

        tensor_done, scalar_done = sem("tensor_done"), sem("scalar_done")
        vector_done, gpsimd_done = sem("vector_done"), sem("gpsimd_done")
        signals = {"tensor_done": tensor_done, "scalar_done": scalar_done, "vector_done": vector_done, "gpsimd_done": gpsimd_done}
        params_in = sem("params_in")
        tokens_in = sem("tokens_in")
        out_stored = sem("out_stored")
        landed = [sem(f"chunk_landed_{i}") for i in range(RING)]

        def step(*key):
            return marks[key][1] if marks else 1

        def step_of(*key):
            return (signals[marks[key][0]], marks[key][1]) if marks else (vector_done, 1)

        def bank(b, lo=0, hi=512):
            return PS[:, b, lo:hi]

        def banks(b, n):
            return PS[:, :, :].rearrange("p b n -> p (b n)")[:, b * 512:b * 512 + n]

        def W(at, n):
            return wk[:, at:at + n]

        def table(name, lo=0, n=None):
            a, m = TAB[name]
            return tab[:, a + lo:a + lo + (m - lo if n is None else n)]

        def col(name, i=0, n=1):
            a, _ = COLS[name]
            return cols[:, a + i:a + i + n]

        def tiles(ap, n):
            return ap.rearrange("p (t n) -> p t n", n=n)

        def over(ap, k):
            return ap.unsqueeze(1).to_broadcast([ap.shape[0], k, ap.shape[1]])

        def each(ap, n):
            return ap.unsqueeze(2).to_broadcast([ap.shape[0], ap.shape[1], n])

        ident = table("ident")
        ones = table("ones", 0, 128)
        blk = table("blk")
        XS = slice(T, 2 * T)
        CS = slice(0, T)

        ff_ax, ff_res, ff_cen, ff_sq = [W(SCR + 2048 * i, 2048) for i in range(4)]
        ff_rstd = W(SCR + 8192, 256)
        ff_sil = [W(SCR + 8448 + 256 * i, 256) for i in range(2)]
        ff_prod = [W(SCR + 8960 + 256 * i, 256) for i in range(2)]
        ff_hhi, ff_hlo = [xhi[:, i, 0:T] for i in range(4)], [xlo[:, i, 0:T] for i in range(4)]
        xt = ff_sq
        qkv = tiles(W(QKV, 3840), 256)
        mqk = tiles(W(MQK, 1024), 256)
        zg, og = res[:, 0:3, CS], res[:, 3:6, CS]
        vt = tiles(W(VT, 1280), 640)
        r_cs, r_rw, r_max, r_nm, r_beta = [W(ROWS + 256 * i, 256) for i in range(5)]
        colt = tiles(W(COLT, 256), 128)
        g_t, g_tt, g_dt, g_at, g_att = [W(SCR + 1536 * i, 1536) for i in range(5)]
        r_u, r_ab, r_ln = [g_at[:, 256 * i:256 * i + 256] for i in range(3)]
        g_x = g_dt
        g0 = SCR + 7680
        g_kb = tiles(W(g0, 768), 256)
        g_eg, g_kg, g_qd, g_kd = [tiles(W(g0 + 768 + 384 * i, 384), 128) for i in range(4)]
        g_ekd = g_kd
        g_vb = qkv[:, 6:9]
        g_vbt = tiles(W(g0 + 2304, 768), 384)
        g_kdt = W(g0 + 3072, 384)
        g_vn = tiles(W(QKV + 1536, 768), 384)
        g_r1, g_s = W(g0, 384), W(g0 + 384, 192)
        o_sq, o_rstd, o_tmp = W(SCR, 768), W(SCR + 1536, 768), W(SCR + 3072, 768)
        m_s, m_pt = W(SCR, 2048), W(SCR + 2048, 2048)
        l_w = W(SCR, 3072)
        l_em, l_h, l_sq, l_rstd = [W(SCR + 4608 + 768 * i, 768) for i in range(4)]
        nm8, sm8 = small[:, 0:8], small[:, 8:16]
        glast = small[:, 16:19]
        rkeep = small[:, 20:21]
        rcoef = small[:, 22:24]

        sq2, xt2 = W(0, 4096), W(4096, 4096)
        k_h = tiles(W(0, 4096), 512)
        v_h = tiles(W(4096, 2048), 512)
        gate2 = tiles(W(6144, 4096), 512)
        cq = tiles(W(10240, 2560), 512)
        q_h = [W(12800 + 512 * i, 512) for i in range(2)]
        p_h = [W(13824 + 1536 * i, 1536) for i in range(2)]
        pt_h = W(16896, 1536)
        rs2 = W(16896, 1024)
        o_prod = W(18432, 512)
        k_rot, q_rot = table("neg_t"), table("neg_q")
        nmx = small[:, 24:32]
        rsm = small[:, 32:40]
        a_k = [tiles(W(0, 1024), 256), tiles(W(1024, 1024), 256)]
        a_q = tiles(W(2048, 1024), 256)
        a_gate = tiles(W(3072, 2048), 256)
        a_v = tiles(W(5120, 4096), 1024)
        a_b = [[tiles(W(9216 + 1024 * (2 * d + s), 1024), 256) for s in range(2)] for d in range(2)]
        a_u, a_ab = W(13312, 2048), W(15360, 2048)
        a_r = W(17408, 512)
        a_atd = W(17920, 1024)
        a_ato = [W(512 * d, 512) for d in range(2)]
        a_st = tiles(W(5120, 2048), 256)
        a_qd = [a_b[d][0] for d in range(2)]
        a_e = [W(13312 + 1024 * i, 1024) for i in range(2)]
        a_m = [W(15360 + 1024 * i, 1024) for i in range(2)]
        a_kd, a_kdt = a_e, a_m
        a_o = W(13312, 2048)
        a_rs = tab[:, TAB["neg_t"][0]:TAB["neg_t"][0] + 1024]
        a_sq = W(15360, 2048)

        GATE, SPLIT_MODS = 8, (2, 5)

        def mixer_ada(m):
            return {0: 0, 1: 1, 3: 2, 4: 3, 6: 4, 7: 5, 9: 6, 10: 7} if m in SPLIT_MODS else {i: i for i in range(12)}

        def late_ada(m, p):
            return GATE + p // 2 if m in SPLIT_MODS and p % 2 and p < 8 else None

        def mod_area(m, ch):
            return 12800 if m == 7 else 0 if m not in SPLIT_MODS else g0 if ch < GATE else 4096

        def mod_acc(m, ch):
            n = 512 if m < 6 else 1024
            return tiles(W(mod_area(m, ch) + n * (ch % 2), n), 256)

        def mod_prod(m, ch):
            return W(mod_area(m, ch) + (1024 if m < 6 else 2048), 2048)

        def by_gpsimd(m, ch):
            if m == 0:
                return []
            if m == 7:
                return [1] if ch % 2 else []
            return [1] if m == 6 else [0]

        block = ctx.enter_context(nc.Block())

        @block.tensor
        def _(eng):
            done = Steps(tensor_done, found)
            last = [None]
            splits = [0]
            x = (xhi, xlo)

            def mm(o, l, r, start, stop, free=False):
                last[0] = nc.tensor.matmul(o, l, r, start=start, stop=stop, skip_group_check=free)

            def turn(o, i, k=128):
                last[0] = nc.tensor.transpose(o, i, ident[0:k, 0:k])

            def row_tile(parity):
                if parity:
                    last[0].then_inc(tensor_done, 1)
                    done.named()
                    eng.wait_ge(tensor_done, done.count)

            def take(*tag):
                n, i = len(order), splits[0]
                order.append(tag)
                splits[0] += 1
                found["chunk_no", i] = ("", n)
                found[("split_no",) + tag] = ("", i)
                eng.wait_ge(vector_done, step("split", i))
                return whi[:, i % SPLIT, :], wlo[:, i % (SPLIT - 1), :]

            def release():
                last[0].then_inc(tensor_done, 1)
                done.named("used", splits[0] - 1)

            def both(w, n):
                return [tiles(part, n) for part in w]

            def mm3(o, l, r, at_l, at_r, start, stop, free=False):
                mm(o, l[0][at_l], r[0][at_r], start, False, free)
                mm(o, l[0][at_l], r[1][at_r], False, False, free)
                mm(o, l[1][at_l], r[0][at_r], False, stop, free)

            def take_plain(*tag):
                n = len(order)
                order.append(tag)
                eng.wait_ge(landed[n % RING], 16 * (n // RING + 1))
                return ring[:, n % RING, :]

            def release_plain():
                last[0].then_inc(tensor_done, 1)
                done.named("chunk", len(order) - 1)

            def leave(*tag):
                found[("chunk_no",) + tag] = ("", len(order))
                order.append(tag)

            def mod_cols(m, ch):
                eng.wait_ge(gpsimd_done, step("modsum", m, ch))
                n = 1 if m < 6 else 2
                if ch == 0 and m:
                    eng.wait_ge(vector_done, step("mod", m - 1))
                late = 32 if m in SPLIT_MODS and ch >= GATE else 0
                for t in range(2):
                    for i in range(n):
                        c = (2 * ch + t) * n + i + late
                        mm(bank(7, c, c + 1), mod_acc(m, ch)[:, 2 * i, P * t:P * t + P], ones[:, 0:1], True, True)
                last[0].then_inc(tensor_done, 1)
                done.named("modcol", m, ch)
                if ch == 11:
                    found["modps", m] = found["modcol", m, ch]

            def ffn(l, f):
                m = 3 * l + 2 * f
                eng.wait_ge(vector_done, step("xm", m, 0))
                for p in range(12):
                    if p < FT // 2:
                        for j in (2 * p, 2 * p + 1):
                            w = both(take("w13", l, f, j), 256)
                            b = 4 + j % 3
                            if j >= 3:
                                eng.wait_ge(vector_done, step("h", m, j - 3))
                            for half in range(2):
                                for k in range(KT):
                                    if j == 0 and half == 0 and k == 4:
                                        eng.wait_ge(vector_done, step("xm", m))
                                    mm3(bank(b, 256 * half, 256 * half + 256), w, x, np.s_[:, k, P * half:P * half + P],
                                        np.s_[:, k, XS], k == 0, k == KT - 1)
                            release()
                            found["ab", m, j] = found["used", splits[0] - 1]
                            if j % 2 == 0 and late_ada(m, p):
                                leave("ada", m, late_ada(m, p))
                    if p >= 1:
                        w = both(take("w2", l, f, p - 1), D)
                        for i in range(2):
                            j = 2 * p - 2 + i
                            eng.wait_ge(vector_done, step("h", m, j))
                            for t in range(KT):
                                mm3(bank(t // 2, 256 * (t % 2), 256 * (t % 2) + 256), w, (ff_hhi[j % 4], ff_hlo[j % 4]),
                                    np.s_[:, i, P * t:P * t + P], np.s_[:, :], j == 0 and t % 2 == 0, j == FT - 1, free=True)
                            if i:
                                release()
                                found["down", m, j] = found["down", m, j - 1] = found["used", splits[0] - 1]
                    leave("ada", m + 1, p)
                    if p and late_ada(m, p - 1):
                        mod_cols(m, late_ada(m, p - 1))
                    if p:
                        mod_cols(m + 1, p - 1)
                found["acc", m] = found["down", m, FT - 1]

            def norm_sums(m):
                for t in range(KT):
                    eng.wait_ge(vector_done, step("res", m, t))
                    mm(bank(4, 0, 256), ones, tiles(ff_res, 256)[:, t], t == 0, t == KT - 1)
                last[0].then_inc(tensor_done, 1)
                done.named("mu", m)
                if m % 3 != 1:
                    mod_cols(m + 1, 11)
                for t in (0, 1, 4, 5):
                    eng.wait_ge(vector_done, step("sqp", m, t // 4))
                    mm(bank(5, 0, 256), ones, tiles(ff_sq, 256)[:, t], t == 0, t == 5)
                last[0].then_inc(tensor_done, 1)
                done.named("var", m)

            def mixer(l):
                m = 3 * l + 1
                eng.wait_ge(vector_done, step("xm", m, 0))
                for i, ch in enumerate(WIN_ORDER):
                    w = both(take("win", l, ch), 256)
                    b = i % 7
                    if i >= 7:
                        eng.wait_ge(*step_of("proj_read", m, i - 7))
                    if ch < 13:
                        for t in range(2):
                            for k in range(KT):
                                if i == 0 and t == 0 and k == 4:
                                    eng.wait_ge(vector_done, step("xm", m))
                                mm3(bank(b, 256 * t, 256 * t + 256), w, x, np.s_[:, k, P * t:P * t + P], np.s_[:, k, XS],
                                    k == 0, k == KT - 1)
                    else:
                        n = 256 if ch < 15 else 128
                        for t in range(2):
                            for k in range(KT):
                                mm3(bank(b, n * t, n * t + n), x, w, np.s_[:, k, T + P * t:T + P * t + P], np.s_[:, k, 0:n],
                                    k == 0, k == KT - 1)
                    release()
                    found["proj", m, i] = found["used", splits[0] - 1]
                    ada = mixer_ada(m + 1)
                    if i in ada:
                        leave("ada", m + 1, ada[i])
                        if i:
                            mod_cols(m + 1, ada[i] - 1)
                    if i == 12:
                        mod_cols(m + 1, len(ada) - 1)
                eng.wait_ge(*step_of("proj_read", m, 15))
                eng.wait_ge(*step_of("proj_read", m, 14))
                eng.wait_ge(*step_of("proj_read", m, 13))
                eng.wait_ge(vector_done, step("mod", m + 1))
                eng.wait_ge(*step_of("proj_read", m, 12))
                eng.wait_ge(*step_of("proj_read", m, 10))
                eng.wait_ge(*step_of("proj_read", m, 11))
                eng.wait_ge(*step_of("proj_read", m, 9))
                eng.wait_ge(scalar_done, step("l2sq", m))
                for t in range(6):
                    mm(banks(1, 1536)[:, 256 * t:256 * t + 256], blk, tiles(g_t, 256)[:, t], True, True)
                last[0].then_inc(tensor_done, 1)
                done.named("l2", m)
                eng.wait_ge(vector_done, step("rows", m))
                for t in range(2):
                    turn(bank(0, P * t, P * t + P), r_rw[:, P * t:P * t + P])
                for t in range(3):
                    mm(banks(4, 768)[:, 256 * t:256 * t + 256],
                       table("pair", P * t, P)[ROW_B:ROW_B + 32, :], r_beta[ROW_B:ROW_B + 32, :], True, True)
                for t in range(3):
                    mm(banks(6, 768)[:, 256 * t:256 * t + 256],
                       table("pair", P * t, P)[0:32, :], r_cs[0:32, :], True, True)
                last[0].then_inc(tensor_done, 1)
                done.named("pairs", m)
                eng.wait_ge(vector_done, step("l2_read", m))
                for h in range(6):
                    mm(banks(1, 1536)[:, 256 * h:256 * h + 256], each(ident[0:32, h:h + 1], 128)[:, 0, :], r_cs[0:32, :], True, True)
                last[0].then_inc(tensor_done, 1)
                done.named("gb", m)
                eng.wait_ge(vector_done, step("kb", m))
                eng.wait_ge(vector_done, step("gb_read", m))

                def head(ap, h, c=None):
                    a = ap[64 * (h % 2):64 * (h % 2) + 64, h // 2, :]
                    return a if c is None else a[:, P * c:P * c + P]
                K, Q = qkv[:, 3:6], qkv[:, 0:3]
                for h in [0, 2, 4, 1, 3, 5]:
                    if h == 1:
                        row_tile(1)
                    for c in range(2):
                        u = 2 * h + c
                        mm(banks(1, 1536)[:, P * u:P * u + P], head(K, h, c), head(g_kb, h, c), True, True)
                last[0].then_inc(tensor_done, 1)
                done.named("kk", m)
                eng.wait_ge(vector_done, step("pairs_read", m))
                eng.wait_ge(vector_done, step("gdn_in", m))
                for h in [0, 2, 4, 1, 3, 5]:
                    if h == 1:
                        row_tile(1)
                    for c in range(2):
                        u = 2 * h + c
                        mm(banks(4, 1536)[:, P * u:P * u + P], head(K, h, c), head(Q, h, c), True, True)
                last[0].then_inc(tensor_done, 1)
                done.named("qk", m)
                for c in range(2):
                    for t in range(3):
                        turn(bank(7 * c, P * t, P * t + P), g_vb[:, t, P * c:P * c + P])
                last[0].then_inc(tensor_done, 1)
                done.named("vbt", m)
                eng.wait_ge(scalar_done, step("vbt_read", m))
                for t in range(3):
                    turn(bank(0, P * t, P * t + P), g_kd[:, t, :])
                last[0].then_inc(tensor_done, 1)
                done.named("kdt", m)
                for li, s in enumerate(LEVELS):
                    for g in range(3):
                        eng.wait_ge(vector_done, step("t", m, li, g))
                        for u in range(4 * g, 4 * g + 4):
                            o = bank(1 + g, P * (u % 4), P * (u % 4) + P)
                            mm(o, g_at[:, P * u:P * u + P], g_t[:, P * u:P * u + P], True, True)
                        last[0].then_inc(tensor_done, 1)
                        done.named("x", m, li, g)
                    for g in range(3):
                        eng.wait_ge(vector_done, step("xs", m, li, g))
                        for u in range(4 * g, 4 * g + 4):
                            us = slice(P * u, P * u + P)
                            if li < 6:
                                mm(bank(1 + g, P * (u % 4), P * (u % 4) + P), g_tt[:, us], g_x[:, us], True, True)
                            mm(bank(4 + g, P * (u % 4), P * (u % 4) + P), g_x[:, us], g_tt[:, us], True, True)
                        last[0].then_inc(tensor_done, 1)
                        done.named("y", m, li, g)
                eng.wait_ge(vector_done, step("t", m, 7, 2))
                eng.wait_ge(vector_done, step("t", m, 7, 1))
                eng.wait_ge(vector_done, step("t", m, 7, 0))
                eng.wait_ge(scalar_done, step("kdt_read", m))

                def tt(h, c):
                    return g_tt[:, P * (2 * h + c):P * (2 * h + c) + P]
                for h in range(6):
                    mm(bank(0, 64 * h, 64 * h + 64), tt(h, 0), g_vbt[:, 0, 64 * h:64 * h + 64], True, True)
                last[0].then_inc(tensor_done, 1)
                done.named("vn0", m)
                eng.wait_ge(vector_done, step("vn0s", m))
                for h in range(6):
                    mm(PS[64 * (h % 2):64 * (h % 2) + 64, 7, 64 * (h // 2):64 * (h // 2) + 64],
                       g_kdt[:, 64 * h:64 * h + 64], g_vn[:, 0, 64 * h:64 * h + 64], True, True)
                last[0].then_inc(tensor_done, 1)
                done.named("s", m)
                eng.wait_ge(vector_done, step("ss", m))
                S = tiles(g_s, 64)
                for h in [0, 2, 4, 1, 3, 5]:
                    if h == 1:
                        row_tile(1)
                    mm(bank(0, 64 * h, 64 * h + 64), head(g_kg, h), head(S, h), True, True)
                last[0].then_inc(tensor_done, 1)
                done.named("ks", m)
                eng.wait_ge(vector_done, step("r1", m))
                for h in range(6):
                    mm(bank(7, 64 * h, 64 * h + 64), tt(h, 1), g_r1[:, 64 * h:64 * h + 64], True, True)
                last[0].then_inc(tensor_done, 1)
                done.named("vn1", m)
                eng.wait_ge(vector_done, step("vn1s", m))
                for h in range(6):
                    for c in range(2):
                        o = banks(0, 1024)[64 * (h % 2):64 * (h % 2) + 64, 256 * (h // 2) + P * c:256 * (h // 2) + P * c + P]
                        u = 2 * h + c
                        mm(o, g_vn[:, c, 64 * h:64 * h + 64], g_att[:, P * u:P * u + P], True, c == 0)
                        if c:
                            mm(o, head(S, h), head(g_qd, h), False, True)
                last[0].then_inc(tensor_done, 1)
                done.named("oa", m)
                eng.wait_ge(scalar_done, step("oa_sq", m))
                for t in range(3):
                    mm(banks(2, 1024)[:, 256 * t:256 * t + 256], blk, tiles(o_sq, 256)[:, t], True, True)
                last[0].then_inc(tensor_done, 1)
                done.named("oa_sum", m)
                for h in [0, 2, 1, 3]:
                    if h == 1:
                        row_tile(1)
                    for t in range(2):
                        u = 2 * h + t
                        mm(banks(4, 2048)[:, 256 * u:256 * u + 256], head(mqk[:, 0:2], h, t), head(mqk[:, 2:4], h), True, True)
                last[0].then_inc(tensor_done, 1)
                done.named("ms", m)
                eng.wait_ge(vector_done, step("mp", m))
                eng.wait_ge(vector_done, step("oa_done", m))
                for h in range(4):
                    for q in range(2):
                        for k in range(2):
                            at = 512 * h + 256 * k + P * q
                            turn(banks(0, 2048)[:, at:at + P], m_s[:, 512 * h + 256 * q + P * k:512 * h + 256 * q + P * k + P])
                last[0].then_inc(tensor_done, 1)
                done.named("mpt", m)
                eng.wait_ge(scalar_done, step("mpts", m))
                for h in range(4):
                    o = PS[64 * (h % 2):64 * (h % 2) + 64, 4, 256 * (h // 2):256 * (h // 2) + 256]
                    for k in range(2):
                        mm(o, vt[:, k, 64 * h:64 * h + 64], m_pt[:, 512 * h + 256 * k:512 * h + 256 * k + 256], k == 0, k == 1)
                last[0].then_inc(tensor_done, 1)
                done.named("mo", m)
                for h in range(6):
                    mm(banks(0, 1536)[:, 256 * h:256 * h + 256],
                       each(ident[ROW_I:ROW_I + 32, ROW_I + h:ROW_I + h + 1], 128)[:, 0, :], r_max[ROW_I:ROW_I + 32, :], True, True)
                eng.wait_ge(vector_done, step("mo_read", m))
                for t in range(3):
                    mm(banks(3, 1024)[:, 256 * t:256 * t + 256],
                       table("pair", P * t, P)[ROW_I:ROW_I + 32, :], r_nm[ROW_I:ROW_I + 32, :], True, True)
                last[0].then_inc(tensor_done, 1)
                done.named("mb", m)
                eng.wait_ge(vector_done, step("mb_read", m))
                eng.wait_ge(scalar_done, step("em", m))
                for h in [0, 2, 4, 1, 3, 5]:
                    if h == 1:
                        row_tile(1)
                    for st in range(2):
                        u = 2 * h + st
                        mm(banks(0, 3072)[:, 256 * u:256 * u + 256], head(qkv[:, 12:15], h, st), head(qkv[:, 9:12], h), True, True)
                last[0].then_inc(tensor_done, 1)
                done.named("ls", m)
                eng.wait_ge(vector_done, step("lp", m))
                for what in range(2):
                    for h in range(6):
                        o = banks(6 if what == 0 else 0, 1024)[64 * (h % 2):64 * (h % 2) + 64, 256 * (h // 2):256 * (h // 2) + 256]
                        for st in range(2):
                            lhs = vt[:, st, 256 + 64 * h:256 + 64 * h + 64] if what == 0 else ones[:, 0:64]
                            mm(o, lhs, l_w[:, 512 * h + 256 * st:512 * h + 256 * st + 256], st == 0, st == 1)
                last[0].then_inc(tensor_done, 1)
                done.named("lo", m)
                eng.wait_ge(vector_done, step("lh", m))
                for t in range(3):
                    mm(banks(2, 1024)[:, 256 * t:256 * t + 256], blk, tiles(l_h, 256)[:, t], True, True)
                last[0].then_inc(tensor_done, 1)
                done.named("lmu", m)
                eng.wait_ge(scalar_done, step("lsq", m))
                for t in range(3):
                    mm(banks(4, 1024)[:, 256 * t:256 * t + 256], blk, tiles(l_sq, 256)[:, t], True, True)
                last[0].then_inc(tensor_done, 1)
                done.named("lvar", m)
                eng.wait_ge(vector_done, step("mixed", m))
                for ch in range(4):
                    w = both(take("wout", l, ch), 256)
                    for t in range(2):
                        for k in range(KT):
                            mm3(bank(ch, 256 * t, 256 * t + 256), w, x, np.s_[:, k, P * t:P * t + P], np.s_[:, k, CS], k == 0, k == KT - 1)
                    release()
                found["acc", m] = found["used", splits[0] - 1]

            def rms(m):
                for t in range(KT):
                    eng.wait_ge(scalar_done, step("sq2", m, t // 4))
                    mm(bank(6), ones, tiles(sq2, 512)[:, t], t == 0, t == KT - 1)
                last[0].then_inc(tensor_done, 1)
                done.named("ms2", m)

            def mla():
                m = 6
                rms(m)
                eng.wait_ge(vector_done, step("xm", m))
                for i in range(7):
                    w = both(take("mla_in", i), 256)
                    for t in range(2):
                        n = 2 * i + t
                        if n >= 6:
                            eng.wait_ge(*step_of("in2_read", m, n - 6))
                        for k in range(KT):
                            mm3(bank(n % 6), w, x, np.s_[:, k, P * t:P * t + P], np.s_[:, k, :], k == 0, k == KT - 1)
                        if t == 0:
                            last[0].then_inc(tensor_done, 1)
                            done.named("in2", m, n)
                    release()
                    found["in2", m, 2 * i + 1] = found["used", splits[0] - 1]
                    for c in ((2 * i, 2 * i + 1) if i < 6 else ()):
                        leave("ada", 7, c)
                    for c in ((2 * i - 2, 2 * i - 1) if i else ()):
                        mod_cols(7, c)
                for n in range(8, 14):
                    eng.wait_ge(*step_of("in2_read", m, n))
                eng.wait_ge(scalar_done, step("cqsq", m))
                for t in range(3):
                    mm(bank(0), ones, tiles(W(0, 2560), 512)[:, t], t == 0, t == 2)
                for t in range(3, 5):
                    mm(bank(1), ones, tiles(W(0, 2560), 512)[:, t], t == 3, t == 4)
                last[0].then_inc(tensor_done, 1)
                done.named("cqsum", m)
                eng.wait_ge(vector_done, step("cqn", m))
                for n in range(8, 14):
                    eng.wait_ge(*step_of("in2_read", m, n))
                eng.wait_ge(vector_done, step("mod", 7))

                def keys_values(g):
                    w = tiles(take_plain("ukv", g), D)
                    for t in range(4):
                        if g:
                            eng.wait_ge(vector_done, step("o_read", 3))
                            eng.wait_ge(scalar_done, step("exp2", 7))
                        for k in range(2):
                            mm(bank(2 + t), w[:, k, P * t:P * t + P], cq[:, 3 + k, :], k == 0, k == 1)
                        last[0].then_inc(tensor_done, 1)
                        done.named("kn", g, t)
                    for t in range(4):
                        eng.wait_ge(scalar_done, step("kn_read", g, t, 0))
                        eng.wait_ge(vector_done, step("kn_read", g, t, 1))
                        for k in range(2):
                            mm(bank(2 + t), cq[:, 3 + k, P * t:P * t + P], w[:, k, 512:1024], k == 0, k == 1)
                        if t < 3:
                            last[0].then_inc(tensor_done, 1)
                            done.named("v2", g, t)
                    release_plain()
                    found["v2", g, 3] = found["chunk", len(order) - 1]
                    for t in range(4):
                        eng.wait_ge(*step_of("v2_read", g, t))
                    eng.wait_ge(scalar_done, step("k_rope", g))

                wq = [None]

                def queries(h):
                    if h % 4 == 0:
                        wq[0] = take_plain("uq", h // 4)[:, 0:1536].rearrange("p (k n) -> p k n", k=3)
                    hh = h % 4
                    if h:
                        eng.wait_ge(vector_done, step("q_read", h - 1))
                    for k in range(3):
                        mm(bank(0), wq[0][:, k, P * hh:P * hh + P], cq[:, k, :], k == 0, k == 2)
                    if hh == 3:
                        release_plain()
                        found["q2", h] = found["chunk", len(order) - 1]
                    else:
                        last[0].then_inc(tensor_done, 1)
                        done.named("q2", h)

                def scores(h):
                    eng.wait_ge(vector_done, step("q_read", h))
                    if h:
                        eng.wait_ge(scalar_done, step("exp2", h - 1))
                    for t in range(2):
                        mm(bank(2, 256 * t, 256 * t + 256), q_h[h % 2][0:96, P * t:P * t + P], k_h[0:96, h % 8, CS], True, True)
                    for t in range(2):
                        mm(bank(3 + t), q_h[h % 2][0:96, T + P * t:T + P * t + P], k_h[0:96, h % 8, :], True, True)
                    last[0].then_inc(tensor_done, 1)
                    done.named("s2", h)

                for h in range(MLA_H):
                    if h % 8 == 0:
                        keys_values(h // 8)
                        for first in (h, h + 1):
                            queries(first)
                            scores(first)
                    eng.wait_ge(gpsimd_done, step("pn", h))
                    if h:
                        eng.wait_ge(scalar_done, step("pt_a", h - 1))
                        eng.wait_ge(vector_done, step("pt_d", h - 1))
                    for q in range(2):
                        for k in range(2):
                            turn(bank(5, 256 * k + P * q, 256 * k + P * q + P), p_h[h % 2][:, 256 * q + P * k:256 * q + P * k + P])
                    for q in range(2):
                        for k in range(4):
                            at = 256 * k + P * q
                            turn(banks(6, 1024)[:, at:at + P], p_h[h % 2][:, 512 + 512 * q + P * k:512 + 512 * q + P * k + P])
                    last[0].then_inc(tensor_done, 1)
                    done.named("pt", h)
                    if h % 8 < 6:
                        queries(h + 2)
                    eng.wait_ge(scalar_done, step("pt_a", h))
                    eng.wait_ge(vector_done, step("pt_d", h))
                    if h % 2 == 0 and h:
                        eng.wait_ge(vector_done, step("o_read", h // 2 - 1))
                    pt = pt_h
                    hp = slice(64 * (h % 2), 64 * (h % 2) + 64)
                    for k in range(2):
                        mm(PS[hp, 1, 0:256], v_h[:, k, 64 * (h % 8):64 * (h % 8) + 64], pt[:, 256 * k:256 * k + 256], k == 0, k == 1)
                    for k in range(4):
                        mm(PS[hp, 1, 256:512], v_h[:, k, 64 * (h % 8):64 * (h % 8) + 64], pt[:, 512 + 256 * k:768 + 256 * k], k == 0, k == 3)
                    last[0].then_inc(tensor_done, 1)
                    done.named("o2", h)
                    if h % 8 < 6:
                        scores(h + 2)
                eng.wait_ge(vector_done, step("o_parts", 7))
                for ch in range(4):
                    w = both(take("wout2", 0, ch), 256)
                    for t in range(2):
                        n = 2 * ch + t
                        b = 2 + n % 4
                        if n >= 4:
                            eng.wait_ge(vector_done, step("res2", m, n - 4))
                        for k in range(KT):
                            mm3(bank(b), w, x, np.s_[:, k, P * t:P * t + P], np.s_[:, k, :], k == 0, k == KT - 1)
                        if t == 0:
                            last[0].then_inc(tensor_done, 1)
                            done.named("y2", m, n)
                    release()
                    found["y2", m, 2 * ch + 1] = found["used", splits[0] - 1]

            def gla():
                m = 7
                rms(m)
                eng.wait_ge(vector_done, step("xm", m))
                for i in range(9):
                    w = both(take("gla_in", i), 256)
                    for t in range(2):
                        n = 2 * i + t
                        if n == 17:
                            break
                        if n >= 6:
                            eng.wait_ge(*step_of("in2_read", m, n - 6))
                        cs = slice(0, 512) if n < 5 else XS
                        for k in range(KT):
                            mm3(bank(n % 6, 0, 512 if n < 5 else 256), w, x, np.s_[:, k, P * t:P * t + P], np.s_[:, k, cs], k == 0, k == KT - 1)
                        if t == 0 and n < 16:
                            last[0].then_inc(tensor_done, 1)
                            done.named("in2", m, n)
                    release()
                    found["in2", m, min(2 * i + 1, 16)] = found["used", splits[0] - 1]
                for ch in range(4):
                    w = both(take("gla_v", ch), 256)
                    for t in range(4):
                        n = 17 + 2 * ch + t // 2
                        if t % 2 == 0:
                            eng.wait_ge(*step_of("in2_read", m, n - 6))
                        at = 256 * (t % 2)
                        for k in range(KT):
                            mm3(bank(n % 6, at, at + 256), x, w, np.s_[:, k, P * t:P * t + P], np.s_[:, k, :], k == 0, k == KT - 1)
                        if t == 1:
                            last[0].then_inc(tensor_done, 1)
                            done.named("in2", m, n)
                    release()
                    found["in2", m, 18 + 2 * ch] = found["used", splits[0] - 1]
                for n in range(19, 25):
                    eng.wait_ge(*step_of("in2_read", m, n))
                for d in range(2):
                    for t in range(4):
                        mm(bank(4 * d + t), wg[32 * d:32 * d + 16, P * t:P * t + P], a_r[32 * d:32 * d + 16, :], True, True)
                    last[0].then_inc(tensor_done, 1)
                    done.named("ga", d)
                for d in range(2):
                    eng.wait_ge(vector_done, step("kd", d))
                    eng.wait_ge(vector_done, step("ga_read", d))
                    for t in range(2):
                        for h in range(4):
                            turn(bank(t, P * h, P * h + P) if d == 0 else bank(4 + t, P * h, P * h + P),
                                 tiles(a_kd[d], 256)[:, h, P * t:P * t + P])
                    last[0].then_inc(tensor_done, 1)
                    done.named("akdt", d)
                    eng.wait_ge(scalar_done, step("akdts", d))
                    for h in range(4):
                        o = banks(2 + 4 * d, 1024)[:, 256 * h:256 * h + 256]
                        for t in range(2):
                            mm(o, a_kdt[d][:, 512 * t + P * h:512 * t + P * h + P], a_v[:, t, 256 * h:256 * h + 256], t == 0, t == 1)
                    last[0].then_inc(tensor_done, 1)
                    done.named("ast", d)
                for h in range(4):
                    for t in range(2):
                        u = 2 * h + t
                        mm(banks(0, 1024)[:, P * u:P * u + P], a_k[1][:, h, P * t:P * t + P], a_q[:, h, P * t:P * t + P], True, True)
                last[0].then_inc(tensor_done, 1)
                done.named("diag")
                n = 0
                for li in range(8):
                    for d in range(2):
                        eng.wait_ge(vector_done, step("z", n))
                        eng.wait_ge(vector_done, step("lev_read", n - 1))
                        eng.wait_ge(scalar_done, step("ast_read", 1))
                        z = tiles(a_e[n % 2], 256)
                        b = 0 if n % 2 else 2
                        for h in range(4):
                            if li < 7:
                                for t in range(2):
                                    u = 2 * h + t
                                    zz = z[:, h, P * t:P * t + P]
                                    mm(banks(b, 1024)[:, P * u:P * u + P], zz, zz, True, True)
                            else:
                                k_, q_ = (z[:, h, 0:P], z[:, h, P:T]) if d == 0 else (z[:, h, P:T], z[:, h, 0:P])
                                mm(bank(b, P * h, P * h + P), k_, q_, True, True)
                        last[0].then_inc(tensor_done, 1)
                        done.named("lev", n)
                        n += 1
                eng.wait_ge(gpsimd_done, step("at_done"))
                eng.wait_ge(vector_done, step("lev_read", 14))
                eng.wait_ge(vector_done, step("lev_read", 15))
                eng.wait_ge(vector_done, step("aqd", 0))
                eng.wait_ge(vector_done, step("aqd", 1))
                for h in range(4):
                    for dvh in range(2):
                        lo = 256 * h + P * dvh
                        for t in range(2):
                            o = banks(4, 2048)[:, 2 * lo + P * t:2 * lo + P * t + P]
                            u = 2 * h + t
                            mm(o, a_v[:, 2 + t, lo:lo + P], a_atd[:, P * u:P * u + P], True, False)
                            mm(o, a_v[:, 3 - t, lo:lo + P], a_ato[1 - t][:, P * h:P * h + P], False, False)
                            for d in range(2):
                                mm(o, a_st[:, 4 * d + h, P * dvh:P * dvh + P], a_qd[d][:, h, P * t:P * t + P], False, d == 1)
                last[0].then_inc(tensor_done, 1)
                done.named("ao")
                eng.wait_ge(scalar_done, step("aosq"))
                for h in range(4):
                    for dvh in range(2):
                        mm(banks(0, 1024)[:, 256 * h:256 * h + 256], ones, tiles(a_sq, 256)[:, 2 * h + dvh], dvh == 0, dvh == 1)
                last[0].then_inc(tensor_done, 1)
                done.named("aosum")
                eng.wait_ge(vector_done, step("aod"))
                for ch in range(4):
                    w = both(take("wout2", 1, ch), 256)
                    for t in range(2):
                        n = 2 * ch + t
                        for k in range(KT):
                            mm3(bank(4 + ch, 256 * t, 256 * t + 256), w, x, np.s_[:, k, P * t:P * t + P], np.s_[:, k, XS], k == 0, k == KT - 1)
                    release()
                    found["y2", m, ch] = found["used", splits[0] - 1]
                for t in range(KT):
                    eng.wait_ge(scalar_done, step("fsq"))
                    mm(bank(0, 0, 256), ones, tiles(ff_sq, 256)[:, t], t == 0, t == KT - 1)
                last[0].then_inc(tensor_done, 1)
                done.named("fsum")

            eng.wait_ge(params_in, 48)
            for ch in range(12):
                leave("ada", 0, ch)
                mod_cols(0, ch)
            for l in range(DEPTH):
                ffn(l, 0)
                norm_sums(3 * l)
                mixer(l)
                norm_sums(3 * l + 1)
                ffn(l, 1)
                norm_sums(3 * l + 2)
            mla()
            gla()

        @block.sync
        def _(eng):
            eng.dma_start(cols[:, :], cols_in).then_inc(params_in, 16)
            eng.dma_start(tab[:, :], tab_in).then_inc(params_in, 16)
            eng.dma_start(wg[:, :], wg_in).then_inc(params_in, 16)
            eng.dma_start(res[:, :, XS], xt_in.rearrange("(k p) t -> p k t", p=P)).then_inc(tokens_in, 16)
            mid = found["chunk_no", found["split_no", "w13", 1, 1, 4][1]][1]
            for n in range(stream.shape[0]):
                if n >= RING:
                    eng.wait_ge(*step_of("chunk", n - RING))
                    if marks and ("chunk_too", n - RING) in marks:
                        eng.wait_ge(*step_of("chunk_too", n - RING))
                eng.dma_start(ring[:, n % RING, :], stream[n]).then_inc(landed[n % RING], 16)
                if n == mid:
                    eng.wait_ge(vector_done, step("lh", 4))
                    eng.dma_start(res[:, :, CS], ct_in.rearrange("(k p) t -> p k t", p=P)).then_inc(tokens_in, 16)
            eng.wait_ge(vector_done, step("final"))
            eng.dma_start(out.rearrange("(k p) t -> p k t", p=P), tiles(ff_cen, 256)).then_inc(out_stored, 16)
            eng.wait_ge(out_stored, 16)

        @block.scalar
        def _(eng):
            done = Steps(scalar_done, found)

            def act(o, i, f, *key, **kw):
                done.named(*key)
                return nc.scalar.activation(o, i, f, **kw)

            splits = [0]

            def split_to(i):
                while splits[0] <= i and ("chunk_no", splits[0]) in found:
                    i0 = splits[0]
                    n = found["chunk_no", i0][1]
                    eng.wait_ge(landed[n % RING], 16 * (n // RING + 1))
                    if i0 >= SPLIT:
                        eng.wait_ge(tensor_done, step("used", i0 - SPLIT))
                    act(whi[:, i0 % SPLIT, :], ring[:, n % RING, :], ACT.Copy, "hi", i0).then_inc(scalar_done, 1)
                    splits[0] += 1

            def split_no(*tag):
                return found[("split_no",) + tag][1]

            def rsqrt(ap, *key):
                eng.wait_ge(scalar_done, done.count)
                act(ap, ap, ACT.Ln).then_inc(scalar_done, 1)
                eng.wait_ge(scalar_done, done.count)
                act(ap, ap, ACT.Exp, *key, scale=-0.5).then_inc(scalar_done, 1)

            def affine(m, o, i, scale, bias, kts, *key):
                for t in kts:
                    act(o[:, t], i[:, t], ACT.Identity, *(key if t == kts[-1] else ()),
                        scale=scale[:, t:t + 1], bias=bias[:, t:t + 1]).then_inc(scalar_done, 1)

            def modulate():
                m, x = 0, aux[:, 0, :]
                eng.wait_ge(vector_done, step("aux", m))
                x3 = tiles(xt, 256)
                affine(m, x3, res[:, :, XS], x[:, 0:8], mod[:, 0, 0:8], range(0, 4), "xm_a", m)
                for half in range(2):
                    ts_ = slice(4 * half, 4 * half + 4)
                    eng.wait_ge(scalar_done, done.count)
                    if half:
                        eng.wait_ge(vector_done, step("xm_d", m))
                    act(xhi[:, ts_, XS], x3[:, ts_], ACT.Copy, "xh", m, half).then_inc(scalar_done, 1)

            def norm(m, last):
                split_to(last + 2)
                for half in range(2):
                    eng.wait_ge(vector_done, step("cen", m, half))
                    act(ff_sq[:, 1024 * half:1024 * half + 1024], ff_cen[:, 1024 * half:1024 * half + 1024], ACT.Square, "sq", m, half).then_inc(scalar_done, 1)
                eng.wait_ge(vector_done, step("ve", m))
                rsqrt(ff_rstd, "rstd", m)
                co = aux[:, (m + 1) % 2, :]
                for half in range(2):
                    if half:
                        eng.wait_ge(gpsimd_done, step("xn", m, 1))
                    else:
                        eng.wait_ge(vector_done, step("xn", m, 0))
                    if m < 5:
                        affine(m, xhi[:, :, XS], tiles(ff_cen, 256), co[:, 16:24], co[:, 24:32], range(4 * half, 4 * half + 4), "xh", m + 1, half)
                if m < 5:
                    found["xm_a", m + 1] = found["xh", m + 1, 1]
                g0_, b0_ = COLS["ln_g"][0] + 8 * m, COLS["ln_b"][0] + 8 * m
                affine(m, res[:, :, XS], tiles(ff_cen, 256), cols[:, g0_:g0_ + 8], cols[:, b0_:b0_ + 8], range(0, 8), "normed", m)

            def ffn(l, f):
                m = 3 * l + 2 * f
                if m == 0:
                    modulate()
                eng.wait_ge(scalar_done, done.count)
                act(tiles(ff_ax, 256), res[:, :, XS], ACT.Copy, "ax", m, scale=ALPHA).then_inc(scalar_done, 1)
                for j in range(FT):
                    split_to(split_no("w13", l, f, j) + 1)
                    eng.wait_ge(tensor_done, step("ab", m, j))
                    if j >= 2:
                        eng.wait_ge(vector_done, step("h", m, j - 2))
                    act(ff_sil[j % 2], bank(4 + j % 3, 0, 256), ACT.Silu, "sil", m, j).then_inc(scalar_done, 1)
                    split_to(split_no("w13", l, f, j) + 2)
                norm(m, split_no("w2", l, f, FT // 2 - 1))

            def mixer(l):
                m = 3 * l + 1
                for i, ch in enumerate(WIN_ORDER):
                    split_to(split_no("win", l, ch) + 1)
                    b = i % 7
                    eng.wait_ge(tensor_done, step("proj", m, i))
                    key = ("proj_read", m, i)
                    if ch in (12, 4):
                        key = ("proj_read_a", m, i)
                    if ch < 13:
                        todo = [t for t in (2 * ch, 2 * ch + 1) if 9 <= t < 16 or 22 <= t < 25]
                        for t in todo:
                            src = bank(b, 256 * (t % 2), 256 * (t % 2) + 256)
                            k = key if t == todo[-1] else ()
                            if t < 12:
                                act(zg[:, t - 9], src, ACT.Silu, *k).then_inc(scalar_done, 1)
                            elif t < 16:
                                act(mqk[:, t - 12], src, ACT.Copy, *k).then_inc(scalar_done, 1)
                            else:
                                act(og[:, t - 22], src, ACT.Sigmoid, *k).then_inc(scalar_done, 1)
                    else:
                        n = 256 if ch < 15 else 128
                        act(vt[:, :, 256 * (ch - 13):256 * (ch - 13) + n], tiles(bank(b, 0, 2 * n), n), ACT.Copy, *key).then_inc(scalar_done, 1)
                    split_to(split_no("win", l, ch) + 2)
                    if ch < 5:
                        for t in (2 * ch, 2 * ch + 1):
                            if t < 9:
                                eng.wait_ge(vector_done, step("conv", m, t))
                                act(qkv[:, t], qkv[:, t], ACT.Silu, *(("silu", m, t))).then_inc(scalar_done, 1)
                    if 8 <= ch < 11:
                        for t in (2 * ch, 2 * ch + 1):
                            eng.wait_ge(vector_done, step("conv", m, t))
                            act(qkv[:, t - 7], qkv[:, t - 7], ACT.Silu, "silu", m, t).then_inc(scalar_done, 1)
                split_to(split_no("win", l, 15) + 2)
                eng.wait_ge(vector_done, step("rab", m))
                eng.wait_ge(scalar_done, done.count)
                act(r_ln, r_ab, ACT.Exp, scale=-1.0).then_inc(scalar_done, 1)
                eng.wait_ge(scalar_done, done.count)
                act(r_ln, r_ln, ACT.Ln, "rln", m, bias=1.0).then_inc(scalar_done, 1)
                eng.wait_ge(scalar_done, done.count)
                act(r_beta[32:64, :], r_u[32:64, :], ACT.Exp, "rbe", m).then_inc(scalar_done, 1)
                eng.wait_ge(scalar_done, done.count)
                act(rcoef[:, 0:1], col("row_log", l), ACT.Exp, "rco", m).then_inc(scalar_done, 1)
                eng.wait_ge(scalar_done, done.count)
                act(g_t, W(QKV, 1536), ACT.Square, "l2sq", m).then_inc(scalar_done, 1)
                eng.wait_ge(vector_done, step("l2e", m))
                rsqrt(g_tt, "ri", m)
                eng.wait_ge(tensor_done, step("pairs", m))
                eng.wait_ge(vector_done, step("glast", m))
                eng.wait_ge(scalar_done, done.count)
                act(g_eg, tiles(banks(6, 768), 256)[:, :, P:T], ACT.Exp, "eg", m).then_inc(scalar_done, 1)
                for t in range(3):
                    act(g_ekd[:, t, :], banks(6, 768)[:, 256 * t:256 * t + P], ACT.Exp, *(("ekd", m) if t == 2 else ()),
                        scale=-1.0, bias=glast[:, t:t + 1]).then_inc(scalar_done, 1)
                eng.wait_ge(vector_done, step("gb_read", m))
                eng.wait_ge(vector_done, step("colt", m))
                for h in range(6):
                    for c in range(2):
                        u = slice(P * (2 * h + c), P * (2 * h + c) + P)
                        act(g_dt[:, u], g_dt[:, u], ACT.Exp, *(("dt", m) if h + c == 6 else ()), bias=colt[:, c, h:h + 1]).then_inc(scalar_done, 1)
                eng.wait_ge(tensor_done, step("vbt", m))
                act(g_vbt[:, 0, :], bank(0, 0, 384), ACT.Copy).then_inc(scalar_done, 1)
                act(g_vbt[:, 1, :], bank(7, 0, 384), ACT.Copy, "vbt_read", m).then_inc(scalar_done, 1)
                eng.wait_ge(tensor_done, step("kdt", m))
                act(g_kdt, bank(0, 0, 384), ACT.Copy, "kdt_read", m).then_inc(scalar_done, 1)
                eng.wait_ge(tensor_done, step("oa", m))
                act(o_sq, banks(0, 768), ACT.Square, "oa_sq", m).then_inc(scalar_done, 1)
                eng.wait_ge(vector_done, step("oa_e", m))
                rsqrt(o_rstd, "oa_r", m)
                eng.wait_ge(vector_done, step("msub", m))
                eng.wait_ge(scalar_done, done.count)
                act(m_s, m_s, ACT.Exp, "mexp", m).then_inc(scalar_done, 1)
                eng.wait_ge(tensor_done, step("mpt", m))
                eng.wait_ge(scalar_done, done.count)
                act(m_pt, banks(0, 2048), ACT.Copy, "mpts", m).then_inc(scalar_done, 1)
                eng.wait_ge(tensor_done, step("mo", m))
                eng.wait_ge(scalar_done, done.count)
                act(xhi[:, 3:5, CS], tiles(bank(4), 256), ACT.Copy, "mo_hi", m).then_inc(scalar_done, 1)
                eng.wait_ge(tensor_done, step("mb", m))
                eng.wait_ge(scalar_done, done.count)
                act(l_em, banks(3, 768), ACT.Exp, "em", m).then_inc(scalar_done, 1)
                eng.wait_ge(vector_done, step("mb_read", m))
                for h in range(6):
                    for st in range(2):
                        u = slice(256 * (2 * h + st), 256 * (2 * h + st) + 256)
                        act(l_w[:, u], l_w[:, u], ACT.Exp, *(("lw", m) if h + st == 6 else ()),
                            bias=colt[:, st, ROW_I + h:ROW_I + h + 1]).then_inc(scalar_done, 1)
                eng.wait_ge(vector_done, step("lcen", m))
                eng.wait_ge(scalar_done, done.count)
                act(l_sq, l_h, ACT.Square, "lsq", m).then_inc(scalar_done, 1)
                eng.wait_ge(vector_done, step("lve", m))
                rsqrt(l_rstd, "mixed_a", m)
                eng.wait_ge(vector_done, step("mixed", m))
                split_to(split_no("wout", l, 3))
                eng.wait_ge(tensor_done, step("acc", m))
                eng.wait_ge(scalar_done, done.count)
                act(tiles(ff_ax, 256), res[:, :, XS], ACT.Copy, "ax", m, scale=ALPHA).then_inc(scalar_done, 1)
                norm(m, split_no("wout", l, 3))

            def rms(m):
                if m == 6:
                    eng.wait_ge(tokens_in, 32)
                if m == 6:
                    eng.wait_ge(tensor_done, step("acc", 5))
                else:
                    eng.wait_ge(vector_done, step("o_read", 7))
                for half in range(2):
                    eng.wait_ge(scalar_done, done.count)
                    if m == 7:
                        eng.wait_ge(vector_done, step("res2", 6, 7))
                    else:
                        eng.wait_ge(scalar_done, step("normed", 5))
                    act(tiles(sq2, 512)[:, 4 * half:4 * half + 4], res[:, 4 * half:4 * half + 4, :], ACT.Square, "sq2", m, half).then_inc(scalar_done, 1)
                eng.wait_ge(vector_done, step("ms2e", m))
                rsqrt(rs2[:, 0:512], "rs2", m)
                eng.wait_ge(vector_done, step("xn2", m))
                eng.wait_ge(vector_done, step("aux", m))
                x = tiles(aux[:, m % 2, 0:32], 2)
                md = tiles(mod[:, m % 2, :], 2)
                x3 = tiles(xt2, 512)
                for t in range(KT):
                    act(x3[:, t, CS], x3[:, t, CS], ACT.Identity, *(("xm_a", m) if t == 7 else ()),
                        scale=x[:, t, 1:2], bias=md[:, t, 1:2]).then_inc(scalar_done, 1)
                eng.wait_ge(scalar_done, done.count)
                act(xhi[:, :, CS], x3[:, :, CS], ACT.Copy, "xh", m, 0).then_inc(scalar_done, 1)
                eng.wait_ge(vector_done, step("xm_d", m))
                act(xhi[:, :, XS], x3[:, :, XS], ACT.Copy, "xh", m, 1).then_inc(scalar_done, 1)

            def mla():
                m = 6
                rms(m)
                for n in range(14):
                    split_to(split_no("mla_in", min(n // 2 + 2, 6)))
                    eng.wait_ge(tensor_done, step("in2", m, n))
                    if n < 5:
                        act(cq[:, n], bank(n % 6), ACT.Copy, "in2_read", m, n).then_inc(scalar_done, 1)
                    elif n > 5:
                        act(gate2[:, n - 6], bank(n % 6), ACT.Silu, "in2_read", m, n).then_inc(scalar_done, 1)
                eng.wait_ge(scalar_done, done.count)
                act(W(0, 2560), W(10240, 2560), ACT.Square, "cqsq", m).then_inc(scalar_done, 1)
                eng.wait_ge(vector_done, step("cqe", m))
                rsqrt(rs2, "cqr", m)
                eng.wait_ge(tensor_done, step("cqsum", m))
                eng.wait_ge(vector_done, step("kr"))
                split_to(split_no("mla_in", 6))
                def exps(h):
                    eng.wait_ge(vector_done, step("nmx", h))
                    if h > 1:
                        eng.wait_ge(tensor_done, step("pt", h - 2))
                    p = p_h[h % 2]
                    eng.wait_ge(scalar_done, done.count)
                    for t in range(2):
                        act(p[:, 256 * t:256 * t + 256], bank(2, 256 * t, 256 * t + 256), ACT.Exp, scale=MLA_SCALE,
                            bias=nmx[:, 4 * (h % 2) + t:4 * (h % 2) + t + 1],
                            accum_out=rsm[:, 4 * (h % 2) + t:4 * (h % 2) + t + 1]).then_inc(scalar_done, 1)
                    for t in range(2):
                        act(p[:, 512 + 512 * t:1024 + 512 * t], bank(3 + t), ACT.Exp, *(("exp2", h) if t else ()), scale=MLA_SCALE,
                            bias=nmx[:, 4 * (h % 2) + 2 + t:4 * (h % 2) + 3 + t],
                            accum_out=rsm[:, 4 * (h % 2) + 2 + t:4 * (h % 2) + 3 + t]).then_inc(scalar_done, 1)

                for h in range(MLA_H):
                    g = h // 8
                    if h % 8 == 0:
                        for t in range(4):
                            eng.wait_ge(tensor_done, step("kn", g, t))
                            act(k_h[0:64, 2 * t], bank(2 + t)[0:64], ACT.Copy, "kn_read", g, t, 0).then_inc(scalar_done, 1)
                        act(k_h[64:96, :, :], over(k_rot[64:96, :], 8), ACT.Copy, "k_rope", g).then_inc(scalar_done, 1)
                        for t in range(0, 4, 2):
                            eng.wait_ge(tensor_done, step("v2", g, t))
                            act(v_h[:, t, :], bank(2 + t), ACT.Copy, "v2_read", g, t).then_inc(scalar_done, 1)
                        exps(h)
                        exps(h + 1)
                    pt_copy(h)
                    if h % 8 < 6:
                        exps(h + 2)
                for ch in range(4):
                    split_to(split_no("wout2", 0, ch) + 1)

            def pt_copy(h):
                eng.wait_ge(tensor_done, step("pt", h))
                act(pt_h[:, 0:1024], banks(5, 1024), ACT.Copy, "pt_a", h).then_inc(scalar_done, 1)

            def gla():
                m = 7
                rms(m)
                eng.wait_ge(tensor_done, step("y2", 6, 7))
                for n in range(1, 17):
                    split_to(split_no("gla_in", n // 2) + 2)
                    eng.wait_ge(tensor_done, step("in2", m, n))
                    if n < 5:
                        act(a_k[0][:, n - 1], bank(n % 6, 0, 256), ACT.Copy).then_inc(scalar_done, 1)
                        act(a_k[1][:, n - 1], bank(n % 6, 256, 512), ACT.Copy, "in2_read", m, n).then_inc(scalar_done, 1)
                    elif n < 9:
                        act(a_q[:, n - 5], bank(n % 6, 0, 256), ACT.Copy, "in2_read", m, n, scale=GLA_SCALE).then_inc(scalar_done, 1)
                    else:
                        act(a_gate[:, n - 9], bank(n % 6, 0, 256), ACT.Silu, "in2_read", m, n).then_inc(scalar_done, 1)
                for ch in range(4):
                    split_to(split_no("gla_v", ch) + 2)
                split_to(split_no("gla_v", 3) + 2)
                for d in range(2):
                    eng.wait_ge(vector_done, step("gab", d))
                    eng.wait_ge(scalar_done, done.count)
                    act(a_ab, a_ab, ACT.Exp, scale=-1.0).then_inc(scalar_done, 1)
                    eng.wait_ge(scalar_done, done.count)
                    act(a_ab, a_ab, ACT.Ln, "gln", d, bias=1.0).then_inc(scalar_done, 1)
                for d in range(2):
                    eng.wait_ge(vector_done, step("cum", d))
                    eng.wait_ge(vector_done, step("cum", 1))
                    e = 255 if d == 0 else 0
                    for h in range(4):
                        act(tiles(a_kd[d], 256)[:, h], a_b[d][0][:, h], ACT.Exp, *(("ekc", d) if h == 3 else ()),
                            scale=-1.0, bias=a_b[d][0][:, h, e:e + 1]).then_inc(scalar_done, 1)
                    eng.wait_ge(scalar_done, done.count)
                    act(a_qd[d], a_b[d][1], ACT.Exp, "eqd", d).then_inc(scalar_done, 1)
                for d in range(2):
                    eng.wait_ge(tensor_done, step("akdt", d))
                    act(a_kdt[d], banks(4 * d, 1024), ACT.Copy, "akdts", d).then_inc(scalar_done, 1)
                for d in range(2):
                    eng.wait_ge(tensor_done, step("ast", d))
                    eng.wait_ge(tensor_done, step("ast", 1))
                    act(a_st[:, 4 * d:4 * d + 4, :], tiles(banks(2 + 4 * d, 1024), 256), ACT.Copy, "ast_read", d).then_inc(scalar_done, 1)
                n = 0
                for li in range(8):
                    for d in range(2):
                        eng.wait_ge(vector_done, step("dif", n))
                        act(a_e[n % 2], a_e[n % 2], ACT.Exp, "ez", n).then_inc(scalar_done, 1)
                        n += 1
                eng.wait_ge(tensor_done, step("ao"))
                eng.wait_ge(scalar_done, done.count)
                act(a_sq, banks(4, 2048), ACT.Square, "aosq").then_inc(scalar_done, 1)
                eng.wait_ge(vector_done, step("aoe"))
                rsqrt(a_rs, "aor")
                for ch in range(4):
                    split_to(split_no("wout2", 1, ch))
                eng.wait_ge(vector_done, step("fres"))
                eng.wait_ge(scalar_done, done.count)
                act(ff_sq, tiles(ff_res, 256), ACT.Square, "fsq").then_inc(scalar_done, 1)
                eng.wait_ge(vector_done, step("fe"))
                rsqrt(ff_rstd, "frs")

            eng.wait_ge(params_in, 48)
            eng.wait_ge(scalar_done, done.count)
            act(sc[:, 0:8], col("c", 0, 8), ACT.Silu).then_inc(scalar_done, 1)
            eng.wait_ge(scalar_done, done.count)
            act(sc[:, 8:24], col("c2", 0, 16), ACT.Silu, "sc").then_inc(scalar_done, 1)
            eng.wait_ge(tokens_in, 16)
            for l in range(DEPTH):
                ffn(l, 0)
                mixer(l)
                ffn(l, 1)
            mla()
            gla()

        @block.vector
        def _(eng):
            done = Steps(vector_done, found)
            v = nc.vector

            def do(ins, *key):
                done.named(*key)
                return ins

            def tt(o, a, b, op, *key):
                return do(v.tensor_tensor(o, a, b, op), *key)

            def ts(o, a, s1, op0, s2=None, op1=None, *key):
                return do(v.tensor_scalar(o, a, s1, None, op0) if op1 is None else v.tensor_scalar(o, a, s1, s2, op0, op1), *key)

            def stt(o, a, s, b, op0, op1, *key):
                return do(v.scalar_tensor_tensor(out=o, in0=a, scalar=s, in1=b, op0=op0, op1=op1), *key)

            def copy(o, a, *key):
                return do(v.tensor_copy(o, a), *key)

            splits = [0]

            def split_to(i):
                while splits[0] <= i and ("chunk_no", splits[0]) in found:
                    i0 = splits[0]
                    n = found["chunk_no", i0][1]
                    eng.wait_ge(scalar_done, step("hi", i0))
                    if i0 >= SPLIT - 1:
                        eng.wait_ge(tensor_done, step("used", i0 - SPLIT + 1))
                    tt(wlo[:, i0 % (SPLIT - 1), :], ring[:, n % RING, :], whi[:, i0 % SPLIT, :].bitcast(F32), SUB, "split", i0).then_inc(vector_done, 1)
                    found["chunk", n] = found["split", i0]
                    splits[0] += 1

            def split_no(*tag):
                return found[("split_no",) + tag][1]

            def parts(hi, lo, whole, *key):
                eng.wait_ge(vector_done, done.count)
                copy(hi, whole).then_inc(vector_done, 1)
                eng.wait_ge(vector_done, done.count)
                tt(lo, whole, hi.bitcast(F32), SUB, *key).then_inc(vector_done, 1)

            MUL, ADD, SUB = ALU.mult, ALU.add, ALU.subtract

            def mod_part(m, ch):
                vecs = [i for i in range(1 if m < 6 else 2) if i not in by_gpsimd(m, ch)]
                if not vecs:
                    return
                n = found["chunk_no", "ada", m, ch][1]
                w = tiles(ring[:, n % RING, :], 256)
                acc = mod_acc(m, ch)
                if m == 0 and ch == 0:
                    eng.wait_ge(scalar_done, step("sc"))
                if ch >= 2:
                    eng.wait_ge(tensor_done, step("modcol", m, ch - 2))
                eng.wait_ge(landed[n % RING], 16 * (n // RING + 1))
                for k in range(KT):
                    for i in vecs:
                        c = sc[:, k:k + 1] if m < 6 else sc[:, 8 + 2 * k + i:9 + 2 * k + i]
                        a = acc[:, 2 * i + k % 2, :]
                        if k < 2:
                            ts(a, w[:, k, :], c, MUL).then_inc(vector_done, 1)
                        else:
                            eng.wait_ge(vector_done, done.count + 1 - 2 * len(vecs))
                            stt(a, w[:, k, :], c, a, MUL, ADD, *(("modacc", m, ch) if k == KT - 1 and i == vecs[-1] else ())).then_inc(vector_done, 1)
                found[("chunk_too" if by_gpsimd(m, ch) else "chunk", n)] = found["modacc", m, ch]

            def gate(m):
                eng.wait_ge(tensor_done, step("modps", m))
                eng.wait_ge(tensor_done, step("modcol", m + 1, 10))
                eng.wait_ge(vector_done, done.count)
                tt(mod[:, m % 2, 16:24], bank(7, 48, 56), col("ada_b", 24 * m + 16, 8), ADD, "gate", m).then_inc(vector_done, 1)
                eng.wait_ge(vector_done, done.count)
                ts(aux[:, m % 2, 8:16], mod[:, m % 2, 16:24], 1.0, ADD, 0.5, MUL).then_inc(vector_done, 1)

            def modulation(m):
                if m in SPLIT_MODS:
                    eng.wait_ge(tensor_done, step("modcol", m, GATE - 1))
                else:
                    eng.wait_ge(tensor_done, step("modps", m))
                if m >= 2:
                    eng.wait_ge(scalar_done, step("xm_a", m - 2))
                o = mod[:, m % 2, :]
                x = aux[:, m % 2, :]
                if m in SPLIT_MODS:
                    eng.wait_ge(vector_done, done.count)
                    tt(o[:, 0:16], bank(7, 0, 16), col("ada_b", 24 * m, 16), ADD, "mod", m).then_inc(vector_done, 1)
                    eng.wait_ge(vector_done, done.count)
                    ts(x[:, 0:8], o[:, 8:16], 1.0, ADD, None, None, "aux", m).then_inc(vector_done, 1)
                elif m < 6:
                    eng.wait_ge(vector_done, done.count)
                    tt(o[:, 0:24], bank(7, 0, 24), col("ada_b", 24 * m, 24), ADD, "mod", m).then_inc(vector_done, 1)
                    eng.wait_ge(vector_done, done.count)
                    ts(x[:, 0:8], o[:, 8:16], 1.0, ADD).then_inc(vector_done, 1)
                    if m % 3 == 1:
                        eng.wait_ge(vector_done, done.count)
                        ts(x[:, 8:16], o[:, 16:24], 1.0, ADD, None, None, "aux", m).then_inc(vector_done, 1)
                    else:
                        eng.wait_ge(vector_done, done.count)
                        ts(x[:, 8:16], o[:, 16:24], 1.0, ADD, 0.5, MUL, "aux", m).then_inc(vector_done, 1)
                else:
                    eng.wait_ge(vector_done, done.count)
                    tt(tiles(o, 2), tiles(bank(7, 0, 48), 2), each(col("ada_b2", 24 * (m - 6), 24), 2), ADD, "mod", m).then_inc(vector_done, 1)
                    eng.wait_ge(vector_done, done.count)
                    ts(x[:, 0:16], o[:, 16:32], 1.0, ADD).then_inc(vector_done, 1)
                    eng.wait_ge(vector_done, done.count)
                    tt(tiles(x[:, 0:16], 2), tiles(x[:, 0:16], 2), each(col("norm_g", 8 * (m - 6), 8), 2), MUL, "aux", m).then_inc(vector_done, 1)

            def affine(o, i, scale, bias, kts, *key):
                eng.wait_ge(vector_done, done.count)
                for t in kts:
                    ts(o[:, t], i[:, t], scale[:, t:t + 1], MUL, bias[:, t:t + 1], ADD, *(key if t == kts[-1] else ())).then_inc(vector_done, 1)

            def modulate():
                m, x = 0, aux[:, 0, :]
                x3 = tiles(xt, 256)
                affine(x3, res[:, :, XS], x[:, 0:8], mod[:, 0, 0:8], range(4, 8), "xm_d", m)
                for half in range(2):
                    low_part(m, half)

            def low_part(m, half):
                ts_ = slice(4 * half, 4 * half + 4)
                eng.wait_ge(scalar_done, step("xh", m, half))
                eng.wait_ge(vector_done, done.count)
                tt(xlo[:, ts_, XS], tiles(xt, 256)[:, ts_], xhi[:, ts_, XS].bitcast(F32), SUB, *(("xm", m) if half else ("xm", m, 0))).then_inc(vector_done, 1)

            def norm(m, last):
                g = aux[:, m % 2, 8:16]
                split_to(last + 1)
                eng.wait_ge(tensor_done, step("acc", m))
                if m in SPLIT_MODS:
                    gate(m)
                eng.wait_ge(scalar_done, step("ax", m))
                eng.wait_ge(vector_done, done.count)
                for t in range(KT):
                    stt(tiles(ff_res, 256)[:, t], bank(t // 2, 256 * (t % 2), 256 * (t % 2) + 256), g[:, t:t + 1],
                        tiles(ff_ax, 256)[:, t], MUL, ADD, "res", m, t).then_inc(vector_done, 1)
                eng.wait_ge(tensor_done, step("mu", m))
                eng.wait_ge(vector_done, done.count)
                cen = tiles(ff_cen, 256)
                for half in range(2):
                    hs = slice(4 * half, 4 * half + 4)
                    stt(cen[:, hs], over(bank(4, 0, 256), 4), -1.0 / D, tiles(ff_res, 256)[:, hs], MUL, ADD, "cen", m, half).then_inc(vector_done, 1)
                for half in range(2):
                    lo = 1024 * half
                    eng.wait_ge(scalar_done, step("sq", m, half))
                    tt(ff_sq[:, lo:lo + 512], ff_sq[:, lo:lo + 512], ff_sq[:, lo + 512:lo + 1024], ADD, "sqp", m, half).then_inc(vector_done, 1)
                split_to(last + 2)
                if m % 3 != 1:
                    modulation(m + 1)
                if m < 5:
                    co = aux[:, (m + 1) % 2, :]
                    eng.wait_ge(vector_done, done.count)
                    tt(co[:, 16:24], col("ln_g", 8 * m, 8), co[:, 0:8], MUL).then_inc(vector_done, 1)
                    tt(co[:, 24:32], col("ln_b", 8 * m, 8), co[:, 0:8], MUL).then_inc(vector_done, 1)
                    eng.wait_ge(vector_done, done.count)
                    tt(co[:, 24:32], co[:, 24:32], mod[:, (m + 1) % 2, 0:8], ADD).then_inc(vector_done, 1)
                eng.wait_ge(tensor_done, step("var", m))
                eng.wait_ge(vector_done, done.count)
                ts(ff_rstd, bank(5, 0, 256), 1.0 / D, MUL, LN_EPS, ADD, "ve", m).then_inc(vector_done, 1)
                eng.wait_ge(scalar_done, step("rstd", m))
                tt(cen[:, 0:4], cen[:, 0:4], over(ff_rstd, 4), MUL, "xn", m, 0).then_inc(vector_done, 1)
                if m < 5:
                    x3 = tiles(xt, 256)
                    affine(x3, cen, co[:, 16:24], co[:, 24:32], range(0, 4))
                    low_part(m + 1, 0)
                    eng.wait_ge(gpsimd_done, step("xn", m, 1))
                    affine(x3, cen, co[:, 16:24], co[:, 24:32], range(4, 8))
                    low_part(m + 1, 1)
                else:
                    eng.wait_ge(gpsimd_done, step("xn", m, 1))
                eng.wait_ge(scalar_done, step("normed", m))

            def ffn(l, f):
                m = 3 * l + 2 * f
                if m == 0:
                    modulate()
                for j in range(FT):
                    split_to(split_no("w13", l, f, j) + 1)
                    eng.wait_ge(tensor_done, step("ab", m, j))
                    eng.wait_ge(scalar_done, step("sil", m, j))
                    tt(ff_prod[j % 2], ff_sil[j % 2], bank(4 + j % 3, 256, 512), MUL).then_inc(vector_done, 1)
                    if j >= 4:
                        eng.wait_ge(tensor_done, step("down", m, j - 4))
                    parts(ff_hhi[j % 4], ff_hlo[j % 4], ff_prod[j % 2], "h", m, j)
                    if j % 2:
                        mod_part(m + 1, j // 2)
                mod_part(m + 1, 11)
                norm(m, split_no("w2", l, f, FT // 2 - 1))

            def mixer(l):
                m = 3 * l + 1
                for i, ch in enumerate(WIN_ORDER):
                    split_to(split_no("win", l, ch) + 1)
                    b = i % 7
                    mine = [t for t in (2 * ch, 2 * ch + 1) if t < 9 or 16 <= t < 22 or t == 25] if ch < 13 else []
                    if mine:
                        eng.wait_ge(tensor_done, step("proj", m, i))
                    if ch in (12, 4):
                        eng.wait_ge(scalar_done, step("proj_read_a", m, i))
                    for t in mine:
                        src = bank(b, 256 * (t % 2), 256 * (t % 2) + 256)
                        key = ("proj_read", m, i) if t == mine[-1] else ()
                        if t == 25:
                            eng.wait_ge(vector_done, done.count)
                            ts(r_u, src, col("row_bias", l), ADD, col("row_sign"), MUL, *key).then_inc(vector_done, 1)
                            eng.wait_ge(vector_done, done.count)
                            stt(r_ab, r_u, -1.0, r_u, MUL, ALU.max, "rab", m).then_inc(vector_done, 1)
                            continue
                        y = qkv[:, t if t < 9 else t - 7]

                        def cw(tap):
                            return col("gconv", 36 * l + 9 * tap + t) if t < 9 else col("mconv", 24 * l + 6 * tap + t - 16)
                        eng.wait_ge(vector_done, done.count)
                        ts(y, src, cw(3), MUL).then_inc(vector_done, 1)
                        for back in (1, 2, 3):
                            if back == 3:
                                eng.wait_ge(vector_done, done.count)
                                v.scalar_tensor_tensor(out=y[:, back:], in0=src[:, :T - back], scalar=cw(3 - back),
                                                                in1=y[:, back:], op0=MUL, op1=ADD).then_inc(vector_done, 1)
                                done.named("conv", m, t)
                            else:
                                eng.wait_ge(vector_done, done.count)
                                stt(y[:, back:], src[:, :T - back], cw(3 - back), y[:, back:], MUL, ADD).then_inc(vector_done, 1)
                    if mine and 25 not in mine:
                        found["proj_read", m, i] = found["conv", m, mine[-1]]
                split_to(split_no("win", l, 15) + 2)
                modulation(m + 1)
                eng.wait_ge(scalar_done, step("rln", m))
                eng.wait_ge(scalar_done, step("rco", m))
                eng.wait_ge(scalar_done, step("rbe", m))
                eng.wait_ge(vector_done, done.count)
                stt(r_ln, r_u, 0.0, r_ln, ALU.max, ADD).then_inc(vector_done, 1)
                eng.wait_ge(vector_done, done.count)
                ts(rcoef[:, 1:2], rcoef[:, 0:1], -1.0, MUL).then_inc(vector_done, 1)
                eng.wait_ge(vector_done, done.count)
                ts(r_ln, r_ln, rcoef[:, 1:2], MUL).then_inc(vector_done, 1)
                onesrow = table("ones")
                eng.wait_ge(vector_done, done.count)
                do(v.tensor_tensor_scan(r_cs[:, 0:P], onesrow[:, 0:P], r_ln[:, 0:P], 0.0, MUL, ADD)).then_inc(vector_done, 1)
                eng.wait_ge(vector_done, done.count)
                ts(rkeep, r_cs[:, P - 1:P], col("row_keep"), MUL).then_inc(vector_done, 1)
                eng.wait_ge(vector_done, done.count)
                do(v.tensor_tensor_scan(r_cs[:, P:T], onesrow[:, 0:P], r_ln[:, P:T], rkeep, MUL, ADD)).then_inc(vector_done, 1)
                eng.wait_ge(vector_done, done.count)
                ts(r_rw, r_cs, -1.0, MUL).then_inc(vector_done, 1)
                I = slice(ROW_I, ROW_I + 32)
                eng.wait_ge(vector_done, done.count)
                copy(r_nm[I, :], r_cs[ROW_F:ROW_F + 32, :]).then_inc(vector_done, 1)
                eng.wait_ge(vector_done, done.count)
                tt(r_rw[I, :], r_u[I, :], r_nm[I, :], SUB).then_inc(vector_done, 1)
                eng.wait_ge(vector_done, done.count)
                do(v.tensor_tensor_scan(r_max[I, :], r_rw[I, :], r_rw[I, :], 0.0, ALU.max, ALU.max)).then_inc(vector_done, 1)
                eng.wait_ge(vector_done, done.count)
                stt(r_nm[I, :], r_max[I, :], -1.0, r_nm[I, :], MUL, SUB).then_inc(vector_done, 1)
                B = slice(ROW_B, ROW_B + 32)
                eng.wait_ge(vector_done, done.count)
                ts(r_beta[B, :], r_beta[B, :], 1.0, ADD).then_inc(vector_done, 1)
                eng.wait_ge(vector_done, done.count)
                do(v.reciprocal(r_beta[B, :], r_beta[B, :]), "rows", m).then_inc(vector_done, 1)
                eng.wait_ge(tensor_done, step("l2", m))
                eng.wait_ge(vector_done, done.count)
                ts(g_tt, banks(1, 1536), EPS, ADD, None, None, "l2e", m).then_inc(vector_done, 1)
                found["l2_read", m] = found["l2e", m]
                eng.wait_ge(scalar_done, step("ri", m))
                eng.wait_ge(vector_done, done.count)
                tt(W(QKV, 1536), W(QKV, 1536), g_tt, MUL).then_inc(vector_done, 1)
                eng.wait_ge(tensor_done, step("pairs", m))
                eng.wait_ge(vector_done, done.count)
                copy(glast, tiles(banks(6, 768), 256)[:, :, P - 1], "glast", m).then_inc(vector_done, 1)
                eng.wait_ge(vector_done, done.count)
                copy(W(COLT, 256), bank(0, 0, 256), "colt", m).then_inc(vector_done, 1)
                eng.wait_ge(vector_done, done.count)
                tt(g_kb, qkv[:, 3:6], tiles(banks(4, 768), 256), MUL, "kb0", m).then_inc(vector_done, 1)
                eng.wait_ge(scalar_done, step("silu", m, 8))
                eng.wait_ge(vector_done, done.count)
                tt(g_vb, qkv[:, 6:9], tiles(banks(4, 768), 256), MUL, "kb", m).then_inc(vector_done, 1)
                eng.wait_ge(tensor_done, step("gb", m))
                eng.wait_ge(vector_done, done.count)
                tt(tiles(g_dt, 128), tiles(banks(1, 1536), 128), over(table("neg_t", 0, 128), 12), ADD, "gb_read", m).then_inc(vector_done, 1)
                eng.wait_ge(scalar_done, step("eg", m))
                eng.wait_ge(scalar_done, step("ekd", m))
                eng.wait_ge(vector_done, done.count)
                tt(g_kg, g_kb[:, :, P:T], g_eg, MUL).then_inc(vector_done, 1)
                eng.wait_ge(vector_done, done.count)
                stt(g_qd, qkv[:, 0:3, P:T], QS, g_eg, MUL, MUL, "pairs_read", m).then_inc(vector_done, 1)
                eng.wait_ge(vector_done, done.count)
                tt(g_kd, qkv[:, 3:6, 0:P], g_ekd, MUL, "gdn_in", m).then_inc(vector_done, 1)
                eng.wait_ge(tensor_done, step("kk", m))
                eng.wait_ge(scalar_done, step("dt", m))
                eng.wait_ge(vector_done, done.count)
                tt(g_at, banks(1, 1536), g_dt, MUL).then_inc(vector_done, 1)
                eng.wait_ge(vector_done, done.count)
                tt(tiles(g_at, 128), tiles(g_at, 128), over(table("strict"), 12), MUL).then_inc(vector_done, 1)
                eng.wait_ge(vector_done, done.count)
                copy(tiles(g_t, 128), over(ident, 12)).then_inc(vector_done, 1)
                eng.wait_ge(vector_done, done.count)
                copy(tiles(g_tt, 128), over(ident, 12)).then_inc(vector_done, 1)
                eng.wait_ge(tensor_done, step("qk", m))
                eng.wait_ge(vector_done, done.count)
                stt(g_att, banks(4, 1536), QS, g_dt, MUL, MUL, "t", m, 0, 0).then_inc(vector_done, 1)
                found["t", m, 0, 1] = found["t", m, 0, 2] = found["t", m, 0, 0]
                for li in range(7):
                    mask = table("second", P * li, P)
                    for g in range(3):
                        sl = slice(512 * g, 512 * g + 512)
                        eng.wait_ge(tensor_done, step("x", m, li, g))
                        eng.wait_ge(vector_done, done.count)
                        tt(tiles(g_x[:, sl], 128), tiles(bank(1 + g), 128), over(mask, 4), MUL, "xs", m, li, g).then_inc(vector_done, 1)
                    for g in range(3):
                        sl = slice(512 * g, 512 * g + 512)
                        eng.wait_ge(tensor_done, step("y", m, li, g))
                        if li < 6:
                            tt(g_t[:, sl], g_t[:, sl], bank(1 + g), SUB).then_inc(vector_done, 1)
                        tt(g_tt[:, sl], g_tt[:, sl], bank(4 + g), SUB, "t", m, li + 1, g).then_inc(vector_done, 1)
                eng.wait_ge(tensor_done, step("vn0", m))
                eng.wait_ge(vector_done, done.count)
                copy(g_vn[:, 0, :], bank(0, 0, 384), "vn0s", m).then_inc(vector_done, 1)
                eng.wait_ge(tensor_done, step("s", m))
                eng.wait_ge(vector_done, done.count)
                copy(g_s, bank(7, 0, 192), "ss", m).then_inc(vector_done, 1)
                eng.wait_ge(tensor_done, step("ks", m))
                eng.wait_ge(scalar_done, step("vbt_read", m))
                eng.wait_ge(vector_done, done.count)
                tt(g_r1, g_vbt[:, 1, :], bank(0, 0, 384), SUB, "r1", m).then_inc(vector_done, 1)
                eng.wait_ge(tensor_done, step("vn1", m))
                eng.wait_ge(vector_done, done.count)
                copy(g_vn[:, 1, :], bank(7, 0, 384), "vn1s", m).then_inc(vector_done, 1)
                eng.wait_ge(tensor_done, step("oa_sum", m))
                eng.wait_ge(vector_done, done.count)
                ts(o_rstd, banks(2, 768), 1.0 / HD, MUL, EPS, ADD, "oa_e", m).then_inc(vector_done, 1)
                eng.wait_ge(scalar_done, step("oa_r", m))
                eng.wait_ge(vector_done, done.count)
                tt(o_tmp, banks(0, 768), o_rstd, MUL).then_inc(vector_done, 1)
                eng.wait_ge(vector_done, done.count)
                stt(tiles(o_tmp, 256), tiles(o_tmp, 256), col("gdn_norm", l), zg, MUL, MUL).then_inc(vector_done, 1)
                parts(xhi[:, 0:3, CS], xlo[:, 0:3, CS], tiles(o_tmp, 256), "oa_done", m)
                eng.wait_ge(tensor_done, step("ms", m))
                eng.wait_ge(vector_done, done.count)
                stt(tiles(m_s, 512), tiles(banks(4, 2048), 512), QS, over(table("neg_q"), 4), MUL, ADD).then_inc(vector_done, 1)
                s3 = tiles(m_s, 256)
                eng.wait_ge(vector_done, done.count)
                do(v.tensor_reduce(nm8, s3, AX.X, ALU.max, negate=True)).then_inc(vector_done, 1)
                eng.wait_ge(vector_done, done.count)
                tt(s3, s3, each(nm8, 256), ADD, "msub", m).then_inc(vector_done, 1)
                eng.wait_ge(scalar_done, step("mexp", m))
                eng.wait_ge(vector_done, done.count)
                do(v.tensor_reduce(sm8, s3, AX.X, ADD)).then_inc(vector_done, 1)
                eng.wait_ge(vector_done, done.count)
                do(v.reciprocal(sm8, sm8)).then_inc(vector_done, 1)
                eng.wait_ge(vector_done, done.count)
                tt(s3, s3, each(sm8, 256), MUL, "mp", m).then_inc(vector_done, 1)
                eng.wait_ge(scalar_done, step("mo_hi", m))
                tt(xlo[:, 3:5, CS], tiles(bank(4), 256), xhi[:, 3:5, CS].bitcast(F32), SUB, "mo_read", m).then_inc(vector_done, 1)
                eng.wait_ge(tensor_done, step("mb", m))
                eng.wait_ge(tensor_done, step("mo", m))
                for h in range(6):
                    tt(tiles(l_w[:, 512 * h:512 * h + 512], 256), tiles(table("neg_t"), 256),
                       over(banks(0, 1536)[:, 256 * h:256 * h + 256], 2), SUB, *(("mb_read", m) if h == 5 else ())).then_inc(vector_done, 1)
                eng.wait_ge(tensor_done, step("ls", m))
                eng.wait_ge(scalar_done, step("lw", m))
                eng.wait_ge(vector_done, done.count)
                stt(l_w, banks(0, 3072), QS, l_w, MUL, MUL, "lp", m).then_inc(vector_done, 1)
                eng.wait_ge(tensor_done, step("lo", m))
                eng.wait_ge(scalar_done, step("em", m))
                eng.wait_ge(vector_done, done.count)
                stt(l_em, banks(0, 768), -1.0, l_em, MUL, ALU.max).then_inc(vector_done, 1)
                eng.wait_ge(vector_done, done.count)
                tt(l_em, banks(0, 768), l_em, ALU.max).then_inc(vector_done, 1)
                eng.wait_ge(vector_done, done.count)
                do(v.reciprocal(l_em, l_em)).then_inc(vector_done, 1)
                eng.wait_ge(vector_done, done.count)
                tt(l_h, banks(6, 768), l_em, MUL).then_inc(vector_done, 1)
                eng.wait_ge(vector_done, done.count)
                tt(tiles(l_h, 256), tiles(l_h, 256), og, MUL, "lh", m).then_inc(vector_done, 1)
                eng.wait_ge(tensor_done, step("lmu", m))
                eng.wait_ge(vector_done, done.count)
                stt(l_h, banks(2, 768), -1.0 / HD, l_h, MUL, ADD, "lcen", m).then_inc(vector_done, 1)
                eng.wait_ge(tensor_done, step("lvar", m))
                eng.wait_ge(vector_done, done.count)
                ts(l_rstd, banks(4, 768), 1.0 / HD, MUL, EPS, ADD, "lve", m).then_inc(vector_done, 1)
                eng.wait_ge(scalar_done, step("mixed_a", m))
                eng.wait_ge(vector_done, done.count)
                for t in range(3):
                    stt(tiles(l_sq, 256)[:, t], tiles(l_h, 256)[:, t], col("ml_norm", 3 * l + t), tiles(l_rstd, 256)[:, t], MUL, MUL).then_inc(vector_done, 1)
                parts(xhi[:, 5:8, CS], xlo[:, 5:8, CS], tiles(l_sq, 256), "mixed", m)
                split_to(split_no("wout", l, 3))
                norm(m, split_no("wout", l, 3))

            def rms(m):
                if m == 6:
                    eng.wait_ge(tokens_in, 32)
                eng.wait_ge(tensor_done, step("ms2", m))
                eng.wait_ge(vector_done, done.count)
                ts(rs2[:, 0:512], bank(6), 1.0 / D, MUL, EPS, ADD, "ms2e", m).then_inc(vector_done, 1)
                eng.wait_ge(scalar_done, step("rs2", m))
                if m == 6:
                    eng.wait_ge(scalar_done, step("normed", 5))
                else:
                    eng.wait_ge(tensor_done, step("y2", 6, 7))
                eng.wait_ge(vector_done, done.count)
                x3 = tiles(xt2, 512)
                tt(x3, res[:, :, :], over(rs2[:, 0:512], KT), MUL, "xn2", m).then_inc(vector_done, 1)
                x = tiles(aux[:, m % 2, 0:32], 2)
                md = tiles(mod[:, m % 2, :], 2)
                eng.wait_ge(vector_done, done.count)
                for t in range(KT):
                    ts(x3[:, t, XS], x3[:, t, XS], x[:, t, 0:1], MUL, md[:, t, 0:1], ADD, *(("xm_d", m) if t == 7 else ())).then_inc(vector_done, 1)
                for half, cs in ((0, CS), (1, XS)):
                    eng.wait_ge(scalar_done, step("xh", m, half))
                    tt(xlo[:, :, cs], x3[:, :, cs], xhi[:, :, cs].bitcast(F32), SUB, *(("xm", m) if half else ())).then_inc(vector_done, 1)

            def mla():
                m = 6
                rms(m)
                rope = table("rope")
                for i in range(6):
                    split_to(split_no("mla_in", min(i + 1, 6)))
                    if i == 3:
                        eng.wait_ge(tensor_done, step("in2", m, 5))
                        eng.wait_ge(vector_done, done.count)
                        tt(k_rot[64:96, :], PS[64:96, 5, :], rope[64:96, :], MUL).then_inc(vector_done, 1)
                        tt(q_rot[64:96, :], PS[96:128, 5, :], rope[96:128, :], MUL, "in2_read", m, 5).then_inc(vector_done, 1)
                        eng.wait_ge(vector_done, done.count)
                        tt(k_rot[64:96, :], k_rot[64:96, :], q_rot[64:96, :], ADD, "kr").then_inc(vector_done, 1)
                    mod_part(7, 2 * i)
                    mod_part(7, 2 * i + 1)
                split_to(split_no("mla_in", 6))
                modulation(7)
                eng.wait_ge(tensor_done, step("cqsum", m))
                eng.wait_ge(vector_done, done.count)
                ts(rs2[:, 0:512], bank(0), 1.0 / 384, MUL, EPS, ADD).then_inc(vector_done, 1)
                eng.wait_ge(vector_done, done.count)
                ts(rs2[:, 512:1024], bank(1), 1.0 / 256, MUL, EPS, ADD, "cqe", m).then_inc(vector_done, 1)
                eng.wait_ge(scalar_done, step("cqr", m))
                for t in range(5):
                    g = col("q_norm", t) if t < 3 else col("kv_norm", t - 3)
                    eng.wait_ge(vector_done, done.count)
                    stt(cq[:, t], cq[:, t], g, rs2[:, 0:512] if t < 3 else rs2[:, 512:1024], MUL, MUL, *(("cqn", m) if t == 4 else ())).then_inc(vector_done, 1)
                def q_part(h):
                    eng.wait_ge(tensor_done, step("q2", h))
                    if h > 1:
                        eng.wait_ge(tensor_done, step("s2", h - 2))
                    q = q_h[h % 2]
                    eng.wait_ge(vector_done, done.count)
                    tt(q[0:96, :], PS[0:96, 0, :], rope[0:96, :], MUL).then_inc(vector_done, 1)
                    tt(q_rot[64:96, :], PS[96:128, 0, :], rope[96:128, :], MUL).then_inc(vector_done, 1)
                    eng.wait_ge(vector_done, done.count)
                    tt(q[64:96, :], q[64:96, :], q_rot[64:96, :], ADD, "q_read", h).then_inc(vector_done, 1)

                def maxima(h):
                    eng.wait_ge(tensor_done, step("s2", h))
                    if h > 1:
                        eng.wait_ge(scalar_done, step("exp2", h - 2))
                    nm = nmx[:, 4 * (h % 2):4 * (h % 2) + 4]
                    do(v.tensor_reduce(nm[:, 0:2], tiles(bank(2), 256), AX.X, ALU.max, negate=True)).then_inc(vector_done, 1)
                    do(v.tensor_reduce(nm[:, 2:4], tiles(banks(3, 1024), 512), AX.X, ALU.max, negate=True)).then_inc(vector_done, 1)
                    eng.wait_ge(vector_done, done.count)
                    ts(nm, nm, MLA_SCALE, MUL, None, None, "nmx", h).then_inc(vector_done, 1)

                def reciprocals(h):
                    eng.wait_ge(scalar_done, step("exp2", h))
                    sm = rsm[:, 4 * (h % 2):4 * (h % 2) + 4]
                    do(v.reciprocal(sm, sm), "rec", h).then_inc(vector_done, 1)

                def out_part(h):
                    eng.wait_ge(tensor_done, step("o2", h))
                    t = h // 2
                    tt(o_prod, bank(1), gate2[:, t, :], MUL, "o_read", t).then_inc(vector_done, 1)
                    parts(xhi[:, t, :], xlo[:, t, :], o_prod, "o_parts", t)

                for h in range(MLA_H):
                    g = h // 8
                    if h % 8 == 0:
                        for t in range(4):
                            eng.wait_ge(tensor_done, step("kn", g, t))
                            copy(k_h[0:64, 2 * t + 1], PS[64:128, 2 + t, :], "kn_read", g, t, 1).then_inc(vector_done, 1)
                        for t in range(1, 4, 2):
                            eng.wait_ge(tensor_done, step("v2", g, t))
                            copy(v_h[:, t, :], bank(2 + t), "v2_read", g, t).then_inc(vector_done, 1)
                        for first in (h, h + 1):
                            q_part(first)
                            maxima(first)
                        reciprocals(h)
                    pt_copy(h)
                    if h % 8 < 7:
                        reciprocals(h + 1)
                    if h % 8 < 6:
                        q_part(h + 2)
                    if h % 2:
                        out_part(h)
                    if h % 8 < 6:
                        maxima(h + 2)
                for ch in range(4):
                    split_to(split_no("wout2", 0, ch) + 1)
                    for t in (2 * ch, 2 * ch + 1):
                        eng.wait_ge(tensor_done, step("y2", m, t))
                        for s, cs in ((1, CS), (0, XS)):
                            stt(res[:, t, cs], PS[:, 2 + t % 4, cs], mod[:, 0, 32 + 2 * t + s:33 + 2 * t + s], res[:, t, cs], MUL, ADD,
                                *(("res2", m, t) if s == 0 else ())).then_inc(vector_done, 1)

            def pt_copy(h):
                eng.wait_ge(tensor_done, step("pt", h))
                copy(pt_h[:, 1024:1536], bank(7), "pt_d", h).then_inc(vector_done, 1)

            def gla():
                m = 7
                rms(m)
                eng.wait_ge(tensor_done, step("in2", m, 0))
                eng.wait_ge(vector_done, done.count)
                copy(a_r, bank(0), "in2_read", m, 0).then_inc(vector_done, 1)
                for i in range(9):
                    split_to(split_no("gla_in", i) + 1)
                for ch in range(4):
                    split_to(split_no("gla_v", ch) + 1)
                    for tp in range(2):
                        n = 17 + 2 * ch + tp
                        eng.wait_ge(tensor_done, step("in2", m, n))
                        copy(a_v[:, 2 * tp:2 * tp + 2, 256 * ch:256 * ch + 256], tiles(bank(n % 6), 256), "in2_read", m, n).then_inc(vector_done, 1)
                split_to(split_no("gla_v", 3) + 2)
                ones1 = table("ones")
                for d in range(2):
                    eng.wait_ge(tensor_done, step("ga", d))
                    eng.wait_ge(vector_done, done.count)
                    for t in range(4):
                        ts(a_u[:, 512 * t:512 * t + 512], bank(4 * d + t), col("b_g", 4 * d + t), ADD, None, None).then_inc(vector_done, 1)
                    eng.wait_ge(vector_done, done.count)
                    stt(a_ab, a_u, -1.0, a_u, MUL, ALU.max, "gab", d).then_inc(vector_done, 1)
                    found["ga_read", d] = found["gab", d]
                    eng.wait_ge(scalar_done, step("gln", d))
                    eng.wait_ge(vector_done, done.count)
                    stt(a_u, a_u, 0.0, a_ab, ALU.min, SUB).then_inc(vector_done, 1)
                    eng.wait_ge(vector_done, done.count)
                    ts(a_u, a_u, 1.0 / 16, MUL).then_inc(vector_done, 1)
                    eng.wait_ge(vector_done, done.count)
                    for h in range(4):
                        for s in range(2):
                            src = a_u[:, 512 * h + 256 * s:512 * h + 256 * s + 256]
                            do(v.tensor_tensor_scan(a_b[d][s][:, h], ones1, src, 0.0, MUL, ADD),
                               *(("cum", 0) if h == 3 and s == 1 and d == 0 else ())).then_inc(vector_done, 1)
                    if d == 1:
                        eng.wait_ge(vector_done, done.count)
                        for s in range(2):
                            b = a_b[1][s]
                            copy(small[:, 40 + 4 * s:44 + 4 * s], b[:, :, T - 1]).then_inc(vector_done, 1)
                        for s in range(2):
                            b = a_b[1][s]
                            eng.wait_ge(vector_done, done.count)
                            tt(b, each(small[:, 40 + 4 * s:44 + 4 * s], 256), b, SUB).then_inc(vector_done, 1)
                            eng.wait_ge(vector_done, done.count)
                            tt(b, b, tiles(a_u, 512)[:, :, 256 * s:256 * s + 256], ADD, *(("cum", 1) if s else ())).then_inc(vector_done, 1)
                for d in range(2):
                    eng.wait_ge(scalar_done, step("ekc", d))
                    eng.wait_ge(scalar_done, step("eqd", d))
                    tt(tiles(a_kd[d], 256), tiles(a_kd[d], 256), a_k[0], MUL, "kd", d).then_inc(vector_done, 1)
                    tt(a_qd[d], a_qd[d], a_q, MUL, "aqd", d).then_inc(vector_done, 1)
                eng.wait_ge(tensor_done, step("diag"))
                eng.wait_ge(vector_done, done.count)
                stt(tiles(a_atd, 128), tiles(banks(0, 1024), 128), 2.0, over(ident, 8), MUL, MUL, "at0").then_inc(vector_done, 1)
                found["lev_read", -1] = found["at0",]

                kx, qx = W(1024, 1024), W(2048, 1024)

                def tree(n):
                    li, d = n // 2, n % 2
                    s = 1 << li
                    eng.wait_ge(tensor_done, step("akdt", n % 2))
                    eng.wait_ge(scalar_done, step("akdts", n % 2))
                    if n >= 2:
                        eng.wait_ge(tensor_done, step("lev", n - 2))
                    b = a_b[d][1].rearrange("p h (n b) -> p (h n) b", b=2 * s)
                    e = a_e[n % 2].rearrange("p (n b) -> p n b", b=2 * s)
                    kk = (kx if d == 0 else qx).rearrange("p (n b) -> p n b", b=2 * s)
                    qq = (qx if d == 0 else kx).rearrange("p (n b) -> p n b", b=2 * s)
                    lo, hi = slice(0, s), slice(s, 2 * s)
                    r = s - 1 if d == 0 else s
                    ref = b[:, :, r:r + 1].to_broadcast([P, T * 4 // (2 * s), s])
                    if d == 0:
                        tt(e[:, :, lo], ref, b[:, :, lo], SUB).then_inc(vector_done, 1)
                        tt(e[:, :, hi], b[:, :, hi], ref, SUB, "dif", n).then_inc(vector_done, 1)
                    else:
                        tt(e[:, :, lo], b[:, :, lo], ref, SUB).then_inc(vector_done, 1)
                        tt(e[:, :, hi], ref, b[:, :, hi], SUB, "dif", n).then_inc(vector_done, 1)
                    return e, kk, qq, lo, hi

                def weigh(n, t):
                    e, kk, qq, lo, hi = t
                    eng.wait_ge(scalar_done, step("ez", n))
                    tt(e[:, :, lo], e[:, :, lo], kk[:, :, lo], MUL).then_inc(vector_done, 1)
                    tt(e[:, :, hi], e[:, :, hi], qq[:, :, hi], MUL, "z", n).then_inc(vector_done, 1)

                def gather(n):
                    li, d = n // 2, n % 2
                    eng.wait_ge(tensor_done, step("lev", n))
                    b = 0 if n % 2 else 2
                    if li < 7:
                        if n >= 2:
                            eng.wait_ge(gpsimd_done, step("at", n - 2))
                        eng.wait_ge(tensor_done, step("ast", 0))
                        eng.wait_ge(tensor_done, step("ast", 1))
                        tt(tiles(a_m[n % 2], 128), tiles(banks(b, 1024), 128), over(table("first" if d == 0 else "second", P * li, P), 8), MUL,
                           "lev_read", n).then_inc(vector_done, 1)
                    else:
                        copy(a_ato[d], bank(b), "lev_read", n).then_inc(vector_done, 1)

                t0 = tree(0)
                for n in range(16):
                    weigh(n, t0)
                    if n < 15:
                        t0 = tree(n + 1)
                    gather(n)
                eng.wait_ge(tensor_done, step("aosum"))
                eng.wait_ge(vector_done, done.count)
                ts(a_rs, banks(0, 1024), 1.0 / 256, MUL, EPS, ADD, "aoe").then_inc(vector_done, 1)
                eng.wait_ge(scalar_done, step("aor"))
                ov = banks(4, 2048).rearrange("p (h v t) -> p h v t", h=4, v=2)
                eng.wait_ge(vector_done, done.count)
                tt(a_o.rearrange("p (h v t) -> p h v t", h=4, v=2), ov,
                   tiles(a_rs, 256).unsqueeze(2).to_broadcast([P, 4, 2, 256]), MUL).then_inc(vector_done, 1)
                eng.wait_ge(vector_done, done.count)
                o4 = a_o.rearrange("p (h v t) -> p h v t", h=4, v=2)
                g4 = a_gate.rearrange("p (h v) t -> p h v t", v=2)
                for h in range(4):
                    for dvh in range(2):
                        stt(o4[:, h, dvh], o4[:, h, dvh], col("o_norm", dvh), g4[:, h, dvh], MUL, MUL).then_inc(vector_done, 1)
                parts(xhi[:, :, XS], xlo[:, :, XS], tiles(a_o, 256), "aod")
                for ch in range(4):
                    split_to(split_no("wout2", 1, ch) + 1)
                    eng.wait_ge(tensor_done, step("y2", m, ch))
                    for t in (2 * ch, 2 * ch + 1):
                        eng.wait_ge(vector_done, done.count)
                        stt(tiles(ff_res, 256)[:, t], bank(4 + ch, 256 * (t % 2), 256 * (t % 2) + 256), mod[:, 1, 32 + 2 * t:33 + 2 * t],
                            res[:, t, XS], MUL, ADD, *(("fres",) if t == 7 else ())).then_inc(vector_done, 1)
                eng.wait_ge(tensor_done, step("fsum"))
                eng.wait_ge(vector_done, done.count)
                ts(ff_rstd, bank(0, 0, 256), 1.0 / D, MUL, EPS, ADD, "fe").then_inc(vector_done, 1)
                eng.wait_ge(scalar_done, step("frs"))
                eng.wait_ge(vector_done, done.count)
                for t in range(KT):
                    stt(tiles(ff_cen, 256)[:, t], tiles(ff_res, 256)[:, t], col("final_g", t), ff_rstd, MUL, MUL,
                        *(("final",) if t == 7 else ())).then_inc(vector_done, 1)

            eng.wait_ge(params_in, 48)
            for ch in range(12):
                mod_part(0, ch)
            modulation(0)
            eng.wait_ge(tokens_in, 16)
            for l in range(DEPTH):
                ffn(l, 0)
                mixer(l)
                ffn(l, 1)
            mla()
            gla()

        @block.gpsimd
        def _(eng):
            done = Steps(gpsimd_done, found)

            def norm_half(m):
                eng.wait_ge(scalar_done, step("rstd", m))
                cen = tiles(ff_cen, 256)[:, 4:8]
                nc.gpsimd.tensor_tensor(cen, cen, over(ff_rstd, 4), ALU.mult).then_inc(gpsimd_done, 1)
                done.named("xn", m, 1)

            def mod_chunk(m, ch):
                acc = mod_acc(m, ch)
                mine = by_gpsimd(m, ch)
                vecs = [i for i in range(1 if m < 6 else 2) if i not in mine]
                if ch == 0 and m:
                    eng.wait_ge(vector_done, step("xm", m - 1))
                if m in SPLIT_MODS and ch == GATE:
                    eng.wait_ge(vector_done, step("xm", m))
                if ch >= 2:
                    eng.wait_ge(tensor_done, step("modcol", m, ch - 2))
                for i in mine:
                    n = found["chunk_no", "ada", m, ch][1]
                    c = sc[:, 0:8] if m < 6 else tiles(sc[:, 8:24], 2)[:, :, i]
                    prod = mod_prod(m, ch)
                    eng.wait_ge(landed[n % RING], 16 * (n // RING + 1))
                    if done.count:
                        eng.wait_ge(gpsimd_done, done.count)
                    nc.gpsimd.tensor_tensor(tiles(prod, 256), tiles(ring[:, n % RING, :], 256), each(c, 256), ALU.mult).then_inc(gpsimd_done, 1)
                    done.named("chunk", n)
                    for half in (1024, 512):
                        eng.wait_ge(gpsimd_done, done.count)
                        nc.gpsimd.tensor_tensor(prod[:, 0:half], prod[:, 0:half], prod[:, half:2 * half], ALU.add).then_inc(gpsimd_done, 1)
                        done.named()
                    eng.wait_ge(gpsimd_done, done.count)
                    nc.gpsimd.tensor_tensor(acc[:, 2 * i], prod[:, 0:256], prod[:, 256:512], ALU.add).then_inc(gpsimd_done, 1)
                    done.named(*(() if vecs else ("modsum", m, ch)))
                if vecs:
                    eng.wait_ge(vector_done, step("modacc", m, ch))
                    a, b = vecs[0], vecs[-1] + 1
                    pair = acc.rearrange("p (v e) n -> p v e n", e=2)[:, a:b]
                    nc.gpsimd.tensor_tensor(pair[:, :, 0, :], pair[:, :, 0, :], pair[:, :, 1, :], ALU.add).then_inc(gpsimd_done, 1)
                    done.named("modsum", m, ch)

            for m in range(8):
                for ch in range(GATE if m in SPLIT_MODS else 12):
                    if m and late_ada(m - 1, ch):
                        mod_chunk(m - 1, late_ada(m - 1, ch))
                    mod_chunk(m, ch)
                if 1 <= m < 7:
                    norm_half(m - 1)
            for h in range(MLA_H):
                eng.wait_ge(vector_done, step("rec", h))
                p = p_h[h % 2]
                r = rsm[:, 4 * (h % 2):4 * (h % 2) + 4]
                nc.gpsimd.tensor_tensor(tiles(p[:, 0:512], 256), tiles(p[:, 0:512], 256), each(r[:, 0:2], 256), ALU.mult).then_inc(gpsimd_done, 1)
                done.named()
                nc.gpsimd.tensor_tensor(tiles(p[:, 512:1536], 512), tiles(p[:, 512:1536], 512), each(r[:, 2:4], 512), ALU.mult).then_inc(gpsimd_done, 1)
                done.named("pn", h)
            for n in range(14):
                eng.wait_ge(vector_done, step("lev_read", n))
                eng.wait_ge(vector_done, step("at0"))
                eng.wait_ge(gpsimd_done, done.count)
                nc.gpsimd.tensor_tensor(a_atd, a_atd, a_m[n % 2], ALU.add).then_inc(gpsimd_done, 1)
                done.named("at", n)
            found["at_done",] = found["at", 13]

    return found, order


def constant_tables():
    t = np.zeros((P, NTAB), np.float32)

    def put(name, a):
        at, n = TAB[name]
        t[:, at:at + n] = a.reshape(P, n)
    i = np.arange(P)
    put("ident", np.eye(P))
    put("ones", np.ones((P, 256)))
    put("blk", (i[:, None] // 64 == i[None, :] // 64))
    first = np.stack([(i[:, None] // (2 * s) == i[None, :] // (2 * s)) & (i[:, None] // s % 2 == 0) & (i[None, :] // s % 2 == 1)
                      for s in LEVELS], 1)
    put("first", first)
    put("second", np.transpose(first, (2, 1, 0)))
    put("strict", i[None, :] > i[:, None])
    q = np.arange(T)
    blocks = np.arange(2)[None, :, None] * P + i[:, None, None]
    put("neg_t", np.where(q[None, None, :] >= blocks, 0, NEG))
    put("neg_q", np.where(q[None, None, :] <= blocks, 0, NEG))
    rope = np.zeros((P, 2 * T))
    rope[0:96] = 1.0
    pos = np.stack([np.arange(T) // 64, np.arange(T) % 64]).astype(np.float32)
    inv = np.float32(10000.0) ** (-np.arange(8, dtype=np.float32) / 8)
    for r in range(32):
        ang = pos[r // 16] * inv[r % 8]
        rope[64 + r, T:] = np.cos(ang)
        rope[96 + r, T:] = np.sin(ang) * (-1 if r % 16 < 8 else 1)
    put("rope", rope)
    put("pair", i[:, None, None] % 32 == 2 * np.arange(3)[None, :, None] + i[None, None, :] // 64)
    return t


def parameter_columns(a):
    c = np.zeros((P, NCOLS), np.float32)

    def put(name, x, lo=0):
        at, _ = COLS[name]
        x = np.asarray(x)
        c[:x.shape[0], at + lo:at + lo + x.shape[1]] = x

    def by_tile(v):
        return np.asarray(v).reshape(-1, P).T
    put("c", by_tile(a["c"]))
    put("c2", np.stack([by_tile(a["c_2"]), by_tile(a["c_ctx_2"])], 2).reshape(P, 16))
    put("ada_b", by_tile(a["ada_b"]))
    put("ada_b2", by_tile(a["ada_b_2"]))
    put("ln_g", by_tile(a["ln_g"]))
    put("ln_b", by_tile(a["ln_b"]))
    put("gconv", by_tile(a["gdn_conv"]))
    put("mconv", by_tile(a["mlstm_conv"]))
    at = COLS["row_bias"][0]
    for l in range(DEPTH):
        c[ROW_A:ROW_A + 6, at + l] = a["gdn_dt_bias"][l]
        c[ROW_I:ROW_I + 6, at + l] = a["mlstm_i_bias"][l]
        c[ROW_F:ROW_F + 6, at + l] = a["mlstm_f_bias"][l]
        c[ROW_A:ROW_A + 6, COLS["row_log"][0] + l] = a["gdn_a_log"][l]
        c[:, COLS["gdn_norm"][0] + l] = np.tile(a["gdn_norm"][l], 2)
    c[:, COLS["row_sign"][0]] = np.repeat([1, -1, 1, -1], 32)
    c[:, COLS["row_keep"][0]] = np.repeat([0, 0, 0, 1], 32)
    put("ml_norm", by_tile(a["mlstm_norm"]))
    put("norm_g", by_tile(a["norm_g_2"]))
    put("final_g", by_tile(a["final_g_2"]))
    put("q_norm", by_tile(a["mla_q_norm_2"]))
    put("kv_norm", by_tile(a["mla_kv_norm_2"]))
    put("b_g", np.concatenate([by_tile(a["gla_b_gf_2"]), by_tile(a["gla_b_gb_2"])], 1))
    put("o_norm", by_tile(a["gla_o_norm_2"]))
    return c


def columns(w, starts, kt):
    w = w.reshape(kt, P, -1)
    parts = [np.transpose(w[:, :, s:s + n], (1, 0, 2)) if s >= 0 else np.zeros((P, kt, n), np.float32) for s, n in starts]
    return np.concatenate(parts, 2)


def chunk_of(tag, a):
    kind = tag[0]
    if kind == "ada":
        m, ch = tag[1:]
        w = a["ada_w"][m // 3] if m < 6 else a["ada_w_2"][m - 6]
        return columns(w, [(3072 * (m % 3 if m < 6 else 0) + 256 * ch, 256)], KT)
    if kind == "w13":
        l, f, j = tag[1:]
        return columns(a["ffn_w13"][l, f], [(P * j, P), (FF + P * j, P)], KT)
    if kind == "w2":
        l, f, p = tag[1:]
        return columns(a["ffn_w2"][l, f][256 * p:256 * p + 256], [(0, D)], 2)
    if kind == "win":
        l, ch = tag[1:]
        w = a["w_in"][l]
        if ch < 12:
            return columns(w, [(WIN_TILES[2 * ch], P), (WIN_TILES[2 * ch + 1], P)], KT)
        if ch == 12:
            return columns(w, [(WIN_TILES[24], P), (GA0, 6), (-1, 26), (GB0, 6), (-1, 26), (MLI0, 6), (-1, 26), (MLF0, 6), (-1, 26)], KT)
        if ch == 13:
            return columns(w, [(MOBA0 + 512, 256)], KT)
        return columns(w, [(MLV0, 256)] if ch == 14 else [(MLV0 + 256, 128), (-1, 128)], KT)
    if kind == "wout":
        return columns(a["w_out"][tag[1]], [(256 * tag[2], 256)], KT)
    if kind == "mla_in":
        w, i = a["mla_w_in_2"][0], tag[1]
        perm = [8, 0, 24, 16]
        kr = [(-1, 64), (640, 32)] + [(640 + p, 8) for p in perm]
        if i < 2:
            return columns(w, [(256 * i, 256)], KT)
        if i == 2:
            return columns(w, [(512, 128)] + kr, KT)
        return columns(w, [(672 + 256 * (i - 3), 256)], KT)
    if kind == "ukv":
        heads = range(8 * tag[1], 8 * tag[1] + 8)
        return columns(a["mla_w_ukv_2"][0], [(128 * h, 64) for h in heads] + [(128 * h + 64, 64) for h in heads], 2)
    if kind == "uq":
        s = []
        for h in range(4 * tag[1], 4 * tag[1] + 4):
            s += [(96 * h, 96)] + [(96 * h + 64 + p, 8) for p in [8, 0, 24, 16]]
        return columns(a["mla_w_uq_2"][0], s, 3)
    if kind == "wout2":
        w = a["mla_w_out_2"][0] if tag[1] == 0 else a["gla_w_out_2"][0]
        return columns(w, [(256 * tag[2], 256)], KT)
    if kind == "gla_in":
        w, i = a["gla_w_in_2"][0], tag[1]
        t = [[(3072, 16), (-1, 16), (3088, 16), (-1, 80)]] + [[(512 + P * k, P)] for k in range(4)] \
            + [[(P * k, P)] for k in range(4)] + [[(2048 + P * k, P)] for k in range(8)] + [[(-1, P)]]
        return columns(w, t[2 * i] + t[2 * i + 1], KT)
    if kind == "gla_v":
        return columns(a["gla_w_in_2"][0], [(1024 + 256 * tag[1], 256)], KT)
    raise ValueError(tag)


def kernel(**inputs):
    import concourse.bacc as bacc
    from concourse.bass_utils import run_bass_kernel_spmd as run

    a = {k: np.asarray(v) for k, v in inputs.items()}

    def program(n_chunks, marks):
        nc = bacc.Bacc("TRN2", target_bir_lowering=False, num_devices=1)
        shapes = {"stream": (n_chunks, P, CHUNK), "cols": (P, NCOLS), "tab": (P, NTAB), "wg": (48, 512), "xt": (D, T), "ct": (D, T)}
        ins = [nc.dram_tensor(f"in_{k}_dram", s, F32, kind="ExternalInput").ap() for k, s in shapes.items()]
        out = nc.dram_tensor("out_0_dram", (D, T), F32, kind="ExternalOutput").ap()
        return nc, build(nc, *ins, out, marks)

    _, (marks, order) = program(1, None)
    nc, _ = program(len(order), marks)
    stream = np.zeros((len(order), P, CHUNK), np.float32)
    for n, tag in enumerate(order):
        c = chunk_of(tag, a).reshape(P, -1)
        stream[n, :, :c.shape[1]] = c
    wg = np.zeros((48, 512), np.float32)
    wg[0:16] = a["gla_w_gf_2"][0]
    wg[32:48] = a["gla_w_gb_2"][0]
    arrays = {"in_stream_dram": stream, "in_cols_dram": parameter_columns(a), "in_tab_dram": constant_tables(), "in_wg_dram": wg,
              "in_xt_dram": np.ascontiguousarray(a["x"][0].T), "in_ct_dram": np.ascontiguousarray(a["ctx_2"][0].T)}
    r = run(nc, [arrays], core_ids=[0])
    return np.ascontiguousarray(r.results[0]["out_0_dram"].T)[None]
```
